# Optimizing a Trainium2 kernel written in Bass

```python
import math
import jax
import jax.numpy as jnp
from jax import lax
import numpy as np
import jax, jax.numpy as jnp

D_MODEL = 2048
BATCH = 1
SEQ = 256
DEPTH = 2

N_MIXERS = 2
N_RET_LAYERS = (DEPTH + 1) // 2
N_GDN_LAYERS = DEPTH // 2
N_MEM = 256
MIX_WIDTH = 2 * D_MODEL
TOK_WIDTH = 3 * MIX_WIDTH // 4
MEM_WIDTH = MIX_WIDTH - TOK_WIDTH
QK_HEAD_DIM = 128
N_QK_HEADS = TOK_WIDTH // 256
QK_WIDTH = N_QK_HEADS * QK_HEAD_DIM
RET_V_HEAD_DIM = TOK_WIDTH // N_QK_HEADS
GDN_V_HEAD_DIM = 128
N_GDN_V_HEADS = TOK_WIDTH // GDN_V_HEAD_DIM
GDN_GQA = N_GDN_V_HEADS // N_QK_HEADS
MEM_HEADS = 4
MEM_HEAD_DIM = MEM_WIDTH // MEM_HEADS
CONV_WIDTH = 4
CHUNK = 64
ROPE_BASE = 10000.0
CONV_CH = 2 * QK_WIDTH + TOK_WIDTH
RET_COLS = CONV_CH + MEM_WIDTH + MIX_WIDTH
GDN_COLS = RET_COLS + 2 * N_GDN_V_HEADS
DEEPNORM_ALPHA = (2.0 * DEPTH) ** 0.25
DEEPNORM_BETA = (8.0 * DEPTH) ** -0.25
LN_EPS = 1e-5
NORM_EPS = 1e-6


def layer_norm(x, g, b):
    xf = x.astype(jnp.float32)
    mu = jnp.mean(xf, -1, keepdims=True)
    var = jnp.mean(jnp.square(xf - mu), -1, keepdims=True)
    return ((xf - mu) * lax.rsqrt(var + LN_EPS) * g.astype(jnp.float32) + b.astype(jnp.float32)).astype(x.dtype)

def rotary(t, positions):
    half = t.shape[-1] // 2
    inv_freq = ROPE_BASE ** (-jnp.arange(half, dtype=jnp.float32) / half)
    ang = positions.astype(jnp.float32)[..., None] * inv_freq
    cos = jnp.cos(ang)[:, :, None, :]
    sin = jnp.sin(ang)[:, :, None, :]
    t1, t2 = t[..., :half], t[..., half:]
    return jnp.concatenate([t1 * cos - t2 * sin, t1 * sin + t2 * cos], -1)

def retention(q, k, v):
    B, S, H, dk = q.shape
    dv = v.shape[-1]
    n = S // CHUNK
    log_gamma = jnp.log1p(-jnp.exp2(-5.0 - jnp.arange(H, dtype=jnp.float32)))
    k = k * dk ** -0.5
    qc = q.reshape(B, n, CHUNK, H, dk)
    kc = k.reshape(B, n, CHUNK, H, dk)
    vc = v.reshape(B, n, CHUNK, H, dv)
    idx = jnp.arange(CHUNK, dtype=jnp.float32)
    rel = idx[:, None] - idx[None, :]
    intra_decay = jnp.where(rel[None] >= 0, jnp.exp(log_gamma[:, None, None] * jnp.maximum(rel, 0.0)[None]), 0.0)
    scores = jnp.einsum('bnihd,bnjhd->bnhij', qc, kc) * intra_decay
    inner = jnp.einsum('bnhij,bnjhv->bnihv', scores, vc)
    q_decay = jnp.exp((idx[:, None] + 1.0) * log_gamma[None, :])
    k_decay = jnp.exp((CHUNK - 1.0 - idx)[:, None] * log_gamma[None, :])
    chunk_decay = jnp.exp(CHUNK * log_gamma)

    def step(state, inp):
        q_i, k_i, v_i = inp
        cross = jnp.einsum('bihd,bhdv->bihv', q_i, state) * q_decay[None, :, :, None]
        state = state * chunk_decay[None, :, None, None] + jnp.einsum('bjhd,bjhv->bhdv', k_i * k_decay[None, :, :, None], v_i)
        return state, cross

    state0 = jnp.zeros((B, H, dk, dv), jnp.float32)
    xs = (jnp.moveaxis(qc, 1, 0), jnp.moveaxis(kc, 1, 0), jnp.moveaxis(vc, 1, 0))
    _, cross = lax.scan(step, state0, xs)
    return (inner + jnp.moveaxis(cross, 0, 1)).reshape(B, S, H, dv)

def _to_chunks(t):
    B, S, H = t.shape[:3]
    t = t.reshape((B, S // CHUNK, CHUNK, H) + t.shape[3:])
    return jnp.moveaxis(t, 3, 1)

def gated_delta_rule(q, k, v, g, beta):
    B, S, H, dk = q.shape
    dv = v.shape[-1]
    qc = _to_chunks(q * dk ** -0.5)
    kc = _to_chunks(k)
    vc = _to_chunks(v)
    bc = _to_chunks(beta)
    g_cum = jnp.cumsum(_to_chunks(g), -1)
    causal = jnp.tril(jnp.ones((CHUNK, CHUNK), bool))
    strict = jnp.tril(jnp.ones((CHUNK, CHUNK), bool), -1)
    diff = g_cum[..., :, None] - g_cum[..., None, :]
    decay = jnp.where(causal, jnp.exp(jnp.where(causal, diff, 0.0)), 0.0)
    k_beta = kc * bc[..., None]
    v_beta = vc * bc[..., None]
    lower = jnp.where(strict, jnp.einsum('bhnid,bhnjd->bhnij', k_beta, kc) * decay, 0.0)
    a_mat = lower + jnp.eye(CHUNK, dtype=jnp.float32)
    u = lax.linalg.triangular_solve(a_mat, v_beta, left_side=True, lower=True, unit_diagonal=True)
    w = lax.linalg.triangular_solve(a_mat, k_beta * jnp.exp(g_cum)[..., None], left_side=True, lower=True, unit_diagonal=True)
    qk = jnp.where(causal, jnp.einsum('bhnid,bhnjd->bhnij', qc, kc) * decay, 0.0)
    q_g = qc * jnp.exp(g_cum)[..., None]
    k_tail = kc * jnp.exp(g_cum[..., -1:] - g_cum)[..., None]
    g_last = jnp.exp(g_cum[..., -1])

    def step(state, inp):
        u_i, w_i, qk_i, q_i, k_i, gl_i = inp
        v_new = u_i - jnp.einsum('bhcd,bhdv->bhcv', w_i, state)
        out = jnp.einsum('bhcd,bhdv->bhcv', q_i, state) + jnp.einsum('bhij,bhjv->bhiv', qk_i, v_new)
        state = state * gl_i[..., None, None] + jnp.einsum('bhcd,bhcv->bhdv', k_i, v_new)
        return state, out

    state0 = jnp.zeros((B, H, dk, dv), jnp.float32)
    xs = tuple(jnp.moveaxis(t, 2, 0) for t in (u, w, qk, q_g, k_tail, g_last))
    _, out = lax.scan(step, state0, xs)
    return out.transpose(1, 0, 3, 2, 4).reshape(B, S, H, dv)

def causal_conv_silu(t, w):
    S = t.shape[1]
    tp = jnp.pad(t, ((0, 0), (CONV_WIDTH - 1, 0), (0, 0)))
    y = tp[:, 0:S, :] * w[0]
    for j in range(1, CONV_WIDTH):
        y = y + tp[:, j:j + S, :] * w[j]
    return jax.nn.silu(y)

def retention_branch(x, positions, w_in, norm_g):
    B, S, _ = x.shape
    h = x @ w_in
    q = h[..., :QK_WIDTH].reshape(B, S, N_QK_HEADS, QK_HEAD_DIM).astype(jnp.float32)
    k = h[..., QK_WIDTH:2 * QK_WIDTH].reshape(B, S, N_QK_HEADS, QK_HEAD_DIM).astype(jnp.float32)
    v = h[..., 2 * QK_WIDTH:CONV_CH].reshape(B, S, N_QK_HEADS, RET_V_HEAD_DIM).astype(jnp.float32)
    mq = h[..., CONV_CH:CONV_CH + MEM_WIDTH]
    z = h[..., CONV_CH + MEM_WIDTH:CONV_CH + MEM_WIDTH + MIX_WIDTH]
    o = retention(rotary(q, positions), rotary(k, positions), v)
    mu = jnp.mean(o, -1, keepdims=True)
    var = jnp.mean(jnp.square(o - mu), -1, keepdims=True)
    o = ((o - mu) * lax.rsqrt(var + NORM_EPS)).reshape(B, S, TOK_WIDTH) * norm_g.astype(jnp.float32)
    return o.astype(x.dtype), mq, z

def gdn_branch(x, w_in, conv_w, a_log, dt_bias, norm_g):
    B, S, _ = x.shape
    h = x @ w_in
    qkv = causal_conv_silu(h[..., :CONV_CH], conv_w).astype(jnp.float32)
    mq = h[..., CONV_CH:CONV_CH + MEM_WIDTH]
    z = h[..., CONV_CH + MEM_WIDTH:CONV_CH + MEM_WIDTH + MIX_WIDTH]
    a = h[..., RET_COLS:RET_COLS + N_GDN_V_HEADS].astype(jnp.float32)
    b = h[..., RET_COLS + N_GDN_V_HEADS:].astype(jnp.float32)
    q = qkv[..., :QK_WIDTH].reshape(B, S, N_QK_HEADS, QK_HEAD_DIM)
    k = qkv[..., QK_WIDTH:2 * QK_WIDTH].reshape(B, S, N_QK_HEADS, QK_HEAD_DIM)
    v = qkv[..., 2 * QK_WIDTH:].reshape(B, S, N_GDN_V_HEADS, GDN_V_HEAD_DIM)
    q = q * lax.rsqrt(jnp.sum(jnp.square(q), -1, keepdims=True) + NORM_EPS)
    k = k * lax.rsqrt(jnp.sum(jnp.square(k), -1, keepdims=True) + NORM_EPS)
    q = jnp.repeat(q, GDN_GQA, axis=2)
    k = jnp.repeat(k, GDN_GQA, axis=2)
    beta = jax.nn.sigmoid(b)
    g = -jnp.exp(a_log.astype(jnp.float32)) * jax.nn.softplus(a + dt_bias.astype(jnp.float32))
    o = gated_delta_rule(q, k, v, g, beta)
    o = o * lax.rsqrt(jnp.mean(jnp.square(o), -1, keepdims=True) + NORM_EPS) * norm_g.astype(jnp.float32)
    return o.reshape(B, S, TOK_WIDTH).astype(x.dtype), mq, z

def memory_attention(mq, mem, w_kv):
    B, S, _ = mq.shape
    kv = mem @ w_kv
    mk = kv[..., :MEM_WIDTH].reshape(B, N_MEM, MEM_HEADS, MEM_HEAD_DIM)
    mv = kv[..., MEM_WIDTH:].reshape(B, N_MEM, MEM_HEADS, MEM_HEAD_DIM)
    q = mq.reshape(B, S, MEM_HEADS, MEM_HEAD_DIM)
    s = jnp.einsum('bshd,bmhd->bhsm', q, mk).astype(jnp.float32) * MEM_HEAD_DIM ** -0.5
    p = jax.nn.softmax(s, -1).astype(mv.dtype)
    return jnp.einsum('bhsm,bmhd->bshd', p, mv).reshape(B, S, MEM_WIDTH)

def first_inputs(seed: int = 0) -> dict:
    key = jax.random.key(seed)
    ks = jax.random.split(key, 14)
    f32 = jnp.float32
    x = jax.random.normal(ks[0], (BATCH, SEQ, D_MODEL), f32)
    mem = jax.random.normal(ks[1], (BATCH, N_MEM, D_MODEL), f32)
    positions = jnp.arange(SEQ, dtype=jnp.int32)[None, :] + jax.random.randint(ks[2], (BATCH, 1), 0, 1024, dtype=jnp.int32)
    w_in_ret = jax.random.normal(ks[3], (N_RET_LAYERS, D_MODEL, RET_COLS), f32) * D_MODEL ** -0.5
    ret_norm_g = 1.0 + 0.02 * jax.random.normal(ks[4], (N_RET_LAYERS, TOK_WIDTH), f32)
    w_in_gdn = jax.random.normal(ks[5], (N_GDN_LAYERS, D_MODEL, GDN_COLS), f32) * D_MODEL ** -0.5
    conv_w = jax.random.normal(ks[6], (N_GDN_LAYERS, CONV_WIDTH, CONV_CH), f32) * CONV_WIDTH ** -0.5
    a_log = jnp.log(jax.random.uniform(ks[7], (N_GDN_LAYERS, N_GDN_V_HEADS), f32, 1.0, 16.0))
    dt = jnp.exp(jax.random.uniform(ks[8], (N_GDN_LAYERS, N_GDN_V_HEADS), f32, math.log(1e-3), math.log(1e-1)))
    dt_bias = dt + jnp.log(-jnp.expm1(-dt))
    gdn_norm_g = 1.0 + 0.02 * jax.random.normal(ks[9], (N_GDN_LAYERS, GDN_V_HEAD_DIM), f32)
    w_mem_kv = jax.random.normal(ks[10], (DEPTH, D_MODEL, 2 * MEM_WIDTH), f32) * D_MODEL ** -0.5
    w_out = jax.random.normal(ks[11], (DEPTH, MIX_WIDTH, D_MODEL), f32) * (MIX_WIDTH ** -0.5 * DEEPNORM_BETA)
    ln_g = 1.0 + 0.02 * jax.random.normal(ks[12], (DEPTH, D_MODEL), f32)
    ln_b = 0.02 * jax.random.normal(ks[13], (DEPTH, D_MODEL), f32)
    return {'x': x, 'mem': mem, 'positions': positions, 'w_in_ret': w_in_ret, 'ret_norm_g': ret_norm_g,
            'w_in_gdn': w_in_gdn, 'conv_w': conv_w, 'a_log': a_log, 'dt_bias': dt_bias, 'gdn_norm_g': gdn_norm_g,
            'w_mem_kv': w_mem_kv, 'w_out': w_out, 'ln_g': ln_g, 'ln_b': ln_b}

def first_block(x, mem, positions, w_in_ret, ret_norm_g, w_in_gdn, conv_w, a_log, dt_bias, gdn_norm_g,
              w_mem_kv, w_out, ln_g, ln_b):
    for i in range(DEPTH):
        j = i // N_MIXERS
        if i % N_MIXERS == 0:
            tok, mq, z = retention_branch(x, positions, w_in_ret[j], ret_norm_g[j])
        else:
            tok, mq, z = gdn_branch(x, w_in_gdn[j], conv_w[j], a_log[j], dt_bias[j], gdn_norm_g[j])
        mem_out = memory_attention(mq, mem, w_mem_kv[i])
        branch = jnp.concatenate([tok, mem_out.astype(tok.dtype)], -1) * jax.nn.silu(z)
        y = branch @ w_out[i]
        x = layer_norm(DEEPNORM_ALPHA * x + y, ln_g[i], ln_b[i])
    return x


DEPTH_2 = 1

MIX_WIDTH_2 = D_MODEL
POOL_WIDTH = MIX_WIDTH_2 // 2
POOL_WINDOWS = (2, 4, 8, 16)
POOL_GROUP = POOL_WIDTH // len(POOL_WINDOWS)
HGRN_WIDTH = MIX_WIDTH_2 - POOL_WIDTH
HGRN_HEAD_DIM = 128
HGRN_HEADS = HGRN_WIDTH // HGRN_HEAD_DIM
IN_WIDTH = POOL_WIDTH + 4 * HGRN_WIDTH
D_FF = 4 * D_MODEL
EPS = 1e-6


def rmsnorm(x, w):
    xf = x.astype(jnp.float32)
    r = xf * lax.rsqrt(jnp.mean(xf * xf, axis=-1, keepdims=True) + EPS)
    return (r * w.astype(jnp.float32)).astype(x.dtype)

def pool_mixer(u, pool_w, pool_b, pool_scale):
    B, S, _ = u.shape
    uf = u.astype(jnp.float32)
    c = jnp.cumsum(uf, axis=1)
    pos = jnp.arange(S)
    outs = []
    for j, w in enumerate(POOL_WINDOWS):
        sl = slice(j * POOL_GROUP, (j + 1) * POOL_GROUP)
        cj = c[..., sl]
        shifted = jnp.pad(cj, ((0, 0), (w, 0), (0, 0)))[:, :S]
        cnt = jnp.minimum(pos + 1, w).astype(jnp.float32)[None, :, None]
        dj = ((cj - shifted) / cnt - uf[..., sl]).astype(u.dtype)
        outs.append(dj @ pool_w[j] + pool_b[j])
    return jnp.concatenate(outs, axis=-1) * pool_scale

def hgrn2_chunk_scan(q, k, v, logf):
    B, S, H, Dk = q.shape
    Dv = v.shape[-1]
    N = S // CHUNK

    def to_chunks(a):
        return a.reshape(B, N, CHUNK, H, a.shape[-1]).transpose(1, 0, 3, 2, 4)

    causal = jnp.tril(jnp.ones((CHUNK, CHUNK), dtype=bool))[None, None, :, :, None]

    def step(state, inp):
        q_c, k_c, v_c, g_c = inp
        b = jnp.cumsum(g_c, axis=2)
        o_inter = jnp.einsum('bhtd,bhde->bhte', q_c * jnp.exp(b), state)
        diff = b[:, :, :, None, :] - b[:, :, None, :, :]
        decay = jnp.exp(jnp.where(causal, diff, -jnp.inf))
        scores = jnp.einsum('bhtd,bhsd,bhtsd->bhts', q_c, k_c, decay)
        o_intra = jnp.einsum('bhts,bhse->bhte', scores, v_c)
        b_last = b[:, :, -1:, :]
        new_state = jnp.exp(b_last[:, :, 0, :])[..., None] * state + jnp.einsum(
            'bhsd,bhse->bhde', k_c * jnp.exp(b_last - b), v_c)
        return new_state, o_inter + o_intra

    init = jnp.zeros((B, H, Dk, Dv), jnp.float32)
    _, o = lax.scan(step, init, (to_chunks(q), to_chunks(k), to_chunks(v), to_chunks(logf)))
    return o.transpose(1, 0, 3, 2, 4).reshape(B, S, H, Dv)

def hgrn2_mixer(q, f_pre, i, g, lb, norm_w):
    B, S, _ = q.shape
    shp = (B, S, HGRN_HEADS, HGRN_HEAD_DIM)
    qf = q.astype(jnp.float32).reshape(shp)
    vf = i.astype(jnp.float32).reshape(shp)
    sig = jax.nn.sigmoid(f_pre.astype(jnp.float32)).reshape(shp)
    lbh = lb.reshape(HGRN_HEADS, HGRN_HEAD_DIM)
    f = lbh + (1.0 - lbh) * sig
    k = (1.0 - lbh) * (1.0 - sig)
    o = hgrn2_chunk_scan(qf, k, vf, jnp.log(f))
    o = o * jax.nn.sigmoid(g.astype(jnp.float32)).reshape(shp)
    o = o * lax.rsqrt(jnp.mean(o * o, axis=-1, keepdims=True) + EPS)
    o = o * norm_w.astype(jnp.float32).reshape(HGRN_HEADS, HGRN_HEAD_DIM)
    return o.reshape(B, S, HGRN_WIDTH).astype(q.dtype)

def second_inputs(seed: int = 0) -> dict:
    key = jax.random.key(seed)
    ks = jax.random.split(key, 16)
    f32 = jnp.float32
    nrm = lambda k, s, sc: jax.random.normal(k, s, f32) * sc
    gain = lambda k, s: 1.0 + 0.05 * jax.random.normal(k, s, f32)
    return {
        "x": jax.random.normal(ks[0], (BATCH, SEQ, D_MODEL), f32),
        "w_in": nrm(ks[1], (DEPTH_2, D_MODEL, IN_WIDTH), D_MODEL ** -0.5),
        "pool_w": nrm(ks[2], (DEPTH_2, len(POOL_WINDOWS), POOL_GROUP, POOL_GROUP), POOL_GROUP ** -0.5),
        "pool_b": nrm(ks[3], (DEPTH_2, len(POOL_WINDOWS), POOL_GROUP), 0.02),
        "pool_scale": gain(ks[4], (DEPTH_2, POOL_WIDTH)),
        "lb_logits": nrm(ks[5], (DEPTH_2 + 1, HGRN_WIDTH), 0.5),
        "hgrn_norm_w": gain(ks[6], (DEPTH_2, HGRN_WIDTH)),
        "w_out": nrm(ks[7], (DEPTH_2, MIX_WIDTH_2, D_MODEL), MIX_WIDTH_2 ** -0.5),
        "norm_mix_pre": gain(ks[8], (DEPTH_2, D_MODEL)),
        "norm_mix_post": gain(ks[9], (DEPTH_2, D_MODEL)),
        "norm_mlp_pre": gain(ks[10], (DEPTH_2, D_MODEL)),
        "norm_mlp_post": gain(ks[11], (DEPTH_2, D_MODEL)),
        "w_mlp_in": nrm(ks[12], (DEPTH_2, D_MODEL, D_FF), D_MODEL ** -0.5),
        "w_mlp_out": nrm(ks[13], (DEPTH_2, D_FF, D_MODEL), D_FF ** -0.5),
    }

def second_block(x, w_in, pool_w, pool_b, pool_scale, lb_logits, hgrn_norm_w, w_out,
              norm_mix_pre, norm_mix_post, norm_mlp_pre, norm_mlp_post,
              w_mlp_in, w_mlp_out):
    lb_all = jnp.cumsum(jax.nn.softmax(lb_logits.astype(jnp.float32), axis=0), axis=0)
    P, H4 = POOL_WIDTH, HGRN_WIDTH
    for l in range(DEPTH_2):
        h = rmsnorm(x, norm_mix_pre[l])
        proj = h @ w_in[l]
        u_pool = proj[..., :P]
        q = proj[..., P:P + H4]
        f_pre = proj[..., P + H4:P + 2 * H4]
        i = proj[..., P + 2 * H4:P + 3 * H4]
        g = proj[..., P + 3 * H4:P + 4 * H4]
        y_pool = pool_mixer(u_pool, pool_w[l], pool_b[l], pool_scale[l])
        y_hgrn = hgrn2_mixer(q, f_pre, i, g, lb_all[l], hgrn_norm_w[l])
        mix = jnp.concatenate([y_pool, y_hgrn], axis=-1) @ w_out[l]
        x = x + rmsnorm(mix, norm_mix_post[l])
        h = rmsnorm(x, norm_mlp_pre[l])
        ff = jnp.square(jax.nn.relu(h @ w_mlp_in[l])) @ w_mlp_out[l]
        x = x + rmsnorm(ff, norm_mlp_post[l])
    return x


def setup_inputs(seed=0):
    out = dict(first_inputs(seed))
    for name, value in second_inputs(seed + 1).items():
        if name != "x":
            out[name + "_2"] = value
    return out


def reference(
    x, mem, positions, w_in_ret, ret_norm_g, w_in_gdn, conv_w, a_log, dt_bias, gdn_norm_g,
    w_mem_kv, w_out, ln_g, ln_b, w_in_2, pool_w_2, pool_b_2, pool_scale_2, lb_logits_2,
    hgrn_norm_w_2, w_out_2, norm_mix_pre_2, norm_mix_post_2, norm_mlp_pre_2, norm_mlp_post_2,
    w_mlp_in_2, w_mlp_out_2,
):
    x = first_block(
        x, mem, positions, w_in_ret, ret_norm_g, w_in_gdn, conv_w, a_log, dt_bias, gdn_norm_g,
        w_mem_kv, w_out, ln_g, ln_b,
    )
    return second_block(
        x, w_in_2, pool_w_2, pool_b_2, pool_scale_2, lb_logits_2, hgrn_norm_w_2, w_out_2,
        norm_mix_pre_2, norm_mix_post_2, norm_mlp_pre_2, norm_mlp_post_2, w_mlp_in_2,
        w_mlp_out_2,
    )


_drawn_inputs = setup_inputs


def setup_inputs(seed=0):
    import zlib

    import numpy as np

    out = dict(_drawn_inputs(seed))
    spreads = {}
    factors = {'ret_norm_g': 8.0,
     'gdn_norm_g': 21.652,
     'pool_b_2': 5.017,
     'mem': 3.738,
     'w_mem_kv': 3.703}
    for name, (base, spread) in spreads.items():
        noise = np.random.default_rng([zlib.crc32(name.encode()), seed]).standard_normal(out[name].shape)
        drawn = base * np.exp(spread * noise) if base else spread * noise
        out[name] = jnp.asarray(drawn.astype(out[name].dtype))
    for name, factor in factors.items():
        out[name] = (out[name] * factor).astype(out[name].dtype)
    return out
```

```python
import math
from contextlib import ExitStack

import numpy as np

import concourse.bass as bass
from concourse import mybir

P = 128
SEQ, D = 256, 2048
TT = SEQ // P
MIX = 2 * D
TOK = 3 * MIX // 4
MEMW = MIX - TOK
QKW = TOK // 2
CONV = 2 * QKW + TOK
NVH = TOK // P
COL = 512
KB = 4
GROUPS = TOK // COL
MGROUPS = MEMW // COL
BR = GROUPS + MGROUPS
ALPHA = (2.0 * 2) ** 0.25
QSCALE = float(P) ** -0.5
MSCALE = 256.0 ** -0.5
LN_EPS, EPS = 1e-5, 1e-6
FF = 4 * D
FFG = FF // COL
W2IN = 1024 + 4 * 1024
LEVELS = [2 ** i for i in range(7)]
WINDOWS = (2, 4, 8, 16)
TWO_PI = 2 * math.pi
TURN_PARTS = (6.28125, 1.9350051879882812e-03, 3.0199159819567e-07)
ROUND = 1.5 * 2 ** 23
PI_BELOW = 3.1415925
TINY = 2.0 ** -64

C_ID, C_TRI, C_LOW, C_M1, C_LV = 0, P, 2 * P, 3 * P, 4 * P
C_FREQ = C_LV + 7 * P
C_MAIN = C_FREQ + 64
C_DEC = C_MAIN
C_POOL = C_DEC + 12 * 2 * P
C_ALL = C_POOL + 4 * 3 * P


def shape_constants():
    c = np.zeros((P, C_ALL), np.float64)
    i = np.arange(P)
    row, col = i[:, None], i[None, :]
    c[:, C_ID:C_ID + P] = np.eye(P)
    c[:, C_TRI:C_TRI + P] = row <= col
    c[:, C_LOW:C_LOW + P] = row > col
    c[:, C_M1:C_M1 + P] = -((row // 2 == col // 2) & (row > col)).astype(float)
    for n, s in enumerate(LEVELS):
        c[:, C_LV + n * P:C_LV + (n + 1) * P] = (row // (2 * s) == col // (2 * s)) & (row % (2 * s) < s) & (col % (2 * s) >= s)
    c[:, C_FREQ:C_FREQ + 64] = (10000.0 ** (-np.arange(64) / 64))[None, :]
    for h in range(12):
        lg = math.log1p(-2.0 ** (-5 - h))
        at = C_DEC + h * 2 * P
        rel = (col - row).astype(float)
        c[:, at:at + P] = np.where(rel >= 0, np.exp(lg * np.maximum(rel, 0)), 0) * QSCALE
        c[:, at + P:at + 2 * P] = np.exp(lg * (rel + P)) * QSCALE
    for n, w in enumerate(WINDOWS):
        at = C_POOL + n * 3 * P
        for blk, (s0, t0) in enumerate(((0, 0), (0, P), (P, P))):
            s, t = row + s0, col + t0
            c[:, at + blk * P:at + (blk + 1) * P] = ((s <= t) & (s > t - w)) / np.minimum(t + 1, w) - (s == t)
    return c.astype(np.float32)


def turned_fills():
    return [[f"f{b}", f"f{b + 4}"] for b in range(4)]


PHASES = [
    ("mem0", 1, turned_fills()),
    ("kv0", 1, [["k0a", "k1a"], ["k0b", "k1b"], [], []]),
    ("x0", 1, turned_fills()),
    ("ret", GROUPS, [["q", "o0"], ["k", "o1"], ["s0", "ba"], ["s1", "bb"]]),
    ("att0", MGROUPS, [["qa", "pa", "ba"], ["qb", "pb", "bb"], ["s0", "o0"], ["s1", "o1"]]),
    ("mem1", 1, turned_fills()),
    ("kv1", 1, [["k0a", "k1a"], ["k0b", "k1b"], [], []]),
    ("x1", 1, turned_fills()),
    ("gates", 1, [["ab"], ["cum"], ["last"], []]),
    ("gdn", GROUPS, [
        ["q", "kn", "qk"] + [f"p{s}_0" for s in LEVELS[1:]] + ["va", "vn0", "qs", "ba"],
        ["k", "row0", "u0"] + [f"n{s}_0" for s in LEVELS[1:]] + ["vb", "o0", "vn1", "bb"],
        ["sq", "row1", "u1"] + [f"p{s}_1" for s in LEVELS[1:]] + ["va2", "st", "o1"],
        ["sk", "kk"] + [f"n{s}_1" for s in LEVELS[1:]] + ["vb2", "ks"],
    ]),
    ("att1", MGROUPS, [["qa", "pa", "ba"], ["qb", "pb", "bb"], ["s0", "o0"], ["s1", "o1"]]),
    ("h2", 1, turned_fills()),
    ("hgrn", 2, [
        ["qa", "fa", "d0"] + [f"l{s}" for s in LEVELS[0::2]] + ["o0", "ba"],
        ["qb", "fb", "d1"] + [f"l{s}" for s in LEVELS[1::2]] + ["o1", "bb"],
        ["x"], []]),
    ("pool", 2, [["da"], ["db"], ["ya"], ["yb"]]),
    ("h3", 1, turned_fills()),
    ("mlp", FFG, [["ba"], ["bb"], [], []]),
]


def fill(phase, step, g=0):
    for bank in range(4):
        before = 0
        for name, rounds, steps in PHASES:
            if name == phase and step in steps[bank]:
                return bank, g * len(steps[bank]) + (before + steps[bank].index(step) + 1)
            before += rounds * len(steps[bank])
    raise KeyError((phase, step))


C_RG, C_GG, C_PB, C_PS, C_LB, C_HW, C_MP, C_LP, N_ROWS = 0, 24, 25, 33, 41, 57, 65, 81, 97
N_LOADS = 12

U_KV0 = 0
U_RET = 4
U_ATT0 = U_RET + 3 + 4 * (GROUPS - 1)
U_KV1 = U_ATT0 + 7
U_GDN = U_KV1 + 4
U_ATT1 = U_GDN + 3 + 4 * (GROUPS - 1)
U_HG = U_ATT1 + 7
U_P0 = U_HG + 8
U_MLP = U_P0 + 6
UNITS = U_MLP + 2 * FFG
W_RET = 4
W_ATT0 = W_RET + 3 * GROUPS
W_KV1 = W_ATT0 + 4
W_GDN = W_KV1 + 4
W_ATT1 = W_GDN + 3 * GROUPS
W_HG = W_ATT1 + 4
W_MLP = W_HG + 10
B_L1, B_HG, B_MLP = BR, 2 * BR, 2 * BR + 4


def build(nc, x_in, mem_in, pos_in, w_ret, ret_g, w_gdn, conv_w, a_log, dt_bias, gdn_g, w_kv, w_out,
          ln_g, ln_b, w_in2, pool_w, pool_b, pool_scale, lb_logits, hgrn_w, w_out2, mix_pre, mix_post,
          mlp_pre, mlp_post, w_mlp_in, w_mlp_out, consts, out):
    f32, f32r, i32, u32 = mybir.dt.float32, mybir.dt.float32r, mybir.dt.int32, mybir.dt.uint32
    ALU, ACT, AX = mybir.AluOpType, mybir.ActivationFunctionType, mybir.AxisListType
    ds = bass.ds

    with ExitStack() as ctx:
        def sb(name, cols, dt=f32):
            return ctx.enter_context(nc.sbuf_tensor(name, [P, cols], dt))

        def psum(name):
            return ctx.enter_context(nc.psum_tensor(name, [P, COL], f32))

        def sem(name):
            return ctx.enter_context(nc.semaphore(name))

        raw = [sb(f"raw{j}", KB * COL) for j in range(4)]
        whi = [sb(f"whi{j}", KB * COL, f32r) for j in range(2)]
        wlo = [sb(f"wlo{j}", KB * COL, f32r) for j in range(2)]
        a_hi, a_lo = sb("a_hi", 16 * SEQ, f32r), sb("a_lo", 16 * SEQ, f32r)
        b_hi, b_lo = sb("b_hi", KB * SEQ, f32r), sb("b_lo", KB * SEQ, f32r)
        x_sb = sb("x_sb", TT * D)
        kv = sb("kv", 2 * 8 * SEQ)
        mk, mv, y_sb = kv[:, 0:8 * SEQ], kv[:, 8 * SEQ:], kv[:, :]
        cst = sb("cst", C_MAIN)
        ones = sb("ones", P)
        cols = sb("cols", 3 * P)
        small = sb("small", 256)
        gates = sb("gates", 6 * TT * NVH)
        eps_sb, lb, pos_sb = sb("eps_sb", 2), sb("lb", 16), sb("pos_sb", TT, i32)
        n0, n1 = sb("n0", 1024), sb("n1", 1024)
        zs, br = sb("zs", 1024), sb("br", 1024)
        cb = sb("cb", 4 * (SEQ + 3))
        cv, sq = sb("cv", 1024), sb("sq", 1024)
        kn, vn, st = sb("kn", COL), sb("vn", COL), sb("st", COL)
        big = sb("big", 6 * 1024)
        lnw = big[:, 0:2 * D]
        dn, dt_, lw, xi, ui, pi = (big[:, k * 1024:(k + 1) * 1024] for k in range(6))
        ident, tri, low, negm1 = (cst[:, c:c + P] for c in (C_ID, C_TRI, C_LOW, C_M1))

        def level_mask(n):
            return cst[:, C_LV + n * P:C_LV + (n + 1) * P]

        acc = [[psum(f"acc{p}{t}") for t in range(TT)] for p in range(2)]
        bank = [psum(f"bank{b}") for b in range(4)]

        raw_loaded = [sem(f"raw_loaded{j}") for j in range(4)]
        hi_ready, lo_ready = sem("hi_ready"), sem("lo_ready")
        sub_used = sem("sub_used")
        wide_taken = sem("wide_taken")
        out_added = sem("out_added")
        filled = [sem(f"filled{b}") for b in range(4)]
        emptied = [sem(f"emptied{b}") for b in range(4)]
        a_hi_in, b_hi_in = sem("a_hi_in"), sem("b_hi_in")
        mem_loaded = [sem(f"mem_loaded{c}") for c in range(2)]
        names = ("ab_hi ab_lo ab_loaded branch_ready cols_ready cols_turned consts_loaded conv_done decay_loaded "
                 "decay_ready g_ready gate_dve gate_step gs_ready h_ready kn_ready ksc_ready lb_arg lb_ready "
                 "lev_arg lev_exp lev_ready ln_root ln_stats logf_ready lower_ready mneg ones_made out_ready "
                 "pool_hi pool_in pool_loaded pool_mapped pos_loaded rms_root root_ready rot_ready rows_loaded "
                 "rows_spread scale_ready shape_constants silu_done squared squares_summed stats stored trig_arg "
                 "trig_ready unit_ready x_final x_loaded y_ready ").split()
        s = {n: sem(n) for n in names}
        block = ctx.enter_context(nc.Block())

        @block.sync
        def _(sp):
            def load(m, j, first, second):
                if not (isinstance(m, int) and m == 0):
                    sp.wait_ge(lo_ready, 4 * m + j - 3)
                view = raw[j][:, :].rearrange("p (k c) -> p k c", k=KB)
                for dst, src in ((first[0](view), first[1]), (second[0](view), second[1])):
                    sp.dma_start(dst, src.rearrange("(k p) c -> p k c", p=P)).then_inc(raw_loaded[j], 16)

            def wide(m, w, col):
                for j in range(4):
                    load(m, j,
                         (lambda v: v[:, 0:2, :], w[COL * j:COL * j + 256, ds(col, COL)]),
                         (lambda v: v[:, 2:4, :], w[COL * j + 256:COL * j + COL, ds(col, COL)]))

            def wide_qk(m, w, g):
                for j in range(4):
                    rows = slice(COL * j, COL * (j + 1))
                    load(m, j,
                         (lambda v: v[:, :, 0:256], w[rows, ds(256 * g, 256)]),
                         (lambda v: v[:, :, 256:512], w[rows, ds(QKW + 256 * g, 256)]))

            def tall(m, w, row):
                for j in range(4):
                    for_cols = slice(COL * j, COL * (j + 1))
                    load(m, j,
                         (lambda v: v[:, 0:2, :], w[ds(row, 256), for_cols]),
                         (lambda v: v[:, 2:4, :], w[ds(row + 256, 256), for_cols]))

            def kv_units(m, layer):
                for c in range(4):
                    wide(m + c, w_kv[layer], COL * c)

            def layer(m, w, wo):
                wide_qk(m, w, 0)
                wide(m + 1, w, 2 * QKW)
                wide(m + 2, w, CONV + MEMW)
                with sp.Fori(1, GROUPS) as g:
                    at = 4 * g + (m - 1)
                    wide_qk(at, w, g)
                    wide(at + 1, w, 2 * QKW + COL * g)
                    tall(at + 2, wo, COL * (g - 1))
                    wide(at + 3, w, CONV + MEMW + COL * g)
                m += 3 + 4 * (GROUPS - 1)
                for g in range(MGROUPS):
                    wide(m, w, CONV + COL * g)
                    wide(m + 1, w, CONV + MEMW + TOK + COL * g)
                    tall(m + 2, wo, COL * (GROUPS + g - 1))
                    m += 3
                tall(m, wo, COL * (BR - 1))

            kv_units(U_KV0, 0)
            layer(U_RET, w_ret[0], w_out[0])
            kv_units(U_KV1, 1)
            layer(U_GDN, w_gdn[0], w_out[1])
            for g in range(2):
                for n in range(4):
                    wide(U_HG + 4 * g + n, w_in2[0], 1024 + 1024 * n + COL * g)
            wide(U_P0, w_in2[0], 0)
            tall(U_P0 + 1, w_out2[0], 1024)
            wide(U_P0 + 2, w_in2[0], COL)
            tall(U_P0 + 3, w_out2[0], 1024 + COL)
            tall(U_P0 + 4, w_out2[0], 0)
            tall(U_P0 + 5, w_out2[0], COL)
            wide(U_MLP, w_mlp_in[0], 0)
            with sp.Fori(1, FFG) as g:
                wide(2 * g + (U_MLP - 1), w_mlp_in[0], COL * g)
                tall(2 * g + U_MLP, w_mlp_out[0], COL * (g - 1))
            tall(UNITS - 1, w_mlp_out[0], COL * (FFG - 1))
            for t in range(TT):
                sp.wait_ge(s["out_ready"], t + 1)
                sp.dma_start(out[0, t * P:(t + 1) * P, :], x_sb[:, t * D:(t + 1) * D]).then_inc(s["stored"], 16)
            sp.wait_ge(s["stored"], 16 * TT)

        @block.gpsimd
        def _(pool):
            pool.memset(ones[:, :], 1.0).then_inc(s["ones_made"], 1)
            for n, eps in enumerate((LN_EPS, EPS)):
                pool.memset(eps_sb[:, n:n + 1], eps).then_inc(s["ones_made"], 1)
            with pool.Fori(0, UNITS) as m:
                for j in range(4):
                    pool.wait_ge(hi_ready, 4 * m + j + 1)
                    pool.tensor_tensor(wlo[j % 2][:, :], raw[j][:, :], whi[j % 2][:, :].bitcast(f32),
                                       ALU.subtract).then_inc(lo_ready, 1)

        @block.tensor
        def _(pe):
            def sub(m, j, hi_t, lo_t, block0, pair, start, stop):
                pe.wait_ge(lo_ready, 4 * m + j + 1)
                for t in range(TT):
                    dst = acc[pair][t][:, :]
                    for k in range(KB):
                        at = (block0 + k) * SEQ + t * P
                        h, l = hi_t[:, at:at + P], lo_t[:, at:at + P]
                        w_h, w_l = (w[j % 2][:, k * COL:(k + 1) * COL] for w in (whi, wlo))
                        pe.matmul(dst, l, w_h, start=start and k == 0, stop=False)
                        pe.matmul(dst, h, w_l, start=False, stop=False)
                        mm = pe.matmul(dst, h, w_h, start=False, stop=stop and k == KB - 1)
                mm.then_inc(sub_used, 1)

            def wide(m, pair, taken, added, between=None):
                if not (isinstance(taken, int) and taken == 0):
                    pe.wait_ge(wide_taken, 2 * taken)
                if not (isinstance(added, int) and added == 0):
                    pe.wait_ge(out_added, 2 * added + 1)
                for j in range(4):
                    sub(m, j, a_hi, a_lo, 4 * j, pair, j == 0, j == 3)
                    if between:
                        between(j)

            def in_place(phase, step, g=0):
                b, n = fill(phase, step, g)
                pe.wait_ge(emptied[b], n)

            def tall(m, b, pair, taken, parts, between=None, added=None, after_tall=False):
                if parts[0] == "pool":
                    pe.wait_ge(s["pool_in"], parts[1] + 1)
                else:
                    in_place(parts[0], "ba", parts[1])
                    in_place(parts[0], "bb", parts[1])
                pe.wait_ge(wide_taken, 2 * taken - 2)
                if added is not None:
                    pe.wait_ge(out_added, 2 * added + 1)
                for j in range(4):
                    if j == 1:
                        pe.wait_ge(wide_taken, 2 * taken)
                    if after_tall or j >= 2:
                        pe.wait_ge(out_added, 2 * (4 * b + j - 1) + 1)
                    sub(m, j, b_hi, b_lo, 0, (pair + j) % 2, True, True)
                    if between:
                        between(j)

            def take(phase, step, g=0):
                b, n = fill(phase, step, g)
                if not (isinstance(n, int) and n == 1):
                    pe.wait_ge(emptied[b], n - 1)
                return bank[b], filled[b]

            def turn(phase, step, g, block):
                dst, done = take(phase, step, g)
                for k in range(2):
                    for t in range(TT):
                        at = k * SEQ + t * P
                        tr = pe.transpose(dst[:, at:at + P], block(k, t), ident)
                tr.then_inc(done, 1)

            def turn_natural(phase, steps, g, src):
                for n, step in enumerate(steps):
                    turn(phase, step, g, lambda k, t: src[:, t * COL + (2 * n + k) * P:t * COL + (2 * n + k + 1) * P])

            def turn_x(phase, src):
                for f in range(8):
                    turn(phase, f"f{f}", 0, lambda k, t: src[:, t * D + (2 * f + k) * P:t * D + (2 * f + k + 1) * P])

            def turn_mem(phase, layer):
                for c in range(4):
                    pe.wait_ge(mem_loaded[c % 2], 16 * (2 * layer + c // 2 + 1))
                    turn_natural(phase, (f"f{2 * c}", f"f{2 * c + 1}"), 0, (n1, n0)[c % 2])

            def a_in_place(phase):
                for f in range(4, 8):
                    in_place(phase, f"f{f}")

            def branch(phase, g, b):
                pe.wait_ge(s["branch_ready"], b + 1)
                turn_natural(phase, ("ba", "bb"), g, br)

            def kv_units(phase, m, w, turned, added):
                a_in_place(turned)

                def keys(c):
                    def between(j):
                        if j == 1:
                            pe.wait_ge(wide_taken, 2 * (w + c + 1))
                            turn_natural(phase, (f"k{c}a", f"k{c}b"), 0, n0)
                    return between
                wide(m, 0, w, added)
                wide(m + 1, 1, w, added, keys(0))
                wide(m + 2, 0, w + 1, added, keys(1))
                wide(m + 3, 1, w + 2, added)

            def ret_qk(g):
                pe.wait_ge(s["rot_ready"], g + 1)
                turn_natural("ret", ("q", "k"), g, cv)

            def ret_scores(g):
                in_place("ret", "q", g)
                in_place("ret", "k", g)
                for h in range(2):
                    dst, done = take("ret", f"s{h}", g)
                    q, k = lw[:, h * SEQ:(h + 1) * SEQ], lw[:, COL + h * SEQ:COL + (h + 1) * SEQ]
                    pe.matmul(dst[:, 0:SEQ], k[:, 0:P], q, start=True, stop=True)
                    pe.matmul(dst[:, SEQ:SEQ + P], k[:, P:SEQ], q[:, P:SEQ], start=True, stop=True).then_inc(done, 1)

            def ret_out(g):
                pe.wait_ge(wide_taken, 2 * (W_RET + 3 * g + 2))
                for h in range(2):
                    in_place("ret", f"s{h}", g)
                    dst, done = take("ret", f"o{h}", g)
                    p = pi[:, h * 384:(h + 1) * 384]
                    v = [n1[:, t * COL + h * SEQ:t * COL + (h + 1) * SEQ] for t in range(TT)]
                    pe.matmul(dst[:, 0:SEQ], p[:, 0:P], v[0], start=True, stop=True)
                    pe.matmul(dst[:, SEQ:COL], p[:, P:2 * P], v[0], start=True, stop=False)
                    pe.matmul(dst[:, SEQ:COL], p[:, 2 * P:384], v[1], start=False, stop=True).then_inc(done, 1)

            def gdn_gates():
                pe.wait_ge(s["ab_lo"], 1)
                dst, done = take("gates", "ab")
                n = 2 * NVH
                for t in range(TT):
                    for k in range(16):
                        at = k * SEQ + t * P
                        h, l = a_hi[:, at:at + P], a_lo[:, at:at + P]
                        w_h, w_l = (w[:, k * n:(k + 1) * n] for w in (b_hi, b_lo))
                        pe.matmul(dst[:, t * n:(t + 1) * n], l, w_h, start=k == 0, stop=False)
                        pe.matmul(dst[:, t * n:(t + 1) * n], h, w_l, start=False, stop=False)
                        mm = pe.matmul(dst[:, t * n:(t + 1) * n], h, w_h, start=False, stop=k == 15)
                mm.then_inc(done, 1)
                pe.wait_ge(s["g_ready"], 1)
                for step, lhs in (("cum", tri), ("last", ones[:, :])):
                    dst, done = take("gates", step)
                    pe.matmul(dst[:, 0:n], lhs, gates[:, 0:n], start=True, stop=True).then_inc(done, 1)

            def head(t, buf, hh):
                return buf[:, t * COL + hh * P:t * COL + (hh + 1) * P]

            def gdn_qk(g):
                pe.wait_ge(wide_taken, 2 * (W_GDN + 3 * g + 1))
                turn_natural("gdn", ("q", "k"), g, n0)

            def gdn_norms(g):
                pe.wait_ge(s["squared"], g + 1)
                for n, step in enumerate(("sq", "sk")):
                    dst, done = take("gdn", step, g)
                    pe.matmul(dst[:, :], ones[:, :], sq[:, n * COL:(n + 1) * COL], start=True, stop=True).then_inc(done, 1)

            def gdn_products(g):
                pe.wait_ge(s["unit_ready"], g + 1)
                dst, done = take("gdn", "kn", g)
                for h in range(2):
                    for t in range(TT):
                        at = COL + h * SEQ + t * P
                        tr = pe.transpose(dst[:, (2 * t + h) * P:(2 * t + h + 1) * P], cv[:, at:at + P], ident)
                tr.then_inc(done, 1)
                pe.wait_ge(s["gs_ready"], g + 1)
                for t in range(TT):
                    dst, done = take("gdn", f"row{t}", g)
                    for hh in range(4):
                        mm = pe.matmul(dst[:, hh * P:(hh + 1) * P], small[:, 4 * t + hh:4 * t + hh + 1].to_broadcast([P, P]),
                                       tri, start=True, stop=True)
                    mm.then_inc(done, 1)
                for step, off in (("kk", COL), ("qk", 0)):
                    dst, done = take("gdn", step, g)
                    for t in range(TT):
                        for h in range(2):
                            at = h * SEQ + t * P
                            mm = pe.matmul(dst[:, (2 * t + h) * P:(2 * t + h + 1) * P], cv[:, COL + at:COL + at + P],
                                           cv[:, off + at:off + at + P], start=True, stop=True)
                    mm.then_inc(done, 1)

            def gdn_first(g):
                for t in range(TT):
                    pe.wait_ge(s["lower_ready"], 2 * g + t + 1)
                    dst, done = take("gdn", f"u{t}", g)
                    for hh in range(4):
                        tr = pe.transpose(dst[:, hh * P:(hh + 1) * P], head(t, xi, hh), ident)
                    tr.then_inc(done, 1)

            def gdn_level(g, n):
                size, last = LEVELS[n], n == len(LEVELS) - 1
                for t in range(TT):
                    in_place("gdn", f"u{t}" if n == 1 else f"n{size // 2}_{t}", g)
                    dst, done = take("gdn", f"p{size}_{t}", g)
                    for hh in range(4):
                        mm = pe.matmul(dst[:, hh * P:(hh + 1) * P], head(t, lw, hh), head(t, ui, hh), start=True, stop=True)
                    mm.then_inc(done, 1)
                for t in range(TT):
                    in_place("gdn", f"p{size}_{t}", g)
                    dst, done = take("gdn", f"n{size}_{t}", g)

                    def half(ap, side):
                        return ap.rearrange("p (n two s) -> p n two s", two=2, s=size)[:, :, side, :]

                    def to(at):
                        return dst[:, at:at + 64].rearrange("p (n s) -> p n s", s=size)
                    for hh in range(4):
                        mm = pe.matmul(to(hh * 64), head(t, xi, hh), half(head(t, pi, hh), 1), start=True, stop=True)
                        if not last:
                            mm = pe.matmul(to(256 + hh * 64), head(t, pi, hh), half(head(t, xi, hh), 0), start=True, stop=True)
                    mm.then_inc(done, 1)

            def gdn_v(g):
                pe.wait_ge(wide_taken, 2 * (W_GDN + 3 * g + 2))
                turn_natural("gdn", ("va", "vb"), g, n1)

            def gdn_v_back(g):
                pe.wait_ge(s["silu_done"], 2 * g + 2)
                for t, step in enumerate(("va2", "vb2")):
                    dst, done = take("gdn", step, g)
                    for k in range(4):
                        tr = pe.transpose(dst[:, k * P:(k + 1) * P], sq[:, k * SEQ + t * P:k * SEQ + (t + 1) * P], ident)
                    tr.then_inc(done, 1)

            def per_head(step, g, lhs, rhs):
                dst, done = take("gdn", step, g)
                for hh in range(4):
                    mm = pe.matmul(dst[:, hh * P:(hh + 1) * P], lhs(hh), rhs[:, hh * P:(hh + 1) * P], start=True, stop=True)
                mm.then_inc(done, 1)

            def gdn_run(g):
                for t in range(TT):
                    in_place("gdn", f"n64_{t}", g)
                in_place("gdn", "va2", g)
                in_place("gdn", "vb2", g)
                per_head("vn0", g, lambda hh: head(0, ui, hh), n1[:, 0:COL])
                in_place("gdn", "vn0", g)
                per_head("o0", g, lambda hh: head(0, dt_, hh), vn)
                pe.wait_ge(s["kn_ready"], g + 1)
                per_head("st", g, lambda hh: head(0, xi, hh), vn)
                in_place("gdn", "st", g)
                for step, off in (("ks", COL), ("qs", 0)):
                    dst, done = take("gdn", step, g)
                    for h in range(2):
                        at = off + h * SEQ + P
                        mm = pe.matmul(dst[:, h * SEQ:(h + 1) * SEQ], cv[:, at:at + P], st[:, h * SEQ:(h + 1) * SEQ],
                                       start=True, stop=True)
                    mm.then_inc(done, 1)
                in_place("gdn", "ks", g)
                per_head("vn1", g, lambda hh: head(1, ui, hh), xi[:, COL:2 * COL])
                in_place("gdn", "vn1", g)
                per_head("o1", g, lambda hh: head(1, dt_, hh), vn)

            def att_q(phase, g, w):
                pe.wait_ge(wide_taken, 2 * (w + 1))
                turn_natural(phase, ("qa", "qb"), g, n0)

            def att_scores(phase, g):
                in_place(phase, "qa", g)
                in_place(phase, "qb", g)
                for t in range(TT):
                    dst, done = take(phase, f"s{t}", g)
                    for h in range(2):
                        for k in range(2):
                            c = 2 * h + k
                            mm = pe.matmul(dst[:, h * SEQ:(h + 1) * SEQ], cv[:, c * SEQ + t * P:c * SEQ + (t + 1) * P],
                                           mk[:, (4 * g + c) * SEQ:(4 * g + c + 1) * SEQ], start=k == 0, stop=k == 1)
                    mm.then_inc(done, 1)

            def att_turn(phase, g):
                in_place(phase, "s0", g)
                in_place(phase, "s1", g)
                for h, step in enumerate(("pa", "pb")):
                    turn(phase, step, g, lambda k, t: lw[:, t * COL + h * SEQ + k * P:t * COL + h * SEQ + (k + 1) * P])

            def att_out(phase, g):
                in_place(phase, "pa", g)
                in_place(phase, "pb", g)
                for t in range(TT):
                    dst, done = take(phase, f"o{t}", g)
                    for h in range(2):
                        for k in range(2):
                            at = h * COL + k * SEQ + t * P
                            v = k * 1024 + g * COL + h * SEQ
                            mm = pe.matmul(dst[:, h * SEQ:(h + 1) * SEQ], ui[:, at:at + P], mv[:, v:v + SEQ],
                                           start=k == 0, stop=k == 1)
                    mm.then_inc(done, 1)

            def layer(m, w, b0, early, late, phase, att):
                def body(g, first=False):
                    at = m if first else 4 * g + (m - 1)
                    wq = w + 3 * g
                    b = b0 + g - 1

                    def in_qk(j):
                        if not first and j == 2:
                            branch(phase, g - 1, b)
                    wide(at, 0, wq, 0, in_qk)
                    wide(at + 1, 1, wq if first else wq - 1, 4 * b0 if first else 4 * b, lambda j: early(g, j))
                    if first:
                        wide(at + 2, 0, wq + 1, 4 * b0, lambda j: late(g, j, True))
                    else:
                        tall(at + 2, b, 0, wq + 2, (phase, g - 1), lambda j: late(g, j))
                        wide(at + 3, 0, wq + 2, 4 * b + 3, lambda j: late(g, j + 4))
                body(0, True)
                with pe.Fori(1, GROUPS) as g:
                    body(g)
                m += 3 + 4 * (GROUPS - 1)
                w += 3 * GROUPS
                for g in range(MGROUPS):
                    b = b0 + GROUPS + g

                    def in_q(j):
                        if j == 2 and g == 0:
                            branch(phase, GROUPS - 1, b - 1)
                        elif j == 2:
                            branch(att, g - 1, b - 1)

                    def in_z(j):
                        if j == 1:
                            att_q(att, g, w + 2 * g)
                        if j == 3:
                            att_scores(att, g)

                    def in_out(j):
                        if j == 1:
                            att_turn(att, g)
                        if j == 2:
                            att_out(att, g)
                    wide(m, 0, w + 2 * g, 4 * (b - 1), in_q)
                    wide(m + 1, 1, w + 2 * g, 4 * (b - 1), in_z)
                    tall(m + 2, b - 1, 0, w + 2 * g + 2, (att, g - 1) if g else (phase, GROUPS - 1), in_out)
                    m += 3
                branch(att, MGROUPS - 1, b0 + BR - 1)
                tall(m, b0 + BR - 1, 0, w + 4, (att, MGROUPS - 1), after_tall=True)

            def ret_early(g, j):
                if j == 1:
                    ret_qk(g)
                if j == 3:
                    ret_scores(g)

            def ret_late(g, j, first=False):
                if j == 1:
                    ret_out(g)

            def gdn_early(g, j):
                if j == 1:
                    gdn_qk(g)
                if j == 3:
                    gdn_norms(g)

            def gdn_late(g, j, first=False):
                for n in (2 * j, 2 * j + 1) if first else (j,):
                    if n == 0:
                        gdn_products(g)
                    elif n <= 6:
                        if n == 1:
                            gdn_first(g)
                        gdn_level(g, n)
                    else:
                        gdn_v(g)
                        gdn_v_back(g)
                        gdn_run(g)

            def hgrn_turn(g):
                pe.wait_ge(wide_taken, 2 * (W_HG + 4 * g + 1))
                turn_natural("hgrn", ("qa", "qb"), g, n0)
                pe.wait_ge(wide_taken, 2 * (W_HG + 4 * g + 2))
                turn_natural("hgrn", ("fa", "fb"), g, n1)

            def hgrn_diagonal(g):
                in_place("hgrn", "qa", g)
                in_place("hgrn", "qb", g)
                pe.wait_ge(s["ksc_ready"], g + 1)
                for t in range(TT):
                    dst, done = take("hgrn", f"d{t}", g)
                    for hh in range(4):
                        at = hh * SEQ + t * P
                        mm = pe.matmul(dst[:, hh * P:(hh + 1) * P], lw[:, at:at + P], cv[:, at:at + P], start=True, stop=True)
                    mm.then_inc(done, 1)

            def hgrn_level(g, n):
                pe.wait_ge(s["lev_ready"], 8 * g + n + 1)
                ks, qs = (xi, ui)[n % 2], dn[:, (n % 2) * COL:(n % 2 + 1) * COL]
                dst, done = take("hgrn", "x" if n == 7 else f"l{LEVELS[n]}", g)
                for hh in range(4):
                    if n == 7:
                        mm = pe.matmul(dst[:, hh * P:(hh + 1) * P], ks[:, hh * SEQ:hh * SEQ + P], qs[:, hh * P:(hh + 1) * P],
                                       start=True, stop=True)
                        continue
                    for t in range(TT):
                        at = (2 * hh + t) * 64
                        mm = pe.matmul(dst[:, at:at + 64], ks[:, hh * SEQ + t * P:hh * SEQ + (t + 1) * P], qs[:, at:at + 64],
                                       start=True, stop=True)
                mm.then_inc(done, 1)

            def hgrn_out(g):
                pe.wait_ge(wide_taken, 2 * (W_HG + 4 * g + 3))
                in_place("hgrn", "x", g)
                in_place("hgrn", "l64", g)
                for t in range(TT):
                    dst, done = take("hgrn", f"o{t}", g)
                    for hh in range(4):
                        to, at = dst[:, hh * P:(hh + 1) * P], hh * P
                        own = dt_[:, (2 * hh + t) * P:(2 * hh + t + 1) * P]
                        if t:
                            pe.matmul(to, kn[:, at:at + P], vn[:, at:at + P], start=True, stop=False)
                        mm = pe.matmul(to, own, (vn, st)[t][:, at:at + P], start=t == 0, stop=True)
                    mm.then_inc(done, 1)

            def pool_bands(g):
                src = (n0, n1)[g]
                pe.wait_ge(wide_taken, 2 * (W_HG + 8 + g + 1))
                pe.wait_ge(s["pool_loaded"], 32)
                for n, step in enumerate(("da", "db")):
                    dst, done = take("pool", step, g)
                    band = big[:, 2048 + (2 * g + n) * 384:2048 + (2 * g + n + 1) * 384]
                    for k in range(2):
                        c = (2 * n + k) * P
                        pe.matmul(dst[:, k * SEQ:k * SEQ + P], src[:, c:c + P], band[:, 0:P], start=True, stop=True)
                        pe.matmul(dst[:, k * SEQ + P:(k + 1) * SEQ], src[:, c:c + P], band[:, P:2 * P], start=True, stop=False)
                        mm = pe.matmul(dst[:, k * SEQ + P:(k + 1) * SEQ], src[:, COL + c:COL + c + P], band[:, 2 * P:384],
                                       start=False, stop=True)
                    mm.then_inc(done, 1)

            def pool_maps(g):
                in_place("pool", "da", g)
                in_place("pool", "db", g)
                for n, step in enumerate(("ya", "yb")):
                    dst, done = take("pool", step, g)
                    for c in range(2):
                        for k in range(2):
                            at = 4096 + ((2 * g + n) * 2 + k) * SEQ + c * P
                            mm = pe.matmul(dst[:, c * SEQ:(c + 1) * SEQ], big[:, at:at + P],
                                           cv[:, (2 * n + k) * SEQ:(2 * n + k + 1) * SEQ], start=k == 0, stop=k == 1)
                    mm.then_inc(done, 1)

            pe.wait_ge(s["ones_made"], 1)
            pe.wait_ge(s["consts_loaded"], 16)
            pe.wait_ge(s["rows_loaded"], 16 * N_LOADS)
            for r, rows in enumerate((N_ROWS, 96, 96)):
                tr = pe.transpose(acc[0][0][:, r * P:r * P + rows], zs[0:rows, r * P:(r + 1) * P], ident[0:rows, 0:rows])
            tr.then_inc(s["cols_turned"], 1)
            turn_mem("mem0", 0)
            pe.wait_ge(s["cols_ready"], 1)
            kv_units("kv0", U_KV0, 0, "mem0", 0)
            pe.wait_ge(s["x_loaded"], 16)
            turn_x("x0", x_sb)
            a_in_place("x0")
            layer(U_RET, W_RET, 0, ret_early, ret_late, "ret", "att0")
            turn_mem("mem1", 1)
            kv_units("kv1", U_KV1, W_KV1, "mem1", 4 * B_L1)
            pe.wait_ge(s["x_final"], 1)
            turn_x("x1", x_sb)
            a_in_place("x1")
            gdn_gates()
            layer(U_GDN, W_GDN, B_L1, gdn_early, gdn_late, "gdn", "att1")
            pe.wait_ge(s["h_ready"], 1)
            turn_x("h2", y_sb)
            a_in_place("h2")

            def in_h1(n):
                def between(j):
                    if n == 0 and j == 1:
                        hgrn_diagonal(0)
                    elif n < 3 and j in (0, 2) and n:
                        hgrn_level(0, 2 * (2 * n - 2) + j)
                        hgrn_level(0, 2 * (2 * n - 2) + j + 1)
                    elif n == 3 and j == 1:
                        hgrn_out(0)
                return between

            def in_p0(j):
                if j == 2:
                    branch("hgrn", 0, B_HG)
                if j == 3:
                    hgrn_turn(1)

            def in_oh0(j):
                if j == 1:
                    hgrn_diagonal(1)
                if j >= 2:
                    hgrn_level(1, 2 * j - 4)
                    hgrn_level(1, 2 * j - 3)

            def in_p1(j):
                if j < 2:
                    hgrn_level(1, 4 + 2 * j)
                    hgrn_level(1, 5 + 2 * j)
                if j == 3:
                    hgrn_out(1)

            w = W_HG
            for n in range(4):
                wide(U_HG + n, n % 2, w + max(n - 1, 0), 4 * B_HG)
            hgrn_turn(0)
            for n in range(4):
                wide(U_HG + 4 + n, n % 2, w + 3 + n, 4 * B_HG, in_h1(n))
            wide(U_P0, 0, w + 7, 4 * B_HG, in_p0)
            tall(U_P0 + 1, B_HG, 1, w + 9, ("hgrn", 0), in_oh0)
            wide(U_P0 + 2, 1, w + 9, 4 * B_HG + 3, in_p1)
            branch("hgrn", 1, B_HG + 1)
            pool_bands(0)
            tall(U_P0 + 3, B_HG + 1, 0, w + 10, ("hgrn", 1), lambda j: pool_maps(0) if j == 1 else None, added=4 * B_HG + 4)
            pool_bands(1)
            tall(U_P0 + 4, B_HG + 2, 0, w + 10, ("pool", 0), lambda j: pool_maps(1) if j == 1 else None, after_tall=True)
            tall(U_P0 + 5, B_HG + 3, 0, w + 10, ("pool", 1), after_tall=True)
            pe.wait_ge(s["h_ready"], 2)
            turn_x("h3", y_sb)
            a_in_place("h3")

            def mlp(g, pair):
                b = g + (B_MLP - 1)
                wide(2 * g + (U_MLP - 1), pair, g + (W_MLP - 1), 4 * b - 1,
                     lambda j: branch("mlp", g - 1, b - 2) if j == 1 else None)
                tall(2 * g + U_MLP, b, 1 - pair, g + (W_MLP + 1), ("mlp", g - 1), added=4 * b)
            wide(U_MLP, 0, W_MLP, 4 * B_MLP)
            with pe.Fori(0, (FFG - 2) // 2) as r:
                mlp(2 * r + 1, 1)
                mlp(2 * r + 2, 0)
            mlp(FFG - 1, 1)
            branch("mlp", FFG - 1, B_MLP + FFG - 3)
            tall(UNITS - 1, B_MLP + FFG - 1, 0, W_MLP + FFG, ("mlp", FFG - 1), after_tall=True)

        @block.scalar
        def _(act):
            def hi(m, j):
                act.wait_ge(raw_loaded[j], 32 * m + 32)
                if not (isinstance(m, int) and 4 * m + j < 2):
                    act.wait_ge(sub_used, 4 * m + j - 1)
                act.activation(whi[j % 2][:, :], raw[j][:, :], ACT.Copy).then_inc(hi_ready, 1)

            def unit(m, between=None, first=0):
                for j in range(first, 4):
                    hi(m, j)
                    if between:
                        between(j)

            def ahead(m):
                hi(m, 0)
                hi(m, 1)

            def wide_out(m, pair, func, dst):
                act.wait_ge(sub_used, 4 * m + 4)
                for t in range(TT):
                    act.activation(dst(t), acc[pair][t][:, :], func).then_inc(wide_taken, 1)

            def gate(n):
                return gates[:, n * TT * NVH:(n + 1) * TT * NVH].rearrange("p (t c) -> p t c", t=TT)

            def tiles(buf):
                return lambda t: buf[:, t * COL:(t + 1) * COL]

            def full(phase, step, g=0):
                b, n = fill(phase, step, g)
                act.wait_ge(filled[b], n)
                return bank[b], emptied[b]

            def copy_out(phase, step, g, dst, src=lambda b: b[:, :], func=ACT.Copy, **kw):
                b, done = full(phase, step, g)
                act.activation(dst, src(b), func, **kw).then_inc(done, 1)

            def a_parts(phase, used, scale=None):
                if used:
                    act.wait_ge(sub_used, 4 * used)
                for f in range(8):
                    b, _ = full(phase, f"f{f}")
                    for k in range(2) if scale is not None else [None]:
                        if k is None:
                            op = act.activation(a_hi[:, f * COL:(f + 1) * COL], b[:, :], ACT.Copy)
                        else:
                            at = f * COL + k * SEQ
                            op = act.activation(a_hi[:, at:at + SEQ], b[:, k * SEQ:(k + 1) * SEQ], ACT.Copy,
                                                scale=cols[:, scale + 2 * f + k:scale + 2 * f + k + 1])
                    op.then_inc(a_hi_in, 1)

            def b_parts(phase, g, used, scale=None):
                if used is not None:
                    act.wait_ge(sub_used, 4 * used)
                for n, step in enumerate(("ba", "bb")):
                    b, _ = full(phase, step, g)
                    if scale is None:
                        op = act.activation(b_hi[:, n * COL:(n + 1) * COL], b[:, :], ACT.Copy)
                    else:
                        for k in range(2):
                            at = n * COL + k * SEQ
                            op = act.activation(b_hi[:, at:at + SEQ], b[:, k * SEQ:(k + 1) * SEQ], ACT.Copy,
                                                scale=scale(2 * n + k))
                    op.then_inc(b_hi_in, 1)

            def mem_load(layer, c):
                src = mem_in[0][:, c * COL:(c + 1) * COL].rearrange("(t p) c -> p t c", p=P)
                dst = (n1, n0)[c % 2][:, :].rearrange("p (t c) -> p t c", t=TT)
                act.dma_start(dst, src).then_inc(mem_loaded[c % 2], 16)

            def mem_parts(phase, layer, used):
                if used:
                    act.wait_ge(sub_used, 4 * used)
                for f in range(8):
                    b, _ = full(phase, f"f{f}")
                    act.activation(a_hi[:, f * COL:(f + 1) * COL], b[:, :], ACT.Copy).then_inc(a_hi_in, 1)
                    if f % 2 and f < 4:
                        mem_load(layer, f // 2 + 2)

            def kv_slots(phase, m, middle=lambda: None):
                def k_out(c, n):
                    def between(j):
                        if j == 0:
                            wide_out(m + n, n % 2, ACT.Copy, tiles(n0))
                        if j == 2:
                            for i, step in enumerate("ab"):
                                at = (4 * c + 2 * i) * SEQ
                                copy_out(phase, f"k{c}{step}", 0, mk[:, at:at + COL])
                    return between

                def v_out(c, n):
                    return lambda j: wide_out(m + n, n % 2, ACT.Copy, lambda t: mv[:, t * 1024 + c * COL:t * 1024 + (c + 1) * COL]) if j == 0 else None
                unit(m, None, 2)
                unit(m + 1, k_out(0, 0))
                middle()
                unit(m + 2, k_out(1, 1))
                unit(m + 3, v_out(0, 2))
                return v_out(1, 3)

            def root(after, n, dst, src, count, scale, eps):
                act.wait_ge(after, n)
                act.activation(small[:, dst:dst + count], src, ACT.Sqrt, scale=scale, bias=eps_sb[:, eps:eps + 1]).then_inc(s["root_ready"], 1)

            def layer(m, w, b0, steps, phase, att, scale, roots):
                def body(g, first=False):
                    at = m if first else 4 * g + (m - 1)

                    def in_qk(j):
                        if first:
                            return
                        if j == 0:
                            b, n = fill(phase, "ba", g - 2)
                            act.wait_ge(filled[b], n)
                            wide_out(at - 1, 0, ACT.Silu, tiles(zs))
                        if j == 3:
                            b_parts(phase, g - 1, at - 1, scale(g - 1))

                    def slots(base):
                        return lambda j: steps(g, base + j, at, first)
                    unit(at, in_qk, 2 if first else 0)
                    unit(at + 1, slots(0))
                    unit(at + 2, slots(4))
                    if not first:
                        unit(at + 3, slots(8))
                    else:
                        for j in range(8, 12):
                            steps(g, j, at, first)
                body(0, True)
                with act.Fori(1, GROUPS) as g:
                    body(g)
                m += 3 + 4 * (GROUPS - 1)
                for g in range(MGROUPS):
                    b = b0 + GROUPS + g

                    def in_q(j):
                        if j == 0 and g == 0:
                            act.wait_ge(s["branch_ready"], b - 1)
                            wide_out(m - 1, 0, ACT.Silu, tiles(zs))
                        if j == 3 and g == 0:
                            b_parts(phase, GROUPS - 1, m - 1, scale(GROUPS - 1))
                        elif j == 3:
                            b_parts(att, g - 1, m)

                    def in_z(j):
                        if j == 0:
                            if g == 0 and phase == "ret":
                                act.wait_ge(s["rot_ready"], GROUPS)
                            wide_out(m, 0, ACT.Copy, tiles(n0))
                        if j == 2:
                            for n, step in enumerate(("qa", "qb")):
                                copy_out(att, step, g, cv[:, n * COL:(n + 1) * COL])

                    def in_out(j):
                        if j == 0:
                            act.wait_ge(s["branch_ready"], b)
                            wide_out(m + 1, 1, ACT.Silu, tiles(zs))
                            for t in range(TT):
                                bk, done = full(att, f"s{t}", g)
                                act.wait_ge(s["mneg"], 2 * (n_att(att) + g) + t + 1)
                                for h in range(2):
                                    c = 2 * t + h
                                    op = act.activation(lw[:, c * SEQ:(c + 1) * SEQ], bk[:, h * SEQ:(h + 1) * SEQ], ACT.Exp,
                                                        scale=MSCALE, bias=small[:, 110 + c:111 + c],
                                                        accum_out=small[:, 120 + c:121 + c])
                                op.then_inc(done, 1)
                        if j == 2:
                            for n, step in enumerate(("pa", "pb")):
                                copy_out(att, step, g, ui[:, n * COL:(n + 1) * COL])
                    unit(m, in_q)
                    unit(m + 1, in_z)
                    unit(m + 2, in_out)
                    m += 3
                ahead(m)
                b_parts(att, MGROUPS - 1, m)
                unit(m, None, 2)

            def n_att(att):
                return 0 if att == "att0" else MGROUPS

            def ret_scale(g):
                def column(k):
                    return small[:, 104 + k:105 + k]
                act.activation(small[:, 104:108], cols[:, ds(4 * g + C_RG, 4)], ACT.Copy).then_inc(s["scale_ready"], 1)
                act.wait_ge(s["scale_ready"], g + 1)
                return column

            def decays(g):
                src = consts[:, ds(C_DEC + 2 * SEQ * g, 2 * SEQ)]
                act.dma_start(dt_[:, 0:2 * SEQ], src).then_inc(s["decay_loaded"], 16)

            def ret_steps(g, n, at, first):
                if n == 0:
                    if not first:
                        act.wait_ge(s["rot_ready"], g)
                        b, c = fill("ret", "s1", g - 1)
                        act.wait_ge(emptied[b], c)
                    wide_out(at, 0, ACT.Copy, tiles(n0))
                    decays(g)
                if n == 2:
                    for i, step in enumerate("qk"):
                        copy_out("ret", step, g, lw[:, i * COL:(i + 1) * COL])
                if n == 4:
                    if not first:
                        b, c = fill("ret", "o1", g - 1)
                        act.wait_ge(filled[b], c)
                    wide_out(at + 1, 1, ACT.Copy, tiles(n1))
                if n == 7:
                    root(s["stats"], g + 1, 36, small[:, 24:32].rearrange("p (n two) -> p n two", two=2)[:, :, 1], 4, 1.0, 1)

            def gdn_steps(g, n, at, first):
                if n == 0:
                    wide_out(at, 0, ACT.Copy, tiles(n0))
                if n == 2:
                    if not first:
                        act.wait_ge(s["conv_done"], 2 * g)
                    for i, step in enumerate("qk"):
                        copy_out("gdn", step, g, cb[:, :].rearrange("p (c s) -> p c s", c=4)[:, 2 * i:2 * i + 2, 3:],
                                 lambda b: b[:, :].rearrange("p (c s) -> p c s", c=2))
                if n == 3:
                    act.wait_ge(s["conv_done"], 2 * g + 1)
                    act.activation(cv[:, :], cv[:, :], ACT.Silu).then_inc(s["silu_done"], 1)
                    act.wait_ge(s["silu_done"], 2 * g + 1)
                    act.activation(sq[:, :], cv[:, :], ACT.Square).then_inc(s["squared"], 1)
                if n == 4:
                    if not first:
                        b, c = fill("gdn", "o1", g - 1)
                        act.wait_ge(filled[b], c)
                    wide_out(at + 1, 1, ACT.Copy, tiles(n1))
                    for i, step in enumerate(("sq", "sk")):
                        copy_out("gdn", step, g, dn[:, i * COL:(i + 1) * COL], func=ACT.Sqrt, bias=eps_sb[:, 1:2])
                if n == 5:
                    copy_out("gdn", "kn", g, kn[:, :])
                    for t in range(TT):
                        b, c = fill("gdn", f"row{t}", g)
                        act.wait_ge(emptied[b], c)
                    for i, buf in enumerate((dn, dt_)):
                        act.activation(buf[:, :], buf[:, :], ACT.Exp, scale=1.0 if i else -1.0).then_inc(s["decay_ready"], 1)
                    for t in range(TT):
                        copy_out("gdn", f"u{t}", g, ui[:, t * COL:(t + 1) * COL])
                if n == 11:
                    for i, step in enumerate(("va", "vb")):
                        copy_out("gdn", step, g, cb[:, :].rearrange("p (c s) -> p c s", c=4)[:, 2 * i:2 * i + 2, 3:],
                                 lambda b: b[:, :].rearrange("p (c s) -> p c s", c=2))
                    act.wait_ge(s["conv_done"], 2 * g + 2)
                    act.activation(sq[:, :], sq[:, :], ACT.Silu).then_inc(s["silu_done"], 1)
                    for t, step in enumerate(("va2", "vb2")):
                        b, done = full("gdn", step, g)
                        for hh in range(4):
                            at_ = t * COL + hh * P
                            op = act.activation(n1[:, at_:at_ + P], b[:, hh * P:(hh + 1) * P], ACT.Copy,
                                                scale=small[:, 16 + 4 * t + hh:17 + 4 * t + hh])
                        op.then_inc(done, 1)
                    copy_out("gdn", "vn0", g, vn[:, :])
                    copy_out("gdn", "st", g, st[:, :])
                    act.wait_ge(s["kn_ready"], g + 1)
                    b, done = full("gdn", "qs", g)
                    for hh in range(4):
                        op = act.activation(kn[:, hh * P:(hh + 1) * P], b[:, hh * P:(hh + 1) * P], ACT.Copy,
                                            scale=small[:, 28 + hh:29 + hh])
                    op.then_inc(done, 1)
                    copy_out("gdn", "vn1", g, vn[:, :])
                    root(s["stats"], GROUPS + g + 1, 226, small[:, 218:226], 8, 1.0 / P, 1)

            def square_sums(src, n):
                for t in range(TT):
                    op = act.activation(big[:, 4096:6144], src[:, t * D:(t + 1) * D], ACT.Square,
                                        accum_out=small[:, 150 + t:151 + t])
                    op.then_inc(s["squares_summed"], 1)
                    act.wait_ge(s["squares_summed"], 2 * n + t + 1)
                act.activation(small[:, 152:154], small[:, 150:152], ACT.Sqrt, scale=1.0 / D, bias=eps_sb[:, 1:2]).then_inc(s["rms_root"], 1)

            def broadcast(dst, row):
                act.dma_start(dst, row.partition_broadcast(P)).then_inc(s["rows_spread"], 16)

            act.dma_start(cst[:, :], consts[:, 0:C_MAIN]).then_inc(s["consts_loaded"], 16)
            mem_load(0, 0)
            mem_load(0, 1)
            at = 0
            for src in (ret_g[0], gdn_g[0], pool_b[0].rearrange("w c -> (w c)"), pool_scale[0],
                        lb_logits.rearrange("l c -> (l c)"), hgrn_w[0], mix_pre[0], mlp_pre[0]):
                rows = src.rearrange("(r p) -> r p", p=P)
                act.dma_start(zs[at:at + rows.shape[0], 0:P], rows).then_inc(s["rows_loaded"], 16)
                at += rows.shape[0]
            for i in range(2):
                for j in range(2):
                    src = conv_w[0][2 * i + j].rearrange("(r p) -> r p", p=P)
                    act.dma_start(zs[48 * j:48 * j + 48, (i + 1) * P:(i + 2) * P], src).then_inc(s["rows_loaded"], 16)
            act.dma_start(pos_sb[:, :], pos_in[0].rearrange("(t p) -> p t", p=P), allow_slow_non_contiguous=True).then_inc(s["pos_loaded"], 16)
            act.dma_start(x_sb[:, :].rearrange("p (t c) -> p t c", t=TT), x_in[0].rearrange("(t p) c -> p t c", p=P)).then_inc(s["x_loaded"], 16)
            ahead(U_KV0)
            act.wait_ge(s["ones_made"], 3)
            act.wait_ge(s["cols_turned"], 1)
            for r, rows in enumerate((N_ROWS, 96, 96)):
                op = act.activation(cols[:, r * P:r * P + rows], acc[0][0][:, r * P:r * P + rows], ACT.Copy)
            op.then_inc(s["cols_ready"], 1)
            mem_parts("mem0", 0, 0)
            act.wait_ge(s["trig_arg"], 1)
            act.activation(gates[:, 0:4 * 64], gates[:, 0:4 * 64], ACT.Sin).then_inc(s["trig_ready"], 1)
            act.wait_ge(s["lb_arg"], 1)
            act.activation(lb[:, 0:8], lb[:, 0:8], ACT.Sigmoid).then_inc(s["lb_ready"], 1)
            last_v = kv_slots("kv0", U_KV0)
            ahead(U_RET)
            last_v(0)
            a_parts("x0", U_KV0 + 4)
            layer(U_RET, W_RET, 0, ret_steps, "ret", "att0", ret_scale, None)

            def layer_norm(i):
                act.wait_ge(s["ln_stats"], i + 1)
                act.activation(small[:, 160:162], small[:, 156:160].rearrange("p (n two) -> p n two", two=2)[:, :, 1],
                               ACT.Sqrt, bias=eps_sb[:, 0:1]).then_inc(s["ln_root"], 1)

            def ln_rows(i):
                broadcast(lnw[:, 0:D], ln_g[i])
                broadcast(lnw[:, D:2 * D], ln_b[i])

            act.wait_ge(s["branch_ready"], B_L1)
            ln_rows(0)
            mem_load(1, 0)
            mem_load(1, 1)
            ahead(U_KV1)
            mem_parts("mem1", 1, U_ATT0 + 5)
            last_v = kv_slots("kv1", U_KV1, lambda: layer_norm(0))
            n48 = 2 * NVH
            act.dma_start(n0[:, 0:16 * n48].rearrange("p (k c) -> p k c", k=16),
                          w_gdn[0][:, CONV + MEMW + MIX:].rearrange("(k p) c -> p k c", p=P)).then_inc(s["ab_loaded"], 16)
            act.dma_start(n1[:, 0:NVH], dt_bias[0].partition_broadcast(P)).then_inc(s["ab_loaded"], 16)
            act.dma_start(n1[:, NVH:n48], a_log[0].partition_broadcast(P)).then_inc(s["ab_loaded"], 16)
            ahead(U_GDN)
            last_v(0)
            act.wait_ge(s["ab_loaded"], 48)
            act.activation(b_hi[:, 0:16 * n48], n0[:, 0:16 * n48], ACT.Copy).then_inc(s["ab_hi"], 1)
            a_parts("x1", U_KV1 + 4)
            b, _ = full("gates", "ab")
            ab = b[:, 0:2 * n48].rearrange("p (t c) -> p t c", t=TT)
            act.activation(gate(2), ab[:, :, NVH:], ACT.Sigmoid).then_inc(s["gate_step"], 1)
            act.wait_ge(s["gate_dve"], 1)
            act.activation(n1[:, 160:208], n1[:, 112:160], ACT.Exp, scale=-1.0).then_inc(s["gate_step"], 1)
            act.wait_ge(s["gate_step"], 2)
            act.activation(n1[:, 208:256], n1[:, 160:208], ACT.Ln, bias=1.0).then_inc(s["gate_step"], 1)
            act.activation(n1[:, 256:256 + NVH], n1[:, NVH:n48], ACT.Exp).then_inc(s["gate_step"], 1)
            b, done = full("gates", "cum")
            act.activation(gates[:, n48:2 * n48], b[:, 0:n48], ACT.Copy)
            act.activation(gates[:, 3 * n48:4 * n48], b[:, 0:n48], ACT.Exp).then_inc(done, 1)
            act.wait_ge(s["gate_dve"], 2)
            act.activation(gates[:, 4 * n48:5 * n48], n1[:, 288:336], ACT.Exp).then_inc(s["gate_step"], 1)
            layer(U_GDN, W_GDN, B_L1, gdn_steps, "gdn", "att1", lambda g: (lambda k: cols[:, C_GG:C_GG + 1]), None)
            act.wait_ge(s["branch_ready"], 2 * BR)
            ln_rows(1)
            ahead(U_HG)
            layer_norm(1)
            act.wait_ge(s["x_final"], 2)
            square_sums(x_sb, 0)
            a_parts("h2", U_ATT1 + 5, C_MP)

            def hgrn_in(g):
                for n, step in enumerate(("qa", "qb")):
                    copy_out("hgrn", step, g, cv[:, n * COL:(n + 1) * COL])
                if g:
                    act.wait_ge(s["branch_ready"], B_HG + g)
                for n, step in enumerate(("fa", "fb")):
                    copy_out("hgrn", step, g, sq[:, n * COL:(n + 1) * COL], func=ACT.Sigmoid)
                act.wait_ge(s["ksc_ready"], g + 1)
                act.activation(dn[:, :], dn[:, :], ACT.Ln).then_inc(s["logf_ready"], 1)

            def hgrn_exp(g, n):
                act.wait_ge(s["lev_arg"], 8 * g + n + 1)
                buf = (sq, br)[n % 2]
                act.activation(buf[:, :], buf[:, :], ACT.Exp).then_inc(s["lev_exp"], 1)

            def hgrn_unit(g, n, extra=lambda j: None):
                def between(j):
                    if j == 0 and n == 1:
                        wide_out(U_HG + 4 * g, 0, ACT.Copy, tiles(n0))
                    if j == 0 and n == 2:
                        wide_out(U_HG + 4 * g + 1, 1, ACT.Copy, tiles(n1))
                    if j == 3 * g and n == 3:
                        if g:
                            b, c = fill("hgrn", "o1", g - 1)
                            act.wait_ge(filled[b], c)
                        wide_out(U_HG + 4 * g + 2, 0, ACT.Copy, lambda t: (vn, st)[t][:, :])
                    extra(j)
                return between

            def gate_out(g):
                if g:
                    b, c = fill("hgrn", "o1", g - 1)
                    act.wait_ge(emptied[b], c)
                wide_out(U_HG + 4 * g + 3, 1, ACT.Sigmoid, tiles(zs))

            def h0_first(j):
                if j == 0:
                    gate_out(0)
                    hgrn_in(0)
                if j == 2:
                    hgrn_exp(0, 0)
                    hgrn_exp(0, 1)

            unit(U_HG, None, 2)
            unit(U_HG + 1, hgrn_unit(0, 1))
            unit(U_HG + 2, hgrn_unit(0, 2))
            unit(U_HG + 3, hgrn_unit(0, 3))
            unit(U_HG + 4, h0_first)
            unit(U_HG + 5, hgrn_unit(1, 1, lambda j: [hgrn_exp(0, n) for n in {0: (2, 3), 2: (4, 5)}.get(j, ())]))
            unit(U_HG + 6, hgrn_unit(1, 2, lambda j: [hgrn_exp(0, n) for n in {0: (6, 7)}.get(j, ())]))
            unit(U_HG + 7, hgrn_unit(1, 3, lambda j: None))
            hi(U_P0, 0)
            hi(U_P0, 1)
            root(s["stats"], 2 * GROUPS + 1, 226, small[:, 218:226], 8, 1.0 / P, 1)
            gate_out(1)
            hi(U_P0, 2)
            hi(U_P0, 3)
            b_parts("hgrn", 0, U_ATT1 + 7, lambda k: cols[:, C_HW + k:C_HW + k + 1])
            hi(U_P0 + 1, 0)
            hgrn_in(1)
            wide_out(U_P0, 0, ACT.Copy, tiles(n0))
            hi(U_P0 + 1, 1)
            hi(U_P0 + 1, 2)
            hgrn_exp(1, 0)
            hgrn_exp(1, 1)
            hi(U_P0 + 1, 3)
            hgrn_exp(1, 2)
            hgrn_exp(1, 3)
            hi(U_P0 + 2, 0)
            hgrn_exp(1, 4)
            hgrn_exp(1, 5)
            hi(U_P0 + 2, 1)
            hgrn_exp(1, 6)
            hgrn_exp(1, 7)
            hi(U_P0 + 2, 2)
            hi(U_P0 + 2, 3)
            hi(U_P0 + 3, 0)
            wide_out(U_P0 + 2, 1, ACT.Copy, tiles(n1))
            hi(U_P0 + 3, 1)
            root(s["stats"], 2 * GROUPS + 2, 226, small[:, 218:226], 8, 1.0 / P, 1)
            act.wait_ge(s["branch_ready"], B_HG + 2)
            act.dma_start(big[:, 2048:2048 + 4 * 384], consts[:, C_POOL:C_POOL + 4 * 384]).then_inc(s["pool_loaded"], 16)
            act.dma_start(big[:, 4096:6144].rearrange("p (k c) -> p k c", k=8),
                          pool_w[0].rearrange("w (k p) c -> p (w k) c", p=P)).then_inc(s["pool_loaded"], 16)
            broadcast(big[:, 0:D], mix_post[0])
            b_parts("hgrn", 1, U_P0 + 2, lambda k: cols[:, C_HW + 4 + k:C_HW + 5 + k])

            def pool_parts(g):
                act.wait_ge(s["pool_mapped"], g + 1)
                act.wait_ge(sub_used, 4 * (U_P0 + 4 + g))
                act.activation(b_hi[:, :], sq[:, :], ACT.Copy).then_inc(s["pool_hi"], 1)

            for n, step in enumerate(("da", "db")):
                copy_out("pool", step, 0, cv[:, n * COL:(n + 1) * COL])
            unit(U_P0 + 3, None, 2)
            ahead(U_P0 + 4)
            pool_parts(0)
            for n, step in enumerate(("da", "db")):
                copy_out("pool", step, 1, cv[:, n * COL:(n + 1) * COL])
            unit(U_P0 + 4, None, 2)
            ahead(U_P0 + 5)
            pool_parts(1)
            unit(U_P0 + 5, None, 2)
            ahead(U_MLP)
            act.wait_ge(s["y_ready"], 1)
            square_sums(y_sb, 1)
            act.wait_ge(s["x_final"], 3)
            broadcast(big[:, 2048:2048 + D], mlp_post[0])
            square_sums(x_sb, 2)
            a_parts("h3", U_P0 + 3, C_LP)

            def relu_out(g, pair):
                act.wait_ge(s["branch_ready"], g + (B_MLP - 2))
                wide_out(2 * g + (U_MLP - 1) if not isinstance(g, int) or g else U_MLP, pair, ACT.Relu, tiles(n0))

            def mlp(g, pair):
                def in_wide(j):
                    if j == 2:
                        b_parts("mlp", g - 1, 2 * g + (U_MLP - 1))
                unit(2 * g + (U_MLP - 1), in_wide)
                unit(2 * g + U_MLP, lambda j: relu_out(g, pair) if j == 0 else None)
            unit(U_MLP, None, 2)
            hi(U_MLP + 1, 0)
            relu_out(0, 0)
            for j in range(1, 4):
                hi(U_MLP + 1, j)
                if j == 2:
                    b_parts("mlp", 0, None)
            unit(U_MLP + 2, lambda j: relu_out(1, 1) if j == 0 else None)
            mlp(2, 0)
            with act.Fori(1, (FFG - 2) // 2) as r:
                mlp(2 * r + 1, 1)
                mlp(2 * r + 2, 0)
            mlp(FFG - 1, 1)
            ahead(UNITS - 1)
            b_parts("mlp", FFG - 1, UNITS - 1)
            unit(UNITS - 1, None, 2)
            act.wait_ge(s["y_ready"], 2)
            square_sums(y_sb, 3)

        @block.vector
        def _(dve):
            tt, ts, stt = dve.tensor_tensor, dve.tensor_scalar, dve.scalar_tensor_tensor
            MUL, ADD, SUB, MAX, MIN = ALU.mult, ALU.add, ALU.subtract, ALU.max, ALU.min

            one_row = ones[:, 0:1].to_broadcast([P, SEQ])

            def full(phase, step, g=0):
                b, n = fill(phase, step, g)
                dve.wait_ge(filled[b], n)
                return bank[b], emptied[b]

            def turned(phase, step, g):
                b, n = fill(phase, step, g)
                dve.wait_ge(filled[b], n)

            def copied(phase, step, g=0):
                b, n = fill(phase, step, g)
                dve.wait_ge(emptied[b], n)

            def a_parts(phase, count, scale=None):
                for f in range(8):
                    b, done = full(phase, f"f{f}")
                    dve.wait_ge(a_hi_in, 8 * count + f + 1)
                    hi = a_hi[:, f * COL:(f + 1) * COL].bitcast(f32)
                    lo = a_lo[:, f * COL:(f + 1) * COL]
                    if scale is None:
                        op = tt(lo, b[:, :], hi, SUB)
                    else:
                        for k in range(2):
                            c = slice(k * SEQ, (k + 1) * SEQ)
                            op = stt(out=lo[:, c], in0=b[:, c], scalar=cols[:, scale + 2 * f + k:scale + 2 * f + k + 1],
                                     in1=hi[:, c], op0=MUL, op1=SUB)
                    op.then_inc(done, 1)

            def b_parts(phase, g, i, scale=None):
                for n, step in enumerate(("ba", "bb")):
                    b, done = full(phase, step, g)
                    dve.wait_ge(b_hi_in, 2 * i + n + 1)
                    hi = b_hi[:, n * COL:(n + 1) * COL].bitcast(f32)
                    lo = b_lo[:, n * COL:(n + 1) * COL]
                    if scale is None:
                        op = tt(lo, b[:, :], hi, SUB)
                    else:
                        for k in range(2):
                            c = slice(k * SEQ, (k + 1) * SEQ)
                            op = stt(out=lo[:, c], in0=b[:, c], scalar=scale(2 * n + k), in1=hi[:, c], op0=MUL, op1=SUB)
                    op.then_inc(done, 1)

            def add(m, j, pair, dst):
                dve.wait_ge(sub_used, 4 * m + j + 1)
                for t in range(TT):
                    to = dst[:, t * D + j * COL:t * D + (j + 1) * COL]
                    tt(to, acc[(pair + j) % 2][t][:, :], to, ADD).then_inc(out_added, 1)

            def by(buf, n):
                return buf.rearrange("p (n c) -> p n c", n=n)

            def spread(ap, n):
                return ap.unsqueeze(1).to_broadcast([P, n, ap.shape[1]])

            def gated(i, phase, g, w, src):
                dve.wait_ge(wide_taken, 2 * (w + 1))
                tt(br[:, :], src, zs[:, :], MUL).then_inc(s["branch_ready"], 1)

            def ret_rotate(g, first):
                dve.wait_ge(wide_taken, 2 * (W_RET + 3 * g + 1))
                if not first:
                    turned("ret", "k", g - 1)
                for t in range(TT):
                    c = slice(t * COL, (t + 1) * COL)
                    cos, sin = gates[:, t * 64:(t + 1) * 64], gates[:, P + t * 64:P + (t + 1) * 64]
                    src = n0[:, c].rearrange("p (h two c) -> p h two c", two=2, c=64)
                    cross = dn[:, c].rearrange("p (h two c) -> p h two c", two=2, c=64)
                    tt(by(sq[:, c], 8), by(n0[:, c], 8), spread(cos, 8), MUL)
                    for half in range(2):
                        tt(cross[:, :, half, :], src[:, :, 1 - half, :], spread(sin, 4), MUL)
                dve.drain()
                for half, op in enumerate((SUB, ADD)):
                    a, b, to = (x[:, :].rearrange("p (h two c) -> p h two c", two=2, c=64)[:, :, half, :] for x in (sq, dn, cv))
                    last = tt(to, a, b, op)
                last.then_inc(s["rot_ready"], 1)

            def ret_decay(g, first):
                dve.wait_ge(s["decay_loaded"], 16 * g + 16)
                for h in range(2):
                    if not first:
                        turned("ret", f"o{h}", g - 1)
                    b, done = full("ret", f"s{h}", g)
                    dec, to = dt_[:, h * SEQ:(h + 1) * SEQ], h * 384
                    tt(pi[:, to:to + SEQ], b[:, 0:SEQ], dec, MUL)
                    tt(pi[:, to + SEQ:to + 384], b[:, SEQ:384], dec[:, 0:P], MUL).then_inc(done, 1)

            def ret_norm(g):
                for h in range(2):
                    b, _ = full("ret", f"o{h}", g)
                    for t in range(TT):
                        dve.bn_stats(small[:, 6 * (2 * h + t):6 * (2 * h + t + 1)], b[:, t * SEQ:(t + 1) * SEQ])
                dve.drain()
                for n in range(4):
                    last = dve.bn_aggr(small[:, 24 + 2 * n:26 + 2 * n], small[:, 6 * n:6 * n + 6])
                last.then_inc(s["stats"], 1)
                dve.wait_ge(s["root_ready"], g + 1)
                dve.wait_ge(s["stats"], g + 1)
                dve.reciprocal(small[:, 40:44], small[:, 36:40])
                dve.drain()
                for h in range(2):
                    b, done = full("ret", f"o{h}", g)
                    for t in range(TT):
                        n = 2 * h + t
                        last = ts(ui[:, t * COL + h * SEQ:t * COL + (h + 1) * SEQ], b[:, t * SEQ:(t + 1) * SEQ],
                                  small[:, 24 + 2 * n:25 + 2 * n], small[:, 40 + n:41 + n], SUB, MUL)
                    last.then_inc(done, 1)
                dve.drain()

            def ret_mid(g, first, adds):
                ret_rotate(g, first)
                ret_decay(g, first)
                adds(0)
                adds(1)
                ret_norm(g)
                adds(2)
                adds(3)

            def ret_gate(g, i):
                gated(i, "ret", g, W_RET + 3 * g + 2, ui[:, :])

            def ret_scale(k):
                return small[:, 104 + k:105 + k]

            def per(t, buf, hh):
                return buf[:, t * COL + hh * P:t * COL + (hh + 1) * P]

            def conv(dst, first_tile):
                src = by(cb[:, :], 4)
                for tap in range(4):
                    for c in range(4):
                        at = 64 + 8 * tap + first_tile + c
                        w, x, y = small[:, at:at + 1], src[:, c, tap:tap + SEQ], dst[:, c * SEQ:(c + 1) * SEQ]
                        if tap == 0:
                            last = ts(y, x, w, None, MUL)
                        else:
                            last = stt(out=y, in0=x, scalar=w, in1=y, op0=MUL, op1=ADD)
                    if tap < 3:
                        dve.drain()
                last.then_inc(s["conv_done"], 1)

            def gdn_group(g):
                dve.tensor_copy(by(small[:, 0:48], 12), by(gates[:, :], 12)[:, :, ds(4 * g, 4)]).then_inc(s["gs_ready"], 1)
                for half in range(2):
                    taps = by(small[:, 64 + 16 * half:80 + 16 * half], 2)
                    src = by(cols[:, P * (1 + half):P * (1 + half) + 96], 2)
                    dve.tensor_copy(taps[:, :, 0:2], src[:, :, ds(2 * g, 2)])
                    dve.tensor_copy(taps[:, :, 2:4], src[:, :, ds(2 * g + 12, 2)])
                    dve.tensor_copy(taps[:, :, 4:8], src[:, :, ds(4 * g + 24, 4)])
                dve.drain()

            def gdn_mid(g, first, adds):
                gdn_group(g)
                copied("gdn", "q", g)
                copied("gdn", "k", g)
                conv(cv, 0)
                for step in ("sq", "sk"):
                    copied("gdn", step, g)
                dve.reciprocal(dn[:, :], dn[:, :])
                dve.drain()
                stt(out=cv[:, 0:COL], in0=cv[:, 0:COL], scalar=QSCALE, in1=dn[:, 0:COL], op0=MUL, op1=MUL)
                tt(cv[:, COL:], cv[:, COL:], dn[:, COL:], MUL).then_inc(s["unit_ready"], 1)
                rows = [full("gdn", f"row{t}", g) for t in range(TT)]
                dve.wait_ge(s["unit_ready"], g + 1)
                for n, (buf, op) in enumerate(((dn, MAX), (dt_, MIN))):
                    for t in range(TT):
                        for hh in range(4):
                            last = ts(per(t, buf, hh), rows[t][0][:, hh * P:(hh + 1) * P], small[:, 8 + 4 * t + hh:9 + 4 * t + hh],
                                      0.0, SUB, op)
                            if n == 1 and hh == 3:
                                last.then_inc(rows[t][1], 1)
                dve.drain()
                adds(0)
                adds(1)
                dve.wait_ge(s["decay_ready"], 2 * g + 1)
                tt(by(dn[:, :], 8), by(dn[:, :], 8), spread(low, 8), MUL)
                dve.wait_ge(s["decay_ready"], 2 * g + 2)
                tt(by(dt_[:, :], 8), by(dt_[:, :], 8), spread(tri, 8), MUL)
                dve.drain()
                kk, kk_done = full("gdn", "kk", g)
                for t in range(TT):
                    for hh in range(4):
                        at = (2 * t + hh // 2) * P
                        last = stt(out=per(t, lw, hh), in0=kk[:, at:at + P], scalar=small[:, 16 + 4 * t + hh:17 + 4 * t + hh],
                                   in1=per(t, dn, hh), op0=MUL, op1=MUL)
                last.then_inc(kk_done, 1)
                dve.drain()
                tt(by(xi[:, :], 8), by(lw[:, :], 8), spread(negm1, 8), MUL)
                dve.drain()
                for t in range(TT):
                    c = slice(t * COL, (t + 1) * COL)
                    tt(by(xi[:, c], 4), by(xi[:, c], 4), spread(ident, 4), ADD).then_inc(s["lower_ready"], 1)
                qk, qk_done = full("gdn", "qk", g)
                for t in range(TT):
                    for v in range(2):
                        to = by(dt_[:, t * COL:(t + 1) * COL], 4).rearrange("p (h v) c -> p h v c", v=2)[:, :, v, :]
                        last = tt(to, to, by(qk[:, 2 * t * P:2 * (t + 1) * P], 2), MUL)
                last.then_inc(qk_done, 1)
                for n in range(1, 7):
                    gdn_level(g, n)
                    if n == 3:
                        adds(2)
                    if n == 5:
                        adds(3)
                copied("gdn", "va", g)
                copied("gdn", "vb", g)
                conv(sq, 4)
                copied("gdn", "kn", g)
                for hh in range(4):
                    last = ts(per(0, xi, hh), kn[:, (hh // 2) * P:(hh // 2 + 1) * P], small[:, 32 + hh:33 + hh], None, MUL)
                last.then_inc(s["kn_ready"], 1)
                b, done = full("gdn", "o0", g)
                dve.tensor_copy(dn[:, 0:COL], b[:, :]).then_inc(done, 1)
                b, done = full("gdn", "ks", g)
                for hh in range(4):
                    last = stt(out=per(1, xi, hh), in0=b[:, hh * P:(hh + 1) * P], scalar=small[:, 44 + hh:45 + hh],
                               in1=per(1, n1, hh), op0=MUL, op1=ADD)
                last.then_inc(done, 1)
                copied("gdn", "qs", g)
                b, done = full("gdn", "o1", g)
                tt(dn[:, COL:], b[:, :], kn[:, :], ADD).then_inc(done, 1)
                head_norm(dn, pi, GROUPS + g)

            def head_norm(src, tmp, n):
                dve.drain()
                tt(tmp[:, :], src[:, 0:1024], src[:, 0:1024], MUL)
                dve.drain()
                dve.tensor_reduce(small[:, 218:226], by(tmp[:, :], 8), AX.X, ADD).then_inc(s["stats"], 1)
                dve.wait_ge(s["root_ready"], n + 1)
                dve.reciprocal(small[:, 234:242], small[:, 226:234])
                dve.drain()
                tt(by(tmp[:, :], 8), by(src[:, 0:1024], 8), small[:, 234:242].unsqueeze(2).to_broadcast([P, 8, P]), MUL)
                dve.drain()

            def gdn_level(g, n):
                size, last_level = LEVELS[n], n == len(LEVELS) - 1
                for t in range(TT):
                    b, done = full("gdn", f"p{size}_{t}", g)
                    tt(by(pi[:, t * COL:(t + 1) * COL], 4), by(b[:, :], 4), spread(level_mask(n), 4), MUL).then_inc(done, 1)
                if n == 1:
                    for t in range(TT):
                        copied("gdn", f"u{t}", g)
                for t in range(TT):
                    b, done = full("gdn", f"n{size}_{t}", g)

                    def halves(buf, side):
                        return buf[:, t * COL:(t + 1) * COL].rearrange("p (n two s) -> p n two s", two=2, s=size)[:, :, side, :]

                    def res(at):
                        return b[:, at:at + 256].rearrange("p (n s) -> p n s", s=size)
                    last = tt(halves(ui, 1), halves(ui, 1), res(0), SUB)
                    if not last_level:
                        last = tt(halves(xi, 0), halves(xi, 0), res(256), SUB)
                    last.then_inc(done, 1)

            def gdn_gate(g, i):
                gated(i, "gdn", g, W_GDN + 3 * g + 2, pi[:, :])

            def att_mid(att, n, g, w, i, adds):
                for t in range(TT):
                    b, _ = full(att, f"s{t}", g)
                    dve.tensor_reduce(small[:, 114 + 2 * t:116 + 2 * t], by(b[:, :], 2), AX.X, MAX)
                dve.drain()
                for t in range(TT):
                    ts(small[:, 110 + 2 * t:112 + 2 * t], small[:, 114 + 2 * t:116 + 2 * t], -MSCALE, None, MUL).then_inc(s["mneg"], 1)
                adds(0)
                adds(1)
                copied(att, "s0", g)
                copied(att, "s1", g)
                dve.reciprocal(small[:, 124:128], small[:, 120:124])
                dve.drain()
                adds(2)
                for t in range(TT):
                    b, done = full(att, f"o{t}", g)
                    for h in range(2):
                        c = 2 * t + h
                        last = ts(pi[:, c * SEQ:(c + 1) * SEQ], b[:, h * SEQ:(h + 1) * SEQ], small[:, 124 + c:125 + c], None, MUL)
                    last.then_inc(done, 1)
                dve.drain()
                gated(i, att, g, w + 2 * g + 1, pi[:, :])
                adds(3)

            def layer(m, w, b0, mid, gate, scale, phase, att, n_att):
                def body(g, first=False):
                    at = m if first else 4 * g + (m - 1)
                    if not first:
                        gate(g - 1, b0 + g - 1)
                        b_parts(phase, g - 1, b0 + g - 1, scale)
                    mid(g, first, (lambda j: None) if first else (lambda j: add(at + 2, j, 0, x_sb)))
                body(0, True)
                with dve.Fori(1, GROUPS) as g:
                    body(g)
                m += 3 + 4 * (GROUPS - 1)
                w += 3 * GROUPS
                for g in range(MGROUPS):
                    i = b0 + GROUPS + g
                    if g == 0:
                        gate(GROUPS - 1, i - 1)
                        b_parts(phase, GROUPS - 1, i - 1, scale)
                    else:
                        b_parts(att, g - 1, i - 1)
                    att_mid(att, n_att + g, g, w, i, lambda j: add(m + 2, j, 0, x_sb))
                    m += 3
                b_parts(att, MGROUPS - 1, b0 + BR - 1)
                for j in range(4):
                    add(m, j, 0, x_sb)
                dve.drain()

            def layer_norm(i):
                for t in range(TT):
                    for c in range(4):
                        dve.bn_stats(small[:, 170 + 6 * (4 * t + c):176 + 6 * (4 * t + c)], x_sb[:, t * D + c * COL:t * D + (c + 1) * COL])
                dve.drain()
                for t in range(TT):
                    last = dve.bn_aggr(small[:, 156 + 2 * t:158 + 2 * t], small[:, 170 + 24 * t:194 + 24 * t])
                last.then_inc(s["ln_stats"], 1)
                dve.wait_ge(s["ln_root"], i + 1)
                dve.wait_ge(s["ln_stats"], i + 1)
                dve.reciprocal(small[:, 162:164], small[:, 160:162])
                dve.drain()
                rows = [x_sb[:, t * D:(t + 1) * D] for t in range(TT)]
                for t in range(TT):
                    ts(rows[t], rows[t], small[:, 156 + 2 * t:157 + 2 * t], small[:, 162 + t:163 + t], SUB, MUL)
                dve.drain()
                dve.wait_ge(s["rows_spread"], 32 * (i + 1))
                for t in range(TT):
                    tt(rows[t], rows[t], lnw[:, 0:D], MUL)
                dve.drain()
                for t in range(TT):
                    last = tt(rows[t], rows[t], lnw[:, D:2 * D], ADD)
                last.then_inc(s["x_final"], 1)

            def scale_x():
                return ts(x_sb[:, :], x_sb[:, :], ALPHA, None, MUL)

            dve.wait_ge(s["pos_loaded"], 16)
            dve.wait_ge(s["consts_loaded"], 16)
            dve.tensor_copy(small[:, 0:TT], pos_sb[:, :])
            dve.drain()
            for t in range(TT):
                ts(gates[:, P + t * 64:P + (t + 1) * 64], cst[:, C_FREQ:C_FREQ + 64], small[:, t:t + 1], None, MUL)
            dve.drain()
            turns, whole = dn[:, 0:2 * P], dn[:, 2 * P:4 * P]
            for k, shift in enumerate((0.25, 0.0)):
                ts(turns[:, k * P:(k + 1) * P], gates[:, P:2 * P], 1 / TWO_PI, shift, MUL, ADD)
            dve.drain()
            ts(whole, turns, ROUND, None, ADD)
            dve.drain()
            ts(turns, whole, ROUND, None, SUB)
            dve.drain()
            for n, part in enumerate(TURN_PARTS):
                for k in (0, 1):
                    to = gates[:, k * P:(k + 1) * P]
                    stt(out=to, in0=turns[:, k * P:(k + 1) * P], scalar=-part, in1=gates[:, P:2 * P] if n == 0 else to, op0=MUL, op1=ADD)
                    if n == 0 and k == 0:
                        dve.drain()
                dve.drain()
            ts(gates[:, 0:P], gates[:, 0:P], math.pi / 2, None, ADD)
            dve.drain()
            ts(gates[:, 0:2 * P], gates[:, 0:2 * P], PI_BELOW, -PI_BELOW, MIN, MAX).then_inc(s["trig_arg"], 1)
            dve.wait_ge(s["cols_ready"], 1)
            tt(lb[:, 0:8], cols[:, C_LB:C_LB + 8], cols[:, C_LB + 8:C_LB + 16], SUB).then_inc(s["lb_arg"], 1)
            a_parts("mem0", 0)
            dve.wait_ge(s["lb_ready"], 1)
            ts(lb[:, 8:16], lb[:, 0:8], -1.0, 1.0, MUL, ADD)
            dve.wait_ge(s["trig_ready"], 1)
            a_parts("x0", 1)
            scale_x().then_inc(out_added, 1)
            dve.drain()
            layer(U_RET, W_RET, 0, ret_mid, ret_gate, ret_scale, "ret", "att0", 0)
            a_parts("mem1", 2)
            layer_norm(0)
            n48 = 2 * NVH
            dve.wait_ge(s["ab_hi"], 1)
            tt(b_lo[:, 0:16 * n48], n0[:, 0:16 * n48], b_hi[:, 0:16 * n48].bitcast(f32), SUB).then_inc(s["ab_lo"], 1)
            dve.memset(cb[:, :], 0.0)
            a_parts("x1", 3)
            scale_x()
            dve.drain()
            b, done = full("gates", "ab")
            xa, xs = n1[:, 64:112], n1[:, 112:160]
            dve.wait_ge(s["gate_step"], 1)
            tt(by(xa, TT), b[:, 0:2 * n48].rearrange("p (t c) -> p t c", t=TT)[:, :, 0:NVH], spread(n1[:, 0:NVH], TT), ADD)
            dve.drain()
            stt(out=xs, in0=xa, scalar=-1.0, in1=xa, op0=MUL, op1=MAX).then_inc(s["gate_dve"], 1)
            ts(xa, xa, 0.0, None, MAX)
            dve.drain()
            dve.wait_ge(s["gate_step"], 4)
            tt(xa, xa, n1[:, 208:256], ADD).then_inc(done, 1)
            dve.drain()
            stt(out=by(gates[:, 0:n48], TT), in0=by(xa, TT), scalar=-1.0, in1=spread(n1[:, 256:256 + NVH], TT), op0=MUL, op1=MUL)\
                .then_inc(s["g_ready"], 1)
            copied("gates", "cum")
            b, done = full("gates", "last")
            tt(n1[:, 288:336], b[:, 0:n48], gates[:, n48:2 * n48], SUB).then_inc(done, 1)
            stt(out=gates[:, 5 * n48:6 * n48], in0=gates[:, 2 * n48:3 * n48], scalar=-1.0, in1=gates[:, 3 * n48:4 * n48], op0=MUL, op1=MUL)\
                .then_inc(s["gate_dve"], 1)
            dve.wait_ge(s["gate_dve"], 2)
            dve.wait_ge(s["gate_step"], 5)
            layer(U_GDN, W_GDN, B_L1, gdn_mid, gdn_gate, lambda k: cols[:, C_GG:C_GG + 1], "gdn", "att1", 2)
            layer_norm(1)

            def normalised(n):
                dve.wait_ge(s["rms_root"], n + 1)
                dve.reciprocal(small[:, 154:156], small[:, 152:154])
                dve.drain()
                for t in range(TT):
                    last = ts(y_sb[:, t * D:(t + 1) * D], x_sb[:, t * D:(t + 1) * D], small[:, 154 + t:155 + t], None, MUL)
                last.then_inc(s["h_ready"], 1)

            def add_normalised(n, w, done, each=False):
                dve.wait_ge(s["rms_root"], n + 1)
                dve.reciprocal(small[:, 154:156], small[:, 152:154])
                dve.drain()
                rows = [(x_sb[:, t * D:(t + 1) * D], y_sb[:, t * D:(t + 1) * D]) for t in range(TT)]
                for t in range(TT):
                    stt(out=rows[t][1], in0=rows[t][1], scalar=small[:, 154 + t:155 + t], in1=w, op0=MUL, op1=MUL)
                dve.drain()
                for t in range(TT):
                    last = tt(rows[t][0], rows[t][0], rows[t][1], ADD)
                    if each or t == TT - 1:
                        last.then_inc(done, 1)

            normalised(0)
            a_parts("h2", 4, C_MP)
            dve.memset(y_sb, 0.0)
            dve.memset(xi[:, :], 0.0)
            dve.memset(ui[:, :], 0.0)
            dve.drain()

            def hgrn_gates(g):
                copied("hgrn", "fa", g)
                copied("hgrn", "fb", g)
                for hh in range(4):
                    c = slice(hh * SEQ, (hh + 1) * SEQ)
                    low_, rest = (lb[:, k + 4 * g + hh:k + 4 * g + hh + 1] for k in (0, 8))
                    ts(dn[:, c], sq[:, c], rest, low_, MUL, ADD)
                    ts(lw[:, c], sq[:, c], -1.0, 1.0, MUL, ADD)
                dve.drain()
                ts(dn[:, :], dn[:, :], TINY, None, MAX)
                for hh in range(4):
                    c = slice(hh * SEQ, (hh + 1) * SEQ)
                    ts(lw[:, c], lw[:, c], lb[:, 8 + 4 * g + hh:9 + 4 * g + hh], None, MUL)
                dve.drain()
                dve.tensor_copy(small[:, 0:1], lw[:, 0:1]).then_inc(s["ksc_ready"], 1)
                dve.wait_ge(s["logf_ready"], g + 1)
                for hh in range(4):
                    c = slice(hh * SEQ, (hh + 1) * SEQ)
                    dve.tensor_tensor_scan(pi[:, c], one_row, dn[:, c], 0.0, MUL, ADD)
                dve.drain()

            def sides(buf, size):
                v = buf[:, :].rearrange("p (n two s) -> p n two s", two=2, s=size)
                return v[:, :, 0, :], v[:, :, 1, :]

            def compact(buf, size):
                return buf.rearrange("p (n s) -> p n s", s=size)

            def hgrn_arg(g, n):
                size = 2 ** n
                left, right = sides(pi, size)
                mid = left[:, :, size - 1:size].to_broadcast([P, COL // size, size])
                buf = (sq, br)[n % 2]
                tt(compact(buf[:, 0:COL], size), right, mid, SUB)
                tt(compact(buf[:, COL:], size), mid, left, SUB).then_inc(s["lev_arg"], 1)

            def hgrn_scale(g, n):
                size = 2 ** n
                buf, ks, qs = (sq, br)[n % 2], (xi, ui)[n % 2], dn[:, (n % 2) * COL:(n % 2 + 1) * COL]
                dve.wait_ge(s["lev_exp"], 8 * g + n + 1)
                if n >= 2:
                    turned("hgrn", f"l{LEVELS[n - 2]}", g)
                elif g:
                    turned("hgrn", "x", g - 1)
                tt(compact(qs, size), sides(cv, size)[1], compact(buf[:, 0:COL], size), MUL)
                tt(sides(ks, size)[0], sides(lw, size)[0], compact(buf[:, COL:], size), MUL).then_inc(s["lev_ready"], 1)

            def hgrn_diagonal(g):
                for t in range(TT):
                    b, done = full("hgrn", f"d{t}", g)
                    to = dt_.rearrange("p (h t c) -> p h t c", t=TT, c=P)[:, :, t, :]
                    tt(to, by(b[:, :], 4), spread(ident, 4), MUL).then_inc(done, 1)
                dve.drain()

            def hgrn_place(g, n):
                if n == 7:
                    b, done = full("hgrn", "x", g)
                    dve.tensor_copy(kn[:, :], b[:, :]).then_inc(done, 1)
                    return
                size = LEVELS[n]
                b, done = full("hgrn", f"l{size}", g)
                for i in range(8):
                    at = i * P
                    to = dt_[:, at:at + P].rearrange("p (n two s) -> p n two s", two=2, s=size)[:, :, 1, :]
                    mask = level_mask(n).bitcast(u32).rearrange("p (n two s) -> p n two s", two=2, s=size)[:, :, 1, :]
                    last = dve.copy_predicated(to, mask, compact(b[:, i * 64:(i + 1) * 64], size))
                last.then_inc(done, 1)
                dve.drain()

            def hgrn_end(g):
                for t in range(TT):
                    b, done = full("hgrn", f"o{t}", g)
                    tt(cb[:, t * COL:(t + 1) * COL], b[:, :], zs[:, t * COL:(t + 1) * COL], MUL).then_inc(done, 1)
                head_norm(cb, sq, 2 * GROUPS + g)
                dve.tensor_copy(br[:, :], sq[:, :]).then_inc(s["branch_ready"], 1)

            def hgrn_levels(g, more=lambda n: None):
                hgrn_arg(g, 0)
                hgrn_arg(g, 1)
                hgrn_diagonal(g)
                for n in range(8):
                    hgrn_scale(g, n)
                    if n >= 1:
                        hgrn_place(g, n - 1)
                    if n + 2 < 8:
                        dve.drain()
                        hgrn_arg(g, n + 2)
                    more(n)
                hgrn_place(g, 7)

            hgrn_gates(0)
            hgrn_levels(0)
            dve.wait_ge(wide_taken, 2 * (W_HG + 4))
            hgrn_end(0)
            b_parts("hgrn", 0, B_HG, lambda k: cols[:, C_HW + k:C_HW + k + 1])
            hgrn_gates(1)
            hgrn_levels(1, lambda n: add(U_P0 + 1, n - n // 3, 1, y_sb) if n in (0, 1, 3, 4) else None)
            dve.wait_ge(wide_taken, 2 * (W_HG + 8))
            hgrn_end(1)
            b_parts("hgrn", 1, B_HG + 1, lambda k: cols[:, C_HW + 4 + k:C_HW + 5 + k])

            def pool_scaled(g):
                for n, step in enumerate(("ya", "yb")):
                    b, done = full("pool", step, g)
                    for c in range(2):
                        i = 4 * g + 2 * n + c
                        last = ts(sq[:, (2 * n + c) * SEQ:(2 * n + c + 1) * SEQ], b[:, c * SEQ:(c + 1) * SEQ],
                                  cols[:, C_PB + i:C_PB + i + 1], cols[:, C_PS + i:C_PS + i + 1], ADD, MUL)
                    last.then_inc(done, 1)
                dve.drain()
                dve.tensor_copy(small[:, 0:1], sq[:, 0:1]).then_inc(s["pool_mapped"], 1)

            def pool_parts(g):
                dve.wait_ge(s["pool_hi"], g + 1)
                tt(b_lo[:, :], sq[:, :], b_hi[:, :].bitcast(f32), SUB).then_inc(s["pool_in"], 1)

            add(U_P0 + 3, 0, 0, y_sb)
            add(U_P0 + 3, 1, 0, y_sb)
            pool_scaled(0)
            add(U_P0 + 3, 2, 0, y_sb)
            add(U_P0 + 3, 3, 0, y_sb)
            pool_parts(0)
            dve.drain()
            add(U_P0 + 4, 0, 0, y_sb)
            add(U_P0 + 4, 1, 0, y_sb)
            pool_scaled(1)
            add(U_P0 + 4, 2, 0, y_sb)
            add(U_P0 + 4, 3, 0, y_sb)
            pool_parts(1)
            dve.drain()
            for j in range(4):
                add(U_P0 + 5, j, 0, y_sb)
            dve.drain()
            dve.tensor_copy(small[:, 0:1], y_sb[:, 0:1]).then_inc(s["y_ready"], 1)
            dve.wait_ge(s["rows_spread"], 16 * 5)
            add_normalised(1, big[:, 0:D], s["x_final"])
            normalised(2)
            a_parts("h3", 5, C_LP)
            dve.memset(y_sb, 0.0)
            dve.drain()

            def mlp(g, pair):
                dve.wait_ge(wide_taken, 2 * g + 2 * W_MLP)
                tt(br[:, :], n0[:, :], n0[:, :], MUL).then_inc(s["branch_ready"], 1)
                b_parts("mlp", g - 1, g + (B_MLP - 3))
                for j in range(4):
                    add(2 * g + U_MLP, j, 1 - pair, y_sb)
            with dve.Fori(0, (FFG - 2) // 2) as r:
                mlp(2 * r + 1, 1)
                mlp(2 * r + 2, 0)
            mlp(FFG - 1, 1)
            dve.wait_ge(wide_taken, 2 * (W_MLP + FFG))
            tt(br[:, :], n0[:, :], n0[:, :], MUL).then_inc(s["branch_ready"], 1)
            b_parts("mlp", FFG - 1, FFG + B_MLP - 3)
            for j in range(4):
                add(UNITS - 1, j, 0, y_sb)
            dve.drain()
            dve.tensor_copy(small[:, 0:1], y_sb[:, 0:1]).then_inc(s["y_ready"], 1)
            dve.wait_ge(s["rows_spread"], 16 * 6)
            add_normalised(3, big[:, 2048:2048 + D], s["out_ready"], each=True)
    return nc


INPUTS = ["x", "mem", "positions", "w_in_ret", "ret_norm_g", "w_in_gdn", "conv_w", "a_log", "dt_bias", "gdn_norm_g",
          "w_mem_kv", "w_out", "ln_g", "ln_b", "w_in_2", "pool_w_2", "pool_b_2", "pool_scale_2", "lb_logits_2",
          "hgrn_norm_w_2", "w_out_2", "norm_mix_pre_2", "norm_mix_post_2", "norm_mlp_pre_2", "norm_mlp_post_2",
          "w_mlp_in_2", "w_mlp_out_2"]


def kernel(**inputs):
    import concourse.bacc as bacc
    from concourse.bass_utils import run_bass_kernel_spmd

    nc = bacc.Bacc("TRN2", target_bir_lowering=False, num_devices=1)
    arrays = {f"in_{n}": np.ascontiguousarray(inputs[n]) for n in INPUTS}
    arrays["shape_constants"] = shape_constants()
    args = [nc.dram_tensor(n, a.shape, mybir.dt.from_np(a.dtype), kind="ExternalInput").ap() for n, a in arrays.items()]
    out = nc.dram_tensor("out", (1, SEQ, D), mybir.dt.float32, kind="ExternalOutput").ap()
    build(nc, *args, out)
    r = run_bass_kernel_spmd(nc, [arrays], core_ids=[0])
    return r.results[0]["out"]
```

```python
import math
from contextlib import ExitStack

import numpy as np

import concourse.bass as bass
from concourse import mybir

P = 128
SEQ, D = 256, 2048
TT = SEQ // P
MIX = 2 * D
TOK = 3 * MIX // 4
MEMW = MIX - TOK
QKW = TOK // 2
CONV = 2 * QKW + TOK
NVH = TOK // P
COL = 512
KB = 4
HALF = KB * COL // 2
GROUPS = TOK // COL
MGROUPS = MEMW // COL
BR = GROUPS + MGROUPS
ALPHA = (2.0 * 2) ** 0.25
QSCALE = float(P) ** -0.5
MSCALE = 256.0 ** -0.5
LN_EPS, EPS = 1e-5, 1e-6
FF = 4 * D
FFG = FF // COL
LEVELS = [2 ** i for i in range(7)]
WINDOWS = (2, 4, 8, 16)
TWO_PI = 2 * math.pi
TURN_PARTS = (6.28125, 1.9350051879882812e-03, 3.0199159819567e-07)
ROUND = 1.5 * 2 ** 23
PI_BELOW = 3.1415925
TINY = 2.0 ** -64

C_ID, C_TRI, C_LOW, C_M1, C_LV = 0, P, 2 * P, 3 * P, 4 * P
C_FREQ = C_LV + 7 * P
C_MAIN = C_FREQ + 64
C_DEC = C_MAIN
C_POOL = C_DEC + 12 * 2 * P
C_ALL = C_POOL + 4 * 3 * P


def shape_constants():
    c = np.zeros((P, C_ALL), np.float64)
    i = np.arange(P)
    row, col = i[:, None], i[None, :]
    c[:, C_ID:C_ID + P] = np.eye(P)
    c[:, C_TRI:C_TRI + P] = row <= col
    c[:, C_LOW:C_LOW + P] = row > col
    c[:, C_M1:C_M1 + P] = -((row // 2 == col // 2) & (row > col)).astype(float)
    for n, s in enumerate(LEVELS):
        c[:, C_LV + n * P:C_LV + (n + 1) * P] = (row // (2 * s) == col // (2 * s)) & (row % (2 * s) < s) & (col % (2 * s) >= s)
    c[:, C_FREQ:C_FREQ + 64] = (10000.0 ** (-np.arange(64) / 64))[None, :]
    for h in range(12):
        lg = math.log1p(-2.0 ** (-5 - h))
        at = C_DEC + h * 2 * P
        rel = (col - row).astype(float)
        c[:, at:at + P] = np.where(rel >= 0, np.exp(lg * np.maximum(rel, 0)), 0) * QSCALE
        c[:, at + P:at + 2 * P] = np.exp(lg * (rel + P)) * QSCALE
    for n, w in enumerate(WINDOWS):
        at = C_POOL + n * 3 * P
        for blk, (s0, t0) in enumerate(((0, 0), (0, P), (P, P))):
            s, t = row + s0, col + t0
            c[:, at + blk * P:at + (blk + 1) * P] = ((s <= t) & (s > t - w)) / np.minimum(t + 1, w) - (s == t)
    return c.astype(np.float32)


def turned_fills():
    return [[f"f{b}", f"f{b + 4}"] for b in range(4)]


PHASES = [
    ("mem0", 1, turned_fills()),
    ("kv0", 1, [["k0a", "k1a"], ["k0b", "k1b"], [], []]),
    ("x0", 1, turned_fills()),
    ("ret", GROUPS, [["q", "o0"], ["k", "o1"], ["s0", "ba"], ["s1", "bb"]]),
    ("att0", MGROUPS, [["qa", "pa", "ba"], ["qb", "pb", "bb"], ["s0", "o0"], ["s1", "o1"]]),
    ("mem1", 1, turned_fills()),
    ("kv1", 1, [["k0a", "k1a"], ["k0b", "k1b"], [], []]),
    ("x1", 1, turned_fills()),
    ("gates", 1, [["ab"], ["cum"], ["last"], []]),
    ("gdn", GROUPS, [
        ["q", "sq", "kn", "qk"] + [f"p{s}_0" for s in LEVELS[1:5]] + ["va2"] + [f"p{s}_0" for s in LEVELS[5:]] + ["vn0", "qs"],
        ["k", "sk", "row0", "va", "u0"] + [f"n{s}_0" for s in LEVELS[1:]] + ["o0", "vn1"],
        ["row1", "vb", "u1"] + [f"p{s}_1" for s in LEVELS[1:6]] + ["vb2"] + [f"p{s}_1" for s in LEVELS[6:]] + ["st", "o1", "ba"],
        ["kk"] + [f"n{s}_1" for s in LEVELS[1:]] + ["ks", "bb"],
    ]),
    ("att1", MGROUPS, [["qa", "pa", "ba"], ["qb", "pb", "bb"], ["s0", "o0"], ["s1", "o1"]]),
    ("h2", 1, turned_fills()),
    ("hgrn", 2, [
        ["qa", "fa", "d0"] + [f"l{s}" for s in LEVELS[0::2]] + ["o0"],
        ["qb", "fb", "d1"] + [f"l{s}" for s in LEVELS[1::2]] + ["o1"],
        ["x", "ba"], ["bb"]]),
    ("pool", 2, [["da"], ["db"], ["ya"], ["yb"]]),
    ("h3", 1, turned_fills()),
    ("mlp", FFG, [["ba"], ["bb"], [], []]),
]


def fill(phase, step, g=0):
    for bank in range(4):
        before = 0
        for name, rounds, steps in PHASES:
            if name == phase and step in steps[bank]:
                return bank, g * len(steps[bank]) + (before + steps[bank].index(step) + 1)
            before += rounds * len(steps[bank])
    raise KeyError((phase, step))


C_RG, C_GG, C_PB, C_PS, C_LB, C_HW, C_MP, C_LP, N_ROWS = 0, 24, 25, 33, 41, 57, 65, 81, 97
N_LOADS = 12

U_KV0 = 0
U_RET = 4
U_ATT0 = U_RET + 3 + 4 * (GROUPS - 1)
U_KV1 = U_ATT0 + 7
U_GDN = U_KV1 + 4
U_ATT1 = U_GDN + 3 + 4 * (GROUPS - 1)
U_HG = U_ATT1 + 7
U_P0 = U_HG + 8
U_MLP = U_P0 + 6
UNITS = U_MLP + 2 * FFG
W_RET = 4
W_ATT0 = W_RET + 3 * GROUPS
W_KV1 = W_ATT0 + 4
W_GDN = W_KV1 + 4
W_ATT1 = W_GDN + 3 * GROUPS
W_HG = W_ATT1 + 4
W_MLP = W_HG + 10
B_L1, B_HG, B_MLP = BR, 2 * BR, 2 * BR + 4


def build(nc, x_in, mem_in, pos_in, w_ret, ret_g, w_gdn, conv_w, a_log, dt_bias, gdn_g, w_kv, w_out,
          ln_g, ln_b, w_in2, pool_w, pool_b, pool_scale, lb_logits, hgrn_w, w_out2, mix_pre, mix_post,
          mlp_pre, mlp_post, w_mlp_in, w_mlp_out, consts, out):
    f32, f32r, i32, u32 = mybir.dt.float32, mybir.dt.float32r, mybir.dt.int32, mybir.dt.uint32
    ALU, ACT, AX = mybir.AluOpType, mybir.ActivationFunctionType, mybir.AxisListType
    ds = bass.ds

    with ExitStack() as ctx:
        def sb(name, cols, dt=f32):
            return ctx.enter_context(nc.sbuf_tensor(name, [P, cols], dt))

        def psum(name):
            return ctx.enter_context(nc.psum_tensor(name, [P, COL], f32))

        def sem(name):
            return ctx.enter_context(nc.semaphore(name))

        raw = [sb(f"raw{j}", KB * COL) for j in range(4)]
        whi = [sb(f"whi{j}", HALF, f32r) for j in range(4)]
        wlo = [sb(f"wlo{j}", HALF, f32r) for j in range(4)]
        a_hi, a_lo = sb("a_hi", 16 * SEQ, f32r), sb("a_lo", 16 * SEQ, f32r)
        b_hi, b_lo = sb("b_hi", KB * SEQ, f32r), sb("b_lo", KB * SEQ, f32r)
        x_sb = sb("x_sb", TT * D)
        kv = sb("kv", 2 * 8 * SEQ)
        mk, mv, y_sb = kv[:, 0:8 * SEQ], kv[:, 8 * SEQ:], kv[:, :]
        cst = sb("cst", C_MAIN)
        ones = sb("ones", P)
        cols = sb("cols", 3 * P)
        small = sb("small", 256)
        gates = sb("gates", 6 * TT * NVH)
        eps_sb, lb, pos_sb = sb("eps_sb", 2), sb("lb", 16), sb("pos_sb", TT, i32)
        n0, n1 = sb("n0", 1024), sb("n1", 1024)
        zs, br = sb("zs", 1024), sb("br", 1024)
        cb = sb("cb", 4 * (SEQ + 3))
        cv, sq = sb("cv", 1024), sb("sq", 1024)
        kn, vn, st = sb("kn", COL), sb("vn", COL), sb("st", COL)
        big = sb("big", 6 * 1024)
        lnw = big[:, 0:2 * D]
        dn, dt_, lw, xi, ui, pi = (big[:, k * 1024:(k + 1) * 1024] for k in range(6))
        ident, tri, low, negm1 = (cst[:, c:c + P] for c in (C_ID, C_TRI, C_LOW, C_M1))

        def inverse_rms(n):
            return small[:, 130 + 2 * n:132 + 2 * n]

        def level_mask(n):
            return cst[:, C_LV + n * P:C_LV + (n + 1) * P]

        acc = [[psum(f"acc{p}{t}") for t in range(TT)] for p in range(2)]
        bank = [psum(f"bank{b}") for b in range(4)]

        raw_loaded = [sem(f"raw_loaded{j}") for j in range(4)]
        hi_ready, lo_ready = sem("hi_ready"), sem("lo_ready")
        sub_used = sem("sub_used")
        wide_taken = sem("wide_taken")
        out_added = sem("out_added")
        filled = [sem(f"filled{b}") for b in range(4)]
        emptied = [sem(f"emptied{b}") for b in range(4)]
        a_hi_in, b_hi_in = sem("a_hi_in"), sem("b_hi_in")
        mem_loaded = [sem(f"mem_loaded{c}") for c in range(4)]
        signals = {
            "ab_hi": "high part of the gates' weights",
            "ab_lo": "low part of the gates' weights",
            "ab_loaded": "the gates' weights and parameters",
            "branch_ready": "a group's gated output, to be turned",
            "cols_ready": "parameters' columns are copied out",
            "cols_turned": "parameters' rows are turned",
            "consts_loaded": "masks and frequencies",
            "conv_done": "a convolution of q and k, or of v",
            "decay_loaded": "a group's retention decays",
            "decay_ready": "a group's decays of the delta rule",
            "g_ready": "log decays of all tokens and heads",
            "gate_dve": "VectorE's steps to the gates",
            "gate_step": "ScalarE's steps to the gates",
            "gs_ready": "a group's gates beside one another",
            "ident_loaded": "the identity",
            "inverse_rms": "the rows' scales",
            "kn_ready": "tile 0's keys with their decays",
            "ksc_ready": "forget gates and keys of HGRN",
            "lb_arg": "argument of the lower bound",
            "lb_ready": "the lower bound",
            "lev_arg": "log decays of a level",
            "lev_exp": "decays of a level",
            "lev_ready": "decayed q and k of a level",
            "ln_root": "standard deviations of the rows",
            "ln_stats": "variances of the rows",
            "logf_ready": "logs of the forget gates",
            "lower_ready": "a tile's lower triangles and 2 x 2 inverses",
            "mneg": "minus the largest scores",
            "ones_made": "ones and epsilons",
            "out_ready": "a finished piece of the output",
            "pool_hi": "high part of a pooled group",
            "pool_in": "a pooled group's operand",
            "pool_loaded": "pooling's bands and maps",
            "pool_mapped": "a pooled group",
            "pos_loaded": "positions",
            "rms_root": "root mean squares of the rows",
            "root_ready": "roots for the heads' norms",
            "rot_ready": "rotated q and k",
            "rows_loaded": "rows of parameters",
            "rows_spread": "a row of gains or offsets on all partitions",
            "scale_ready": "a group's gains",
            "silu_done": "silu of q and k, or of v",
            "squared": "squares of q and k",
            "stats": "variances or sums of squares of the heads",
            "stored": "output in DRAM",
            "trig_arg": "the rotation's angles",
            "trig_ready": "cosines and sines",
            "unit_ready": "q and k at unit length",
            "x_final": "a chunk of x after a norm or a block",
            "x_loaded": "x",
            "y_squared": "sums of squares of y's chunks",
            "y_summed": "and their sums",
        }
        s = {name: sem(name) for name in signals}
        block = ctx.enter_context(nc.Block())

        @block.sync
        def _(sp):
            def load(m, j, first, second):
                if not (isinstance(m, int) and m == 0):
                    sp.wait_ge(lo_ready, 8 * m + 2 * j - 6)
                view = raw[j][:, :].rearrange("p (k c) -> p k c", k=KB)
                for dst, src in ((first[0](view), first[1]), (second[0](view), second[1])):
                    sp.dma_start(dst, src.rearrange("(k p) c -> p k c", p=P)).then_inc(raw_loaded[j], 16)

            def wide(m, w, col):
                for j in range(4):
                    load(m, j,
                         (lambda v: v[:, 0:2, :], w[COL * j:COL * j + 256, ds(col, COL)]),
                         (lambda v: v[:, 2:4, :], w[COL * j + 256:COL * j + COL, ds(col, COL)]))

            def wide_qk(m, w, g):
                for j in range(4):
                    rows = slice(COL * j, COL * (j + 1))
                    load(m, j,
                         (lambda v: v[:, :, 0:256], w[rows, ds(256 * g, 256)]),
                         (lambda v: v[:, :, 256:512], w[rows, ds(QKW + 256 * g, 256)]))

            def tall(m, w, row):
                for j in range(4):
                    for_cols = slice(COL * j, COL * (j + 1))
                    load(m, j,
                         (lambda v: v[:, 0:2, :], w[ds(row, 256), for_cols]),
                         (lambda v: v[:, 2:4, :], w[ds(row + 256, 256), for_cols]))

            sp.wait_ge(mem_loaded[1], 16)

            def kv_units(m, layer):
                for c in range(4):
                    wide(m + c, w_kv[layer], COL * c)

            def layer(m, w, wo):
                wide_qk(m, w, 0)
                wide(m + 1, w, 2 * QKW)
                wide(m + 2, w, CONV + MEMW)
                with sp.Fori(1, GROUPS) as g:
                    at = 4 * g + (m - 1)
                    wide_qk(at, w, g)
                    wide(at + 1, w, 2 * QKW + COL * g)
                    wide(at + 2, w, CONV + MEMW + COL * g)
                    tall(at + 3, wo, COL * (g - 1))
                m += 3 + 4 * (GROUPS - 1)
                for g in range(MGROUPS):
                    wide(m, w, CONV + COL * g)
                    wide(m + 1, w, CONV + MEMW + TOK + COL * g)
                    tall(m + 2, wo, COL * (GROUPS + g - 1))
                    m += 3
                tall(m, wo, COL * (BR - 1))

            kv_units(U_KV0, 0)
            layer(U_RET, w_ret[0], w_out[0])
            kv_units(U_KV1, 1)
            layer(U_GDN, w_gdn[0], w_out[1])
            for g in range(2):
                for n in range(4):
                    wide(U_HG + 4 * g + n, w_in2[0], 1024 + 1024 * n + COL * g)
            wide(U_P0, w_in2[0], 0)
            tall(U_P0 + 1, w_out2[0], 1024)
            wide(U_P0 + 2, w_in2[0], COL)
            tall(U_P0 + 3, w_out2[0], 1024 + COL)
            tall(U_P0 + 4, w_out2[0], 0)
            tall(U_P0 + 5, w_out2[0], COL)
            wide(U_MLP, w_mlp_in[0], 0)
            with sp.Fori(1, FFG) as g:
                wide(2 * g + (U_MLP - 1), w_mlp_in[0], COL * g)
                tall(2 * g + U_MLP, w_mlp_out[0], COL * (g - 1))
            tall(UNITS - 1, w_mlp_out[0], COL * (FFG - 1))
            for c in range(4):
                for t in range(TT):
                    sp.wait_ge(s["out_ready"], 2 * c + t + 1)
                    at = t * D + c * COL
                    sp.dma_start(out[0, t * P:(t + 1) * P, c * COL:(c + 1) * COL], x_sb[:, at:at + COL]).then_inc(s["stored"], 16)
            sp.wait_ge(s["stored"], 16 * 8)

        @block.gpsimd
        def _(pool):
            pool.memset(ones[:, :], 1.0).then_inc(s["ones_made"], 1)
            for n, eps in enumerate((LN_EPS, EPS)):
                pool.memset(eps_sb[:, n:n + 1], eps).then_inc(s["ones_made"], 1)
            with pool.Fori(0, UNITS) as m:
                for q in range(8):
                    raw_half = raw[q // 2][:, (q % 2) * HALF:(q % 2 + 1) * HALF]
                    pool.wait_ge(hi_ready, 8 * m + q + 1)
                    pool.tensor_tensor(wlo[q % 4][:, :], raw_half, whi[q % 4][:, :].bitcast(f32),
                                       ALU.subtract).then_inc(lo_ready, 1)

        @block.tensor
        def _(pe):
            def loads(step):
                return lambda q: step(q // 2) if q % 2 else None

            def sub(m, j, hi_t, lo_t, block0, pair, start, stop, between):
                for q in (2 * j, 2 * j + 1):
                    pe.wait_ge(lo_ready, 8 * m + q + 1)
                    for t in range(TT):
                        dst = acc[pair][t][:, :]
                        for k in range(2):
                            block = (q % 2) * 2 + k
                            at = (block0 + block) * SEQ + t * P
                            h, l = hi_t[:, at:at + P], lo_t[:, at:at + P]
                            w_h, w_l = (w[q % 4][:, k * COL:(k + 1) * COL] for w in (whi, wlo))
                            pe.matmul(dst, l, w_h, start=start and block == 0, stop=False)
                            pe.matmul(dst, h, w_l, start=False, stop=False)
                            mm = pe.matmul(dst, h, w_h, start=False, stop=stop and block == KB - 1)
                    mm.then_inc(sub_used, 1)
                    if between:
                        between(q)

            def wide(m, pair, taken, added, between=None):
                if not (isinstance(taken, int) and taken == 0):
                    pe.wait_ge(wide_taken, 2 * taken)
                if not (isinstance(added, int) and added <= 0):
                    pe.wait_ge(out_added, 2 * added)
                for j in range(4):
                    sub(m, j, a_hi, a_lo, 4 * j, pair, j == 0, j == 3, between)

            def in_place(phase, step, g=0):
                b, n = fill(phase, step, g)
                pe.wait_ge(emptied[b], n)

            def tall(m, b, pair, taken, parts, between=None, added=None, after_tall=False):
                operand, first = (b_hi, b_lo), 0
                if parts[0] == "pool":
                    pe.wait_ge(s["pool_in"], parts[1] + 1)
                    operand, first = (a_hi, a_lo), KB * parts[1]
                else:
                    in_place(parts[0], "ba", parts[1])
                    in_place(parts[0], "bb", parts[1])
                pe.wait_ge(wide_taken, 2 * taken - 2)
                if added is not None:
                    pe.wait_ge(out_added, 2 * added)
                for j in range(4):
                    if j == 1:
                        pe.wait_ge(wide_taken, 2 * taken)
                    if after_tall or j >= 2:
                        pe.wait_ge(out_added, 2 * (4 * b + j - 1))
                    sub(m, j, *operand, first, (pair + j) % 2, True, True, between)

            def take(phase, step, g=0):
                b, n = fill(phase, step, g)
                if not (isinstance(n, int) and n == 1):
                    pe.wait_ge(emptied[b], n - 1)
                return bank[b], filled[b]

            def turn(phase, step, g, block):
                dst, done = take(phase, step, g)
                for k in range(2):
                    for t in range(TT):
                        at = k * SEQ + t * P
                        tr = pe.transpose(dst[:, at:at + P], block(k, t), ident)
                tr.then_inc(done, 1)

            def turn_natural(phase, steps, g, src):
                for n, step in enumerate(steps):
                    turn(phase, step, g, lambda k, t: src[:, t * COL + (2 * n + k) * P:t * COL + (2 * n + k + 1) * P])

            def turn_x(phase, src, norms):
                for f in range(8):
                    if norms:
                        pe.wait_ge(s["x_final"], 8 * norms - 6 + 2 * (f // 2))
                    turn(phase, f"f{f}", 0, lambda k, t: src[:, t * D + (2 * f + k) * P:t * D + (2 * f + k + 1) * P])

            def turn_mem(phase, layer):
                for c in range(4):
                    pe.wait_ge(mem_loaded[c], 16 * (layer + 1))
                    turn_natural(phase, (f"f{2 * c}", f"f{2 * c + 1}"), 0, (n1, n0, cv, sq)[c])

            def a_in_place(phase):
                for f in range(4, 8):
                    in_place(phase, f"f{f}")

            def branch(phase, g, b):
                pe.wait_ge(s["branch_ready"], b + 1)
                turn_natural(phase, ("ba", "bb"), g, br)

            def kv_units(phase, m, w, turned, added, first=None):
                a_in_place(turned)

                def keys(c):
                    def between(j):
                        if j == 1:
                            pe.wait_ge(wide_taken, 2 * (w + c + 1))
                            turn_natural(phase, (f"k{c}a", f"k{c}b"), 0, n0)
                    return loads(between)
                wide(m, 0, w, added, first)
                wide(m + 1, 1, w, added, keys(0))
                wide(m + 2, 0, w + 1, added, keys(1))
                wide(m + 3, 1, w + 2, added)

            def ret_qk(g):
                pe.wait_ge(s["rot_ready"], g + 1)
                turn_natural("ret", ("q", "k"), g, cv)

            def ret_scores(g):
                in_place("ret", "q", g)
                in_place("ret", "k", g)
                for h in range(2):
                    dst, done = take("ret", f"s{h}", g)
                    q, k = lw[:, h * SEQ:(h + 1) * SEQ], lw[:, COL + h * SEQ:COL + (h + 1) * SEQ]
                    pe.matmul(dst[:, 0:SEQ], k[:, 0:P], q, start=True, stop=True)
                    pe.matmul(dst[:, SEQ:SEQ + P], k[:, P:SEQ], q[:, P:SEQ], start=True, stop=True).then_inc(done, 1)

            def ret_out(g):
                pe.wait_ge(wide_taken, 2 * (W_RET + 3 * g + 2))
                for h in range(2):
                    in_place("ret", f"s{h}", g)
                    dst, done = take("ret", f"o{h}", g)
                    p = pi[:, h * 384:(h + 1) * 384]
                    v = [n1[:, t * COL + h * SEQ:t * COL + (h + 1) * SEQ] for t in range(TT)]
                    pe.matmul(dst[:, 0:SEQ], p[:, 0:P], v[0], start=True, stop=True)
                    pe.matmul(dst[:, SEQ:COL], p[:, P:2 * P], v[0], start=True, stop=False)
                    pe.matmul(dst[:, SEQ:COL], p[:, 2 * P:384], v[1], start=False, stop=True).then_inc(done, 1)

            def gdn_gates():
                pe.wait_ge(s["ab_lo"], 1)
                dst, done = take("gates", "ab")
                n = 2 * NVH
                for t in range(TT):
                    for k in range(16):
                        at = k * SEQ + t * P
                        h, l = a_hi[:, at:at + P], a_lo[:, at:at + P]
                        w_h, w_l = (w[:, k * n:(k + 1) * n] for w in (b_hi, b_lo))
                        pe.matmul(dst[:, t * n:(t + 1) * n], l, w_h, start=k == 0, stop=False)
                        pe.matmul(dst[:, t * n:(t + 1) * n], h, w_l, start=False, stop=False)
                        mm = pe.matmul(dst[:, t * n:(t + 1) * n], h, w_h, start=False, stop=k == 15)
                mm.then_inc(done, 1)

            def gdn_sums():
                n = 2 * NVH
                pe.wait_ge(s["g_ready"], 1)
                for step, lhs in (("cum", tri), ("last", ones[:, :])):
                    dst, done = take("gates", step)
                    pe.matmul(dst[:, 0:n], lhs, gates[:, 0:n], start=True, stop=True).then_inc(done, 1)

            def head(t, buf, hh):
                return buf[:, t * COL + hh * P:t * COL + (hh + 1) * P]

            def gdn_qk(g):
                pe.wait_ge(wide_taken, 2 * (W_GDN + 3 * g + 1))
                turn_natural("gdn", ("q", "k"), g, n0)

            def gdn_norms(g):
                pe.wait_ge(s["squared"], g + 1)
                for n, step in enumerate(("sq", "sk")):
                    dst, done = take("gdn", step, g)
                    pe.matmul(dst[:, :], ones[:, :], sq[:, n * COL:(n + 1) * COL], start=True, stop=True).then_inc(done, 1)

            def gdn_products(g):
                pe.wait_ge(s["unit_ready"], g + 1)
                dst, done = take("gdn", "kn", g)
                for h in range(2):
                    for t in range(TT):
                        at = COL + h * SEQ + t * P
                        tr = pe.transpose(dst[:, (2 * t + h) * P:(2 * t + h + 1) * P], cv[:, at:at + P], ident)
                tr.then_inc(done, 1)
                pe.wait_ge(s["gs_ready"], g + 1)
                for t in range(TT):
                    dst, done = take("gdn", f"row{t}", g)
                    for hh in range(4):
                        mm = pe.matmul(dst[:, hh * P:(hh + 1) * P], small[:, 4 * t + hh:4 * t + hh + 1].to_broadcast([P, P]),
                                       tri, start=True, stop=True)
                    mm.then_inc(done, 1)
                for step, off in (("kk", COL), ("qk", 0)):
                    dst, done = take("gdn", step, g)
                    for t in range(TT):
                        for h in range(2):
                            at = h * SEQ + t * P
                            mm = pe.matmul(dst[:, (2 * t + h) * P:(2 * t + h + 1) * P], cv[:, COL + at:COL + at + P],
                                           cv[:, off + at:off + at + P], start=True, stop=True)
                    mm.then_inc(done, 1)

            def gdn_first(g):
                for t in range(TT):
                    pe.wait_ge(s["lower_ready"], 2 * g + t + 1)
                    dst, done = take("gdn", f"u{t}", g)
                    for hh in range(4):
                        tr = pe.transpose(dst[:, hh * P:(hh + 1) * P], head(t, xi, hh), ident)
                    tr.then_inc(done, 1)

            def gdn_level_p(g, n):
                size = LEVELS[n]
                for t in range(TT):
                    in_place("gdn", f"u{t}" if n == 1 else f"n{size // 2}_{t}", g)
                    dst, done = take("gdn", f"p{size}_{t}", g)
                    for hh in range(4):
                        mm = pe.matmul(dst[:, hh * P:(hh + 1) * P], head(t, lw, hh), head(t, ui, hh), start=True, stop=True)
                    mm.then_inc(done, 1)

            def gdn_level_n(g, n):
                size, last = LEVELS[n], n == len(LEVELS) - 1
                for t in range(TT):
                    in_place("gdn", f"p{size}_{t}", g)
                    dst, done = take("gdn", f"n{size}_{t}", g)

                    def half(ap, side):
                        return ap.rearrange("p (n two s) -> p n two s", two=2, s=size)[:, :, side, :]

                    def to(at):
                        return dst[:, at:at + 64].rearrange("p (n s) -> p n s", s=size)
                    for hh in range(4):
                        mm = pe.matmul(to(hh * 64), head(t, xi, hh), half(head(t, pi, hh), 1), start=True, stop=True)
                        if not last:
                            mm = pe.matmul(to(256 + hh * 64), head(t, pi, hh), half(head(t, xi, hh), 0), start=True, stop=True)
                    mm.then_inc(done, 1)

            def gdn_v(g):
                pe.wait_ge(wide_taken, 2 * (W_GDN + 3 * g + 2))
                turn_natural("gdn", ("va", "vb"), g, n1)

            def gdn_v_back(g, t):
                pe.wait_ge(s["silu_done"], 2 * g + 2)
                dst, done = take("gdn", ("va2", "vb2")[t], g)
                for k in range(4):
                    tr = pe.transpose(dst[:, k * P:(k + 1) * P], sq[:, k * SEQ + t * P:k * SEQ + (t + 1) * P], ident)
                tr.then_inc(done, 1)

            def per_head(step, g, lhs, rhs):
                dst, done = take("gdn", step, g)
                for hh in range(4):
                    mm = pe.matmul(dst[:, hh * P:(hh + 1) * P], lhs(hh), rhs[:, hh * P:(hh + 1) * P], start=True, stop=True)
                mm.then_inc(done, 1)

            def gdn_run(g, n):
                if n == 0:
                    in_place("gdn", "n64_0", g)
                    per_head("vn0", g, lambda hh: head(0, ui, hh), n1[:, 0:COL])
                if n == 1:
                    in_place("gdn", "vn0", g)
                    pe.wait_ge(s["kn_ready"], g + 1)
                    per_head("st", g, lambda hh: head(0, xi, hh), vn)
                    per_head("o0", g, lambda hh: head(0, dt_, hh), vn)
                if n == 2:
                    in_place("gdn", "st", g)
                    for step, off in (("ks", COL), ("qs", 0)):
                        dst, done = take("gdn", step, g)
                        for h in range(2):
                            at = off + h * SEQ + P
                            mm = pe.matmul(dst[:, h * SEQ:(h + 1) * SEQ], cv[:, at:at + P], st[:, h * SEQ:(h + 1) * SEQ],
                                           start=True, stop=True)
                        mm.then_inc(done, 1)
                if n == 3:
                    in_place("gdn", "ks", g)
                    per_head("vn1", g, lambda hh: head(1, ui, hh), xi[:, COL:2 * COL])
                if n == 4:
                    in_place("gdn", "vn1", g)
                    per_head("o1", g, lambda hh: head(1, dt_, hh), vn)

            def att_q(phase, g, w):
                pe.wait_ge(wide_taken, 2 * (w + 1))
                turn_natural(phase, ("qa", "qb"), g, n0)

            def att_scores(phase, g):
                in_place(phase, "qa", g)
                in_place(phase, "qb", g)
                for t in range(TT):
                    dst, done = take(phase, f"s{t}", g)
                    for h in range(2):
                        for k in range(2):
                            c = 2 * h + k
                            mm = pe.matmul(dst[:, h * SEQ:(h + 1) * SEQ], cv[:, c * SEQ + t * P:c * SEQ + (t + 1) * P],
                                           mk[:, (4 * g + c) * SEQ:(4 * g + c + 1) * SEQ], start=k == 0, stop=k == 1)
                    mm.then_inc(done, 1)

            def att_turn(phase, g):
                in_place(phase, "s0", g)
                in_place(phase, "s1", g)
                for h, step in enumerate(("pa", "pb")):
                    turn(phase, step, g, lambda k, t: lw[:, t * COL + h * SEQ + k * P:t * COL + h * SEQ + (k + 1) * P])

            def att_out(phase, g):
                in_place(phase, "pa", g)
                in_place(phase, "pb", g)
                for t in range(TT):
                    dst, done = take(phase, f"o{t}", g)
                    for h in range(2):
                        for k in range(2):
                            at = h * COL + k * SEQ + t * P
                            v = k * 1024 + g * COL + h * SEQ
                            mm = pe.matmul(dst[:, h * SEQ:(h + 1) * SEQ], ui[:, at:at + P], mv[:, v:v + SEQ],
                                           start=k == 0, stop=k == 1)
                    mm.then_inc(done, 1)

            def layer(m, w, b0, steps, phase, att):
                def body(g, pair, first=False):
                    at = m if first else 4 * g + (m - 1)
                    wq = w + 3 * g
                    b = b0 + g - 1

                    def in_v(q):
                        if not first:
                            steps(g - 1, 40 + q)
                        steps(g, 8 + q)

                    def in_z(q):
                        steps(g - 1, 48 + q)
                        steps(g, 16 + q)

                    def in_first_z(q):
                        steps(g, 16 + 2 * q)
                        steps(g, 17 + 2 * q)
                    if first:
                        wide(at, pair, wq, 0, lambda q: gdn_sums() if phase == "gdn" and q == 3 else None)
                        wide(at + 1, 1 - pair, wq, 4 * b0, in_v)
                        wide(at + 2, pair, wq + 1, 4 * b0, in_first_z)
                    else:
                        wide(at, pair, wq - 1, 4 * b - 1, lambda q: steps(g - 1, 32 + q))
                        wide(at + 1, 1 - pair, wq, 4 * b, in_v)
                        wide(at + 2, pair, wq + 1, 0, in_z)
                        tall(at + 3, b, 1 - pair, wq + 3, (phase, g - 1), lambda q: steps(g, 24 + q))
                body(0, 0, True)
                body(1, 1)
                with pe.Fori(0, (GROUPS - 2) // 2) as r:
                    body(2 * r + 2, 0)
                    body(2 * r + 3, 1)
                m += 3 + 4 * (GROUPS - 1)
                w += 3 * GROUPS
                for g in range(MGROUPS):
                    b = b0 + GROUPS + g

                    def in_q(q):
                        if g == 0:
                            steps(GROUPS - 1, 32 + q)
                        elif q == 5:
                            branch(att, g - 1, b - 1)

                    def in_z(q):
                        if g == 0:
                            steps(GROUPS - 1, 40 + q)
                        if g == 0 and q == 7:
                            steps(GROUPS - 1, 48)
                        if q == 3:
                            att_q(att, g, w + 2 * g)
                        if q == 7:
                            att_scores(att, g)

                    def in_out(q):
                        if q == 3:
                            att_turn(att, g)
                        if q == 5:
                            att_out(att, g)
                        if q == 7 and g == MGROUPS - 1:
                            branch(att, g, b)
                    wide(m, 0, w + 2 * g, 4 * (b - 1), in_q)
                    wide(m + 1, 1, w + 2 * g, 4 * (b - 1), in_z)
                    tall(m + 2, b - 1, 0, w + 2 * g + 2, (att, g - 1) if g else (phase, GROUPS - 1), in_out)
                    m += 3
                tall(m, b0 + BR - 1, 0, w + 4, (att, MGROUPS - 1), after_tall=True)

            def ret_steps(g, q):
                if q == 11:
                    ret_qk(g)
                if q == 15:
                    ret_scores(g)
                if q == 19:
                    ret_out(g)
                if q == 37:
                    branch("ret", g, g)

            def gdn_steps(g, q):
                if q == 9:
                    gdn_qk(g)
                if q == 14:
                    gdn_norms(g)
                if q == 17:
                    gdn_products(g)
                if q == 19:
                    gdn_v(g)
                if q == 24:
                    gdn_first(g)
                if q in range(26, 38, 2):
                    gdn_level_p(g, (q - 24) // 2)
                if q in range(27, 38, 2):
                    gdn_level_n(g, (q - 25) // 2)
                if q in (33, 35):
                    gdn_v_back(g, (q - 33) // 2)
                if q in range(38, 43):
                    gdn_run(g, q - 38)
                if q == 48:
                    branch("gdn", g, B_L1 + g)

            def hgrn_turn(g, n):
                pe.wait_ge(wide_taken, 2 * (W_HG + 4 * g + 1 + n))
                turn_natural("hgrn", (("qa", "qb"), ("fa", "fb"))[n], g, (n0, n1)[n])

            def hgrn_diagonal(g):
                in_place("hgrn", "qa", g)
                in_place("hgrn", "qb", g)
                pe.wait_ge(s["ksc_ready"], g + 1)
                for t in range(TT):
                    dst, done = take("hgrn", f"d{t}", g)
                    for hh in range(4):
                        at = hh * SEQ + t * P
                        mm = pe.matmul(dst[:, hh * P:(hh + 1) * P], lw[:, at:at + P], cv[:, at:at + P], start=True, stop=True)
                    mm.then_inc(done, 1)

            def hgrn_level(g, n):
                pe.wait_ge(s["lev_ready"], 8 * g + n + 1)
                ks, qs = (xi, ui)[n % 2], dn[:, (n % 2) * COL:(n % 2 + 1) * COL]
                dst, done = take("hgrn", "x" if n == 7 else f"l{LEVELS[n]}", g)
                for hh in range(4):
                    if n == 7:
                        mm = pe.matmul(dst[:, hh * P:(hh + 1) * P], ks[:, hh * SEQ:hh * SEQ + P], qs[:, hh * P:(hh + 1) * P],
                                       start=True, stop=True)
                        continue
                    for t in range(TT):
                        at = (2 * hh + t) * 64
                        mm = pe.matmul(dst[:, at:at + 64], ks[:, hh * SEQ + t * P:hh * SEQ + (t + 1) * P], qs[:, at:at + 64],
                                       start=True, stop=True)
                mm.then_inc(done, 1)

            def hgrn_out(g):
                pe.wait_ge(wide_taken, 2 * (W_HG + 4 * g + 3))
                in_place("hgrn", "x", g)
                in_place("hgrn", "l64", g)
                for t in range(TT):
                    dst, done = take("hgrn", f"o{t}", g)
                    for hh in range(4):
                        to, at = dst[:, hh * P:(hh + 1) * P], hh * P
                        own = dt_[:, (2 * hh + t) * P:(2 * hh + t + 1) * P]
                        if t:
                            pe.matmul(to, kn[:, at:at + P], vn[:, at:at + P], start=True, stop=False)
                        mm = pe.matmul(to, own, (vn, st)[t][:, at:at + P], start=t == 0, stop=True)
                    mm.then_inc(done, 1)

            def pool_bands(g):
                src = (n0, n1)[g]
                pe.wait_ge(wide_taken, 2 * (W_HG + 8 + g + 1))
                pe.wait_ge(s["pool_loaded"], 32)
                for n, step in enumerate(("da", "db")):
                    dst, done = take("pool", step, g)
                    band = big[:, 2048 + (2 * g + n) * 384:2048 + (2 * g + n + 1) * 384]
                    for k in range(2):
                        c = (2 * n + k) * P
                        pe.matmul(dst[:, k * SEQ:k * SEQ + P], src[:, c:c + P], band[:, 0:P], start=True, stop=True)
                        pe.matmul(dst[:, k * SEQ + P:(k + 1) * SEQ], src[:, c:c + P], band[:, P:2 * P], start=True, stop=False)
                        mm = pe.matmul(dst[:, k * SEQ + P:(k + 1) * SEQ], src[:, COL + c:COL + c + P], band[:, 2 * P:384],
                                       start=False, stop=True)
                    mm.then_inc(done, 1)

            def pool_maps(g):
                in_place("pool", "da", g)
                in_place("pool", "db", g)
                for n, step in enumerate(("ya", "yb")):
                    dst, done = take("pool", step, g)
                    for c in range(2):
                        for k in range(2):
                            at = 4096 + ((2 * g + n) * 2 + k) * SEQ + c * P
                            mm = pe.matmul(dst[:, c * SEQ:(c + 1) * SEQ], big[:, at:at + P],
                                           cv[:, (2 * n + k) * SEQ:(2 * n + k + 1) * SEQ], start=k == 0, stop=k == 1)
                    mm.then_inc(done, 1)

            def turn_columns(q):
                if q == 3:
                    pe.wait_ge(s["rows_loaded"], 16 * N_LOADS)
                    for r, rows in enumerate((N_ROWS, 96, 96)):
                        tr = pe.transpose(acc[1][0][:, r * P:r * P + rows], zs[0:rows, r * P:(r + 1) * P], ident[0:rows, 0:rows])
                    tr.then_inc(s["cols_turned"], 1)
                if q == 7:
                    pe.wait_ge(s["cols_ready"], 1)

            pe.wait_ge(s["ones_made"], 1)
            pe.wait_ge(s["ident_loaded"], 16)
            turn_mem("mem0", 0)
            kv_units("kv0", U_KV0, 0, "mem0", 0, turn_columns)
            pe.wait_ge(s["consts_loaded"], 16)
            pe.wait_ge(s["x_loaded"], 16)
            turn_x("x0", x_sb, 0)
            a_in_place("x0")
            layer(U_RET, W_RET, 0, ret_steps, "ret", "att0")
            turn_mem("mem1", 1)
            kv_units("kv1", U_KV1, W_KV1, "mem1", 4 * B_L1)
            turn_x("x1", x_sb, 1)
            a_in_place("x1")
            gdn_gates()
            layer(U_GDN, W_GDN, B_L1, gdn_steps, "gdn", "att1")
            turn_x("h2", x_sb, 2)
            a_in_place("h2")

            def hgrn_steps(g, q):
                if q in (-1, 1):
                    hgrn_turn(g, (q + 1) // 2)
                if q == 5:
                    hgrn_diagonal(g)
                if q in range(8, 23, 2):
                    hgrn_level(g, (q - 8) // 2)
                if q == 24:
                    hgrn_out(g)
                if q == 30:
                    branch("hgrn", g, B_HG + g)

            def beside(n):
                def between(q):
                    for g in range(2):
                        hgrn_steps(g, 8 * (n - 2 - 4 * g) + q)
                return between

            def in_p1(q):
                beside(10)(q)
                if q == 3:
                    pool_bands(0)

            def in_o1(q):
                if q == 1:
                    pool_maps(0)
                    pool_bands(1)
                if q == 5:
                    pool_maps(1)

            w = W_HG
            for n in range(8):
                wide(U_HG + n, n % 2, w + max(n - 1, 0), 4 * B_HG, beside(n))
            wide(U_P0, 0, w + 7, 4 * B_HG, beside(8))
            tall(U_P0 + 1, B_HG, 1, w + 9, ("hgrn", 0), beside(9))
            wide(U_P0 + 2, 1, w + 9, 4 * B_HG + 3, in_p1)
            tall(U_P0 + 3, B_HG + 1, 0, w + 10, ("hgrn", 1), in_o1, added=4 * B_HG + 4)
            tall(U_P0 + 4, B_HG + 2, 0, w + 10, ("pool", 0), after_tall=True)
            tall(U_P0 + 5, B_HG + 3, 0, w + 10, ("pool", 1), after_tall=True)
            turn_x("h3", x_sb, 3)
            a_in_place("h3")

            def mlp(g, pair, last=None):
                b = g + (B_MLP - 1)
                wide(2 * g + (U_MLP - 1), pair, g + (W_MLP - 1), 4 * b - 1,
                     lambda q: branch("mlp", g - 1, b - 2) if q == 3 else None)
                tall(2 * g + U_MLP, b, 1 - pair, g + (W_MLP + 1), ("mlp", g - 1), last, added=4 * b)
            wide(U_MLP, 0, W_MLP, 4 * B_MLP)
            with pe.Fori(0, (FFG - 2) // 2) as r:
                mlp(2 * r + 1, 1)
                mlp(2 * r + 2, 0)
            mlp(FFG - 1, 1, lambda q: branch("mlp", FFG - 1, B_MLP + FFG - 3) if q == 6 else None)
            tall(UNITS - 1, B_MLP + FFG - 1, 0, W_MLP + FFG, ("mlp", FFG - 1), after_tall=True)

        @block.scalar
        def _(act):
            def half(m, q):
                j = q // 2
                if q % 2 == 0:
                    act.wait_ge(raw_loaded[j], 32 * m + 32)
                if not (isinstance(m, int) and 8 * m + q < 4):
                    act.wait_ge(sub_used, 8 * m + q - 3)
                act.activation(whi[q % 4][:, :], raw[j][:, (q % 2) * HALF:(q % 2 + 1) * HALF], ACT.Copy).then_inc(hi_ready, 1)

            def hi(m, j):
                half(m, 2 * j)
                half(m, 2 * j + 1)

            def unit(m, between=None, first=0):
                for q in range(2 * first, 8):
                    half(m, q)
                    if between:
                        between(q)

            def loads(step):
                return lambda q: step(q // 2) if q % 2 else None

            def last_unit(m, parts):
                for q in range(8):
                    if q == 3:
                        parts()
                    half(m, q)

            def ahead(m):
                hi(m, 0)
                hi(m, 1)

            def wide_out(m, pair, func, dst, norm=None):
                act.wait_ge(sub_used, 8 * m + 8)
                for t in range(TT):
                    scale = 1.0 if norm is None else inverse_rms(norm)[:, t:t + 1]
                    act.activation(dst(t), acc[pair][t][:, :], func, scale=scale).then_inc(wide_taken, 1)

            def gate(n):
                return gates[:, n * TT * NVH:(n + 1) * TT * NVH].rearrange("p (t c) -> p t c", t=TT)

            def tiles(buf):
                return lambda t: buf[:, t * COL:(t + 1) * COL]

            def full(phase, step, g=0):
                b, n = fill(phase, step, g)
                act.wait_ge(filled[b], n)
                return bank[b], emptied[b]

            def copy_out(phase, step, g, dst, src=lambda b: b[:, :], func=ACT.Copy, **kw):
                b, done = full(phase, step, g)
                act.activation(dst, src(b), func, **kw).then_inc(done, 1)

            def a_parts(phase, used, scale=None):
                if used:
                    act.wait_ge(sub_used, 8 * used)
                for f in range(8):
                    b, _ = full(phase, f"f{f}")
                    for k in range(2) if scale is not None else [None]:
                        if k is None:
                            op = act.activation(a_hi[:, f * COL:(f + 1) * COL], b[:, :], ACT.Copy)
                        else:
                            at = f * COL + k * SEQ
                            op = act.activation(a_hi[:, at:at + SEQ], b[:, k * SEQ:(k + 1) * SEQ], ACT.Copy,
                                                scale=cols[:, scale + 2 * f + k:scale + 2 * f + k + 1])
                    op.then_inc(a_hi_in, 1)

            def b_parts(phase, g, used, scale=None):
                if used is not None:
                    act.wait_ge(sub_used, 8 * used)
                for n, step in enumerate(("ba", "bb")):
                    b, _ = full(phase, step, g)
                    if scale is None:
                        op = act.activation(b_hi[:, n * COL:(n + 1) * COL], b[:, :], ACT.Copy)
                    else:
                        for k in range(2):
                            at = n * COL + k * SEQ
                            op = act.activation(b_hi[:, at:at + SEQ], b[:, k * SEQ:(k + 1) * SEQ], ACT.Copy,
                                                scale=scale(2 * n + k))
                    op.then_inc(b_hi_in, 1)

            def mem_load(layer, c):
                src = mem_in[0][:, c * COL:(c + 1) * COL].rearrange("(t p) c -> p t c", p=P)
                dst = (n1, n0, cv, sq)[c][:, :].rearrange("p (t c) -> p t c", t=TT)
                act.dma_start(dst, src).then_inc(mem_loaded[c], 16)

            def mem_parts(phase, used):
                if used:
                    act.wait_ge(sub_used, 8 * used)
                for f in range(8):
                    b, _ = full(phase, f"f{f}")
                    act.activation(a_hi[:, f * COL:(f + 1) * COL], b[:, :], ACT.Copy).then_inc(a_hi_in, 1)

            def kv_slots(phase, m, middle=lambda: None):
                def k_out(c, n):
                    def between(j):
                        if j == 0:
                            wide_out(m + n, n % 2, ACT.Copy, tiles(n0))
                        if j == 2:
                            for i, step in enumerate("ab"):
                                at = (4 * c + 2 * i) * SEQ
                                copy_out(phase, f"k{c}{step}", 0, mk[:, at:at + COL])
                    return loads(between)

                def v_out(c, n):
                    return lambda q: wide_out(m + n, n % 2, ACT.Copy, lambda t: mv[:, t * 1024 + c * COL:t * 1024 + (c + 1) * COL]) if q == 2 else None
                unit(m, columns_out if m == U_KV0 else None, 2)
                unit(m + 1, k_out(0, 0))
                middle()
                unit(m + 2, k_out(1, 1))
                unit(m + 3, v_out(0, 2))
                return v_out(1, 3)

            def root(n, dst, src, count, scale):
                act.wait_ge(s["stats"], n)
                act.activation(small[:, dst:dst + count], src, ACT.Sqrt, scale=scale, bias=eps_sb[:, 1:2]).then_inc(s["root_ready"], 1)

            def head_roots(n):
                root(n, 226, small[:, 218:226], 8, 1.0 / P)

            def layer(m, w, b0, steps, phase, att, first_steps=None):
                def body(g, pair, first=False):
                    at = m if first else 4 * g + (m - 1)
                    before = m if isinstance(g, int) and g == 1 else at - 4

                    def in_qk(q):
                        if isinstance(g, int) and g == 1 and q == 2:
                            z_out(phase, 0, m + 2, 0)
                        steps(g - 1, 32 + q, before, 1 - pair)

                    def in_v(q):
                        if not first:
                            steps(g - 1, 40 + q, before, 1 - pair)
                        steps(g, 8 + q, at, pair)

                    def in_z(q):
                        steps(g - 1, 48 + q, before, 1 - pair)
                        steps(g, 16 + q, at, pair)

                    def in_out(q):
                        if q == 2:
                            z_out(phase, g, at + 2, pair)
                        steps(g, 24 + q, at, pair)
                    if first:
                        unit(at, first_steps, 2)
                        unit(at + 1, in_v)
                        for q in range(8):
                            half(at + 2, q)
                            steps(g, 16 + 2 * q, at, pair)
                            steps(g, 17 + 2 * q, at, pair)
                    else:
                        unit(at, in_qk)
                        unit(at + 1, in_v)
                        unit(at + 2, in_z)
                        unit(at + 3, in_out)
                body(0, 0, True)
                body(1, 1)
                with act.Fori(0, (GROUPS - 2) // 2) as r:
                    body(2 * r + 2, 0)
                    body(2 * r + 3, 1)
                m += 3 + 4 * (GROUPS - 1)
                for g in range(MGROUPS):
                    b = b0 + GROUPS + g

                    def in_q(q):
                        if g == 0:
                            steps(GROUPS - 1, 32 + q, m - 4, 1)
                        elif q == 7:
                            b_parts(att, g - 1, m)

                    def in_z(q):
                        if g == 0:
                            steps(GROUPS - 1, 40 + q, m - 4, 1)
                        if q == 2:
                            if g == 0 and phase == "ret":
                                act.wait_ge(s["rot_ready"], GROUPS)
                            wide_out(m, 0, ACT.Copy, tiles(n0))
                        if q == 7:
                            for n, step in enumerate(("qa", "qb")):
                                copy_out(att, step, g, cv[:, n * COL:(n + 1) * COL])

                    def in_out(q):
                        if g == 0 and q in (0, 2):
                            steps(GROUPS - 1, 48 + 2 * q, m - 4, 1)
                        if q == 2:
                            act.wait_ge(s["branch_ready"], b)
                            wide_out(m + 1, 1, ACT.Silu, tiles(zs))
                            for t in range(TT):
                                bk, done = full(att, f"s{t}", g)
                                act.wait_ge(s["mneg"], 2 * (n_att(att) + g) + t + 1)
                                for h in range(2):
                                    c = 2 * t + h
                                    op = act.activation(lw[:, c * SEQ:(c + 1) * SEQ], bk[:, h * SEQ:(h + 1) * SEQ], ACT.Exp,
                                                        scale=MSCALE, bias=small[:, 110 + c:111 + c],
                                                        accum_out=small[:, 120 + c:121 + c])
                                op.then_inc(done, 1)
                        if q == 6:
                            for n, step in enumerate(("pa", "pb")):
                                copy_out(att, step, g, ui[:, n * COL:(n + 1) * COL])
                    unit(m, in_q)
                    unit(m + 1, in_z)
                    unit(m + 2, in_out)
                    m += 3
                last_unit(m, lambda: b_parts(att, MGROUPS - 1, m))

            def n_att(att):
                return 0 if att == "att0" else MGROUPS

            def ret_scale(g):
                def column(k):
                    return small[:, 104 + k:105 + k]
                act.activation(small[:, 104:108], cols[:, ds(4 * g + C_RG, 4)], ACT.Copy).then_inc(s["scale_ready"], 1)
                act.wait_ge(s["scale_ready"], g + 1)
                return column

            def decays(g):
                src = consts[:, ds(C_DEC + 2 * SEQ * g, 2 * SEQ)]
                act.dma_start(dt_[:, 0:2 * SEQ], src).then_inc(s["decay_loaded"], 16)

            def is_first(g):
                return isinstance(g, int) and g == 0

            def z_out(phase, g, m, pair):
                if not is_first(g):
                    b, n = fill(phase, "ba", g - 1)
                    act.wait_ge(filled[b], n)
                wide_out(m, pair, ACT.Silu, tiles(zs))

            def ret_steps(g, n, at, pair):
                if n == 10:
                    if not is_first(g):
                        act.wait_ge(s["rot_ready"], g)
                        b, c = fill("ret", "s1", g - 1)
                        act.wait_ge(emptied[b], c)
                    wide_out(at, pair, ACT.Copy, tiles(n0))
                    decays(g)
                if n == 14:
                    for i, step in enumerate("qk"):
                        copy_out("ret", step, g, lw[:, i * COL:(i + 1) * COL])
                if n == 18:
                    if not is_first(g):
                        b, c = fill("ret", "o1", g - 1)
                        act.wait_ge(filled[b], c)
                    wide_out(at + 1, 1 - pair, ACT.Copy, tiles(n1))
                if n == 23:
                    root(g + 1, 36, small[:, 24:32].rearrange("p (n two) -> p n two", two=2)[:, :, 1], 4, 1.0)
                if n == 39:
                    b_parts("ret", g, at + (3 if is_first(g) else 4), ret_scale(g))

            def gdn_steps(g, n, at, pair):
                if n == 10:
                    wide_out(at, pair, ACT.Copy, tiles(n0))
                if n == 13:
                    if not is_first(g):
                        act.wait_ge(s["conv_done"], 2 * g)
                    for i, step in enumerate("qk"):
                        copy_out("gdn", step, g, cb[:, :].rearrange("p (c s) -> p c s", c=4)[:, 2 * i:2 * i + 2, 3:],
                                 lambda b: b[:, :].rearrange("p (c s) -> p c s", c=2))
                if n == 15:
                    act.wait_ge(s["conv_done"], 2 * g + 1)
                    act.activation(cv[:, :], cv[:, :], ACT.Silu).then_inc(s["silu_done"], 1)
                    act.wait_ge(s["silu_done"], 2 * g + 1)
                    act.activation(sq[:, :], cv[:, :], ACT.Square).then_inc(s["squared"], 1)
                if n == 17:
                    for i, step in enumerate(("sq", "sk")):
                        copy_out("gdn", step, g, lw[:, i * COL:(i + 1) * COL], func=ACT.Sqrt, bias=eps_sb[:, 1:2])
                if n == 18:
                    if not is_first(g):
                        b, c = fill("gdn", "o1", g - 1)
                        act.wait_ge(filled[b], c)
                    wide_out(at + 1, 1 - pair, ACT.Copy, tiles(n1))
                if n == 21:
                    if not is_first(g):
                        b, c = fill("gdn", "o1", g - 1)
                        act.wait_ge(emptied[b], c)
                    copy_out("gdn", "kn", g, kn[:, :])
                if n == 22:
                    for t in range(TT):
                        b, c = fill("gdn", f"row{t}", g)
                        act.wait_ge(emptied[b], c)
                    for i, buf in enumerate((dn, dt_)):
                        act.activation(buf[:, :], buf[:, :], ACT.Exp, scale=1.0 if i else -1.0).then_inc(s["decay_ready"], 1)
                if n == 23:
                    for i, step in enumerate(("va", "vb")):
                        copy_out("gdn", step, g, cb[:, :].rearrange("p (c s) -> p c s", c=4)[:, 2 * i:2 * i + 2, 3:],
                                 lambda b: b[:, :].rearrange("p (c s) -> p c s", c=2))
                if n == 28:
                    for t in range(TT):
                        copy_out("gdn", f"u{t}", g, ui[:, t * COL:(t + 1) * COL])
                if n == 35:
                    act.wait_ge(s["conv_done"], 2 * g + 2)
                    act.activation(sq[:, :], sq[:, :], ACT.Silu).then_inc(s["silu_done"], 1)
                if n in (37, 39):
                    t = (n - 37) // 2
                    b, done = full("gdn", ("va2", "vb2")[t], g)
                    for hh in range(4):
                        to = t * COL + hh * P
                        op = act.activation(n1[:, to:to + P], b[:, hh * P:(hh + 1) * P], ACT.Copy,
                                            scale=small[:, 16 + 4 * t + hh:17 + 4 * t + hh])
                    op.then_inc(done, 1)
                if n == 41:
                    copy_out("gdn", "vn0", g, vn[:, :])
                if n == 43:
                    copy_out("gdn", "st", g, st[:, :])
                if n == 44:
                    act.wait_ge(s["kn_ready"], g + 1)
                    b, done = full("gdn", "qs", g)
                    for hh in range(4):
                        op = act.activation(kn[:, hh * P:(hh + 1) * P], b[:, hh * P:(hh + 1) * P], ACT.Copy,
                                            scale=small[:, 28 + hh:29 + hh])
                    op.then_inc(done, 1)
                if n == 45:
                    copy_out("gdn", "vn1", g, vn[:, :])
                if n == 48:
                    head_roots(GROUPS + g + 1)
                if n == 52:
                    b_parts("gdn", g, at + (3 if is_first(g) else 4), gdn_scale)

            def gdn_scale(k):
                return cols[:, C_GG:C_GG + 1]

            def rms_root(n):
                act.activation(small[:, 242 + 2 * n:244 + 2 * n], small[:, 148:150], ACT.Sqrt, scale=1.0 / D, bias=eps_sb[:, 1:2])\
                    .then_inc(s["rms_root"], 1)

            def x_square_sums(n):
                act.wait_ge(s["x_final"], 16 + 8 * (n // 2))
                for t in range(TT):
                    act.activation(big[:, 4096:6144], x_sb[:, t * D:(t + 1) * D], ACT.Square, accum_out=small[:, 148 + t:149 + t])
                    act.drain()
                rms_root(n)

            def y_square_sums(n, b, between=lambda c: None):
                for c in range(4):
                    act.wait_ge(out_added, 2 * (4 * b + c + 1))
                    for t in range(TT):
                        op = act.activation(zs[:, t * COL:(t + 1) * COL], y_sb[:, t * D + c * COL:t * D + (c + 1) * COL], ACT.Square,
                                            accum_out=small[:, 140 + 4 * t + c:141 + 4 * t + c])
                    if c < 3:
                        act.drain()
                        for k in {1: (0, 1), 2: (2, 3)}.get(c, ()):
                            between(k)
                op.then_inc(s["y_squared"], 1)
                act.wait_ge(s["y_summed"], n // 2 + 1)
                rms_root(n)

            def broadcast(dst, row):
                act.dma_start(dst, row.partition_broadcast(P)).then_inc(s["rows_spread"], 16)

            act.dma_start(cst[:, 0:P], consts[:, 0:P]).then_inc(s["ident_loaded"], 16)
            for c in range(4):
                mem_load(0, c)
            at = 0
            for src in (ret_g[0], gdn_g[0], pool_b[0].rearrange("w c -> (w c)"), pool_scale[0],
                        lb_logits.rearrange("l c -> (l c)"), hgrn_w[0], mix_pre[0], mlp_pre[0]):
                rows = src.rearrange("(r p) -> r p", p=P)
                act.dma_start(zs[at:at + rows.shape[0], 0:P], rows).then_inc(s["rows_loaded"], 16)
                at += rows.shape[0]
            for i in range(2):
                for j in range(2):
                    src = conv_w[0][2 * i + j].rearrange("(r p) -> r p", p=P)
                    act.dma_start(zs[48 * j:48 * j + 48, (i + 1) * P:(i + 2) * P], src).then_inc(s["rows_loaded"], 16)
            act.dma_start(pos_sb[:, :], pos_in[0].rearrange("(t p) -> p t", p=P), allow_slow_non_contiguous=True).then_inc(s["pos_loaded"], 16)
            ahead(U_KV0)
            act.wait_ge(s["ones_made"], 3)
            mem_parts("mem0", 0)
            act.dma_start(x_sb[:, :].rearrange("p (t c) -> p t c", t=TT), x_in[0].rearrange("(t p) c -> p t c", p=P)).then_inc(s["x_loaded"], 16)
            act.dma_start(cst[:, P:], consts[:, P:C_MAIN]).then_inc(s["consts_loaded"], 16)

            def columns_out(q):
                if q == 7:
                    act.wait_ge(s["cols_turned"], 1)
                    for r, rows in enumerate((N_ROWS, 96, 96)):
                        op = act.activation(cols[:, r * P:r * P + rows], acc[1][0][:, r * P:r * P + rows], ACT.Copy)
                    op.then_inc(s["cols_ready"], 1)

            def rotation_and_bound():
                act.wait_ge(s["trig_arg"], 1)
                act.activation(gates[:, 0:4 * 64], gates[:, 0:4 * 64], ACT.Sin).then_inc(s["trig_ready"], 1)
                act.wait_ge(s["lb_arg"], 1)
                act.activation(lb[:, 0:8], lb[:, 0:8], ACT.Sigmoid).then_inc(s["lb_ready"], 1)
            last_v = kv_slots("kv0", U_KV0, rotation_and_bound)
            ahead(U_RET)
            last_v(2)
            a_parts("x0", U_KV0 + 4)
            layer(U_RET, W_RET, 0, ret_steps, "ret", "att0")

            def layer_norm(i):
                act.wait_ge(s["ln_stats"], i + 1)
                act.activation(small[:, 160:162], small[:, 156:160].rearrange("p (n two) -> p n two", two=2)[:, :, 1],
                               ACT.Sqrt, bias=eps_sb[:, 0:1]).then_inc(s["ln_root"], 1)

            def ln_rows(i):
                broadcast(lnw[:, 0:D], ln_g[i])
                broadcast(lnw[:, D:2 * D], ln_b[i])

            act.wait_ge(s["branch_ready"], B_L1)
            for c in range(4):
                mem_load(1, c)
            ln_rows(0)
            ahead(U_KV1)
            mem_parts("mem1", U_ATT0 + 5)
            last_v = kv_slots("kv1", U_KV1, lambda: layer_norm(0))
            n48 = 2 * NVH
            act.dma_start(n0[:, 0:16 * n48].rearrange("p (k c) -> p k c", k=16),
                          w_gdn[0][:, CONV + MEMW + MIX:].rearrange("(k p) c -> p k c", p=P)).then_inc(s["ab_loaded"], 16)
            act.dma_start(n1[:, 0:NVH], dt_bias[0].partition_broadcast(P)).then_inc(s["ab_loaded"], 16)
            act.dma_start(n1[:, NVH:n48], a_log[0].partition_broadcast(P)).then_inc(s["ab_loaded"], 16)
            ahead(U_GDN)
            last_v(2)
            act.wait_ge(s["ab_loaded"], 48)
            act.activation(b_hi[:, 0:16 * n48], n0[:, 0:16 * n48], ACT.Copy).then_inc(s["ab_hi"], 1)
            a_parts("x1", U_KV1 + 4)
            b, _ = full("gates", "ab")
            ab = b[:, 0:2 * n48].rearrange("p (t c) -> p t c", t=TT)
            act.activation(gate(2), ab[:, :, NVH:], ACT.Sigmoid).then_inc(s["gate_step"], 1)
            act.wait_ge(s["gate_dve"], 1)
            act.activation(n1[:, 160:208], n1[:, 112:160], ACT.Exp, scale=-1.0).then_inc(s["gate_step"], 1)
            act.wait_ge(s["gate_step"], 2)
            act.activation(n1[:, 208:256], n1[:, 160:208], ACT.Ln, bias=1.0).then_inc(s["gate_step"], 1)
            act.activation(n1[:, 256:256 + NVH], n1[:, NVH:n48], ACT.Exp).then_inc(s["gate_step"], 1)

            def gate_sums(q):
                if q != 7:
                    return
                b, done = full("gates", "cum")
                act.activation(gates[:, n48:2 * n48], b[:, 0:n48], ACT.Copy)
                act.activation(gates[:, 3 * n48:4 * n48], b[:, 0:n48], ACT.Exp).then_inc(done, 1)
                act.wait_ge(s["gate_dve"], 2)
                act.activation(gates[:, 4 * n48:5 * n48], n1[:, 288:336], ACT.Exp).then_inc(s["gate_step"], 1)

            layer(U_GDN, W_GDN, B_L1, gdn_steps, "gdn", "att1", gate_sums)
            act.wait_ge(s["branch_ready"], 2 * BR)
            ln_rows(1)
            ahead(U_HG)
            layer_norm(1)
            a_parts("h2", U_ATT1 + 5, C_MP)
            x_square_sums(0)
            act.wait_ge(s["inverse_rms"], 1)

            def hgrn_steps(g, q):
                u = U_HG + 4 * g
                if q == -6:
                    wide_out(u, 0, ACT.Copy, tiles(n0), 0)
                if q == 2:
                    wide_out(u + 1, 1, ACT.Copy, tiles(n1), 0)
                if q == 3:
                    for n, step in enumerate(("qa", "qb")):
                        copy_out("hgrn", step, g, cv[:, n * COL:(n + 1) * COL])
                if q == 5:
                    for n, step in enumerate(("fa", "fb")):
                        copy_out("hgrn", step, g, sq[:, n * COL:(n + 1) * COL], func=ACT.Sigmoid)
                if q == 7:
                    act.wait_ge(s["ksc_ready"], g + 1)
                    act.activation(dn[:, :], dn[:, :], ACT.Ln).then_inc(s["logf_ready"], 1)
                if q == 10:
                    wide_out(u + 2, 0, ACT.Copy, lambda t: (vn, st)[t][:, :], 0)
                if q == 18:
                    wide_out(u + 3, 1, ACT.Sigmoid, tiles(zs), 0)
                for n in range(8):
                    if q == (9 if n < 2 else 8 + 2 * n):
                        act.wait_ge(s["lev_arg"], 8 * g + n + 1)
                        buf = (sq, br)[n % 2]
                        act.activation(buf[:, :], buf[:, :], ACT.Exp).then_inc(s["lev_exp"], 1)
                if q == 29:
                    head_roots(2 * GROUPS + g + 1)
                if q == 34:
                    b_parts("hgrn", g, (U_ATT1 + 7, U_P0 + 2)[g], lambda k: cols[:, C_HW + 4 * g + k:C_HW + 4 * g + k + 1])

            def beside(n):
                def between(q):
                    for g in range(2):
                        hgrn_steps(g, 8 * (n - 2 - 4 * g) + q)
                return between

            def pool_parts(g):
                act.wait_ge(s["pool_mapped"], g + 1)
                act.activation(a_hi[:, g * KB * SEQ:(g + 1) * KB * SEQ], (sq, br)[g][:, :], ACT.Copy).then_inc(s["pool_hi"], 1)

            def pool_in(g):
                for n, step in enumerate(("da", "db")):
                    copy_out("pool", step, g, cv[:, n * COL:(n + 1) * COL])

            def in_o0(q):
                beside(9)(q)
                if q == 2:
                    wide_out(U_P0, 0, ACT.Copy, tiles(n0), 0)
                if q == 6:
                    b, c = fill("hgrn", "o1", 1)
                    act.wait_ge(filled[b], c)
                    act.dma_start(big[:, 2048:2048 + 4 * 384], consts[:, C_POOL:C_POOL + 4 * 384]).then_inc(s["pool_loaded"], 16)
                    act.dma_start(big[:, 4096:6144].rearrange("p (k c) -> p k c", k=8),
                                  pool_w[0].rearrange("w (k p) c -> p (w k) c", p=P)).then_inc(s["pool_loaded"], 16)
                    broadcast(big[:, 0:D], mix_post[0])

            def in_p1(q):
                beside(10)(q)
                if q == 7:
                    pool_in(0)

            def in_o1(q):
                if q == 2:
                    wide_out(U_P0 + 2, 1, ACT.Copy, tiles(n1), 0)
                if q == 5:
                    b, c = fill("pool", "yb", 0)
                    act.wait_ge(filled[b], c)
                    pool_in(1)
                if q == 6:
                    pool_parts(0)

            unit(U_HG, beside(0), 2)
            for n in range(1, 9):
                unit(U_HG + n, beside(n))
            unit(U_P0 + 1, in_o0)
            unit(U_P0 + 2, in_p1)
            unit(U_P0 + 3, in_o1)
            unit(U_P0 + 4, lambda q: pool_parts(1) if q == 1 else None)
            unit(U_P0 + 5)
            y_square_sums(1, B_HG + 3, lambda c: half(U_MLP, c))
            act.wait_ge(s["x_final"], 18)
            broadcast(big[:, 2048:2048 + D], mlp_post[0])
            a_parts("h3", U_P0 + 6, C_LP)
            x_square_sums(2)
            act.wait_ge(s["inverse_rms"], 2)

            def relu_out(g, pair):
                act.wait_ge(s["branch_ready"], g + (B_MLP - 2))
                wide_out(2 * g + (U_MLP - 1) if not isinstance(g, int) or g else U_MLP, pair, ACT.Relu, tiles(n0), 2)

            def mlp(g, pair):
                def in_wide(q):
                    if q == 5:
                        b_parts("mlp", g - 1, 2 * g + (U_MLP - 1))
                unit(2 * g + (U_MLP - 1), in_wide)
                unit(2 * g + U_MLP, lambda q: relu_out(g, pair) if q == 2 else None)
            unit(U_MLP, None, 2)
            hi(U_MLP + 1, 0)
            relu_out(0, 0)
            for j in range(1, 4):
                hi(U_MLP + 1, j)
                if j == 2:
                    b_parts("mlp", 0, None)
            unit(U_MLP + 2, lambda q: relu_out(1, 1) if q == 2 else None)
            mlp(2, 0)
            with act.Fori(1, (FFG - 2) // 2) as r:
                mlp(2 * r + 1, 1)
                mlp(2 * r + 2, 0)
            mlp(FFG - 1, 1)
            last_unit(UNITS - 1, lambda: b_parts("mlp", FFG - 1, UNITS - 1))
            y_square_sums(3, B_MLP + FFG - 1)

        @block.vector
        def _(dve):
            tt, ts, stt = dve.tensor_tensor, dve.tensor_scalar, dve.scalar_tensor_tensor
            MUL, ADD, SUB, MAX, MIN = ALU.mult, ALU.add, ALU.subtract, ALU.max, ALU.min

            one_row = ones[:, 0:1].to_broadcast([P, SEQ])

            def full(phase, step, g=0):
                b, n = fill(phase, step, g)
                dve.wait_ge(filled[b], n)
                return bank[b], emptied[b]

            def turned(phase, step, g):
                b, n = fill(phase, step, g)
                dve.wait_ge(filled[b], n)

            def copied(phase, step, g=0):
                b, n = fill(phase, step, g)
                dve.wait_ge(emptied[b], n)

            def a_part(f, phase, count, scale=None):
                b, done = full(phase, f"f{f}")
                dve.wait_ge(a_hi_in, 8 * count + f + 1)
                hi = a_hi[:, f * COL:(f + 1) * COL].bitcast(f32)
                lo = a_lo[:, f * COL:(f + 1) * COL]
                if scale is None:
                    op = tt(lo, b[:, :], hi, SUB)
                else:
                    for k in range(2):
                        c = slice(k * SEQ, (k + 1) * SEQ)
                        op = stt(out=lo[:, c], in0=b[:, c], scalar=cols[:, scale + 2 * f + k:scale + 2 * f + k + 1],
                                 in1=hi[:, c], op0=MUL, op1=SUB)
                op.then_inc(done, 1)

            def a_parts(phase, count, scale=None):
                for f in range(8):
                    a_part(f, phase, count, scale)

            def by_chunks(chunk, part=None):
                for c in range(4):
                    chunk(c)
                    if part and c:
                        part(2 * c - 2)
                        part(2 * c - 1)
                if part:
                    part(6)
                    part(7)

            def b_parts(phase, g, i, scale=None):
                for n, step in enumerate(("ba", "bb")):
                    b, done = full(phase, step, g)
                    dve.wait_ge(b_hi_in, 2 * i + n + 1)
                    hi = b_hi[:, n * COL:(n + 1) * COL].bitcast(f32)
                    lo = b_lo[:, n * COL:(n + 1) * COL]
                    if scale is None:
                        op = tt(lo, b[:, :], hi, SUB)
                    else:
                        for k in range(2):
                            c = slice(k * SEQ, (k + 1) * SEQ)
                            op = stt(out=lo[:, c], in0=b[:, c], scalar=scale(2 * n + k), in1=hi[:, c], op0=MUL, op1=SUB)
                    op.then_inc(done, 1)

            def add(m, j, pair, dst):
                dve.wait_ge(sub_used, 8 * m + 2 * j + 2)
                for t in range(TT):
                    to = dst[:, t * D + j * COL:t * D + (j + 1) * COL]
                    tt(to, acc[(pair + j) % 2][t][:, :], to, ADD).then_inc(out_added, 1)

            def by(buf, n):
                return buf.rearrange("p (n c) -> p n c", n=n)

            def spread(ap, n):
                return ap.unsqueeze(1).to_broadcast([P, n, ap.shape[1]])

            def gated(i, phase, g, w, src):
                dve.wait_ge(wide_taken, 2 * (w + 1))
                tt(br[:, :], src, zs[:, :], MUL).then_inc(s["branch_ready"], 1)

            def ret_rotate(g, first):
                dve.wait_ge(wide_taken, 2 * (W_RET + 3 * g + 1))
                if not first:
                    turned("ret", "k", g - 1)
                for t in range(TT):
                    c = slice(t * COL, (t + 1) * COL)
                    cos, sin = gates[:, t * 64:(t + 1) * 64], gates[:, P + t * 64:P + (t + 1) * 64]
                    src = n0[:, c].rearrange("p (h two c) -> p h two c", two=2, c=64)
                    cross = dn[:, c].rearrange("p (h two c) -> p h two c", two=2, c=64)
                    tt(by(sq[:, c], 8), by(n0[:, c], 8), spread(cos, 8), MUL)
                    for half in range(2):
                        tt(cross[:, :, half, :], src[:, :, 1 - half, :], spread(sin, 4), MUL)
                dve.drain()
                for half, op in enumerate((SUB, ADD)):
                    a, b, to = (x[:, :].rearrange("p (h two c) -> p h two c", two=2, c=64)[:, :, half, :] for x in (sq, dn, cv))
                    last = tt(to, a, b, op)
                last.then_inc(s["rot_ready"], 1)

            def ret_decay(g, first):
                dve.wait_ge(s["decay_loaded"], 16 * g + 16)
                for h in range(2):
                    if not first:
                        turned("ret", f"o{h}", g - 1)
                    b, done = full("ret", f"s{h}", g)
                    dec, to = dt_[:, h * SEQ:(h + 1) * SEQ], h * 384
                    tt(pi[:, to:to + SEQ], b[:, 0:SEQ], dec, MUL)
                    tt(pi[:, to + SEQ:to + 384], b[:, SEQ:384], dec[:, 0:P], MUL).then_inc(done, 1)

            def ret_norm(g):
                for h in range(2):
                    b, _ = full("ret", f"o{h}", g)
                    for t in range(TT):
                        dve.bn_stats(small[:, 6 * (2 * h + t):6 * (2 * h + t + 1)], b[:, t * SEQ:(t + 1) * SEQ])
                dve.drain()
                for n in range(4):
                    last = dve.bn_aggr(small[:, 24 + 2 * n:26 + 2 * n], small[:, 6 * n:6 * n + 6])
                last.then_inc(s["stats"], 1)
                dve.wait_ge(s["root_ready"], g + 1)
                dve.reciprocal(small[:, 40:44], small[:, 36:40])
                dve.drain()
                for h in range(2):
                    b, done = full("ret", f"o{h}", g)
                    for t in range(TT):
                        n = 2 * h + t
                        last = ts(ui[:, t * COL + h * SEQ:t * COL + (h + 1) * SEQ], b[:, t * SEQ:(t + 1) * SEQ],
                                  small[:, 24 + 2 * n:25 + 2 * n], small[:, 40 + n:41 + n], SUB, MUL)
                    last.then_inc(done, 1)
                dve.drain()

            def ret_mid(g, first, adds):
                ret_rotate(g, first)
                ret_decay(g, first)
                ret_norm(g)
                for j in range(4):
                    adds(j)

            def ret_end(g, i):
                gated(i, "ret", g, W_RET + 3 * g + 2, ui[:, :])
                b_parts("ret", g, i, ret_scale)

            def ret_scale(k):
                return small[:, 104 + k:105 + k]

            def per(t, buf, hh):
                return buf[:, t * COL + hh * P:t * COL + (hh + 1) * P]

            def conv_tap(dst, first_tile, tap):
                src = by(cb[:, :], 4)
                for c in range(4):
                    at = 64 + 8 * tap + first_tile + c
                    w, x, y = small[:, at:at + 1], src[:, c, tap:tap + SEQ], dst[:, c * SEQ:(c + 1) * SEQ]
                    if tap == 0:
                        last = ts(y, x, w, None, MUL)
                    else:
                        last = stt(out=y, in0=x, scalar=w, in1=y, op0=MUL, op1=ADD)
                if tap < 3:
                    dve.drain()
                else:
                    last.then_inc(s["conv_done"], 1)

            def gdn_qk(g):
                for half in range(2):
                    taps = by(small[:, 64 + 16 * half:80 + 16 * half], 2)
                    src = by(cols[:, P * (1 + half):P * (1 + half) + 96], 2)
                    dve.tensor_copy(taps[:, :, 0:2], src[:, :, ds(2 * g, 2)])
                    dve.tensor_copy(taps[:, :, 2:4], src[:, :, ds(2 * g + 12, 2)])
                    dve.tensor_copy(taps[:, :, 4:8], src[:, :, ds(4 * g + 24, 4)])
                dve.drain()
                copied("gdn", "q", g)
                copied("gdn", "k", g)
                for tap in range(4):
                    conv_tap(cv, 0, tap)

            def gdn_unit(g):
                dve.tensor_copy(by(small[:, 0:48], 12), by(gates[:, :], 12)[:, :, ds(4 * g, 4)]).then_inc(s["gs_ready"], 1)
                for step in ("sq", "sk"):
                    copied("gdn", step, g)
                dve.reciprocal(lw[:, :], lw[:, :])
                dve.drain()
                stt(out=cv[:, 0:COL], in0=cv[:, 0:COL], scalar=QSCALE, in1=lw[:, 0:COL], op0=MUL, op1=MUL)
                tt(cv[:, COL:], cv[:, COL:], lw[:, COL:], MUL).then_inc(s["unit_ready"], 1)

            def gdn_mid(g, adds):
                dve.wait_ge(s["gs_ready"], g + 1)
                dve.wait_ge(s["unit_ready"], g + 1)
                rows = [full("gdn", f"row{t}", g) for t in range(TT)]
                for buf, op in ((dn, MAX), (dt_, MIN)):
                    for t in range(TT):
                        for hh in range(4):
                            last = ts(per(t, buf, hh), rows[t][0][:, hh * P:(hh + 1) * P], small[:, 8 + 4 * t + hh:9 + 4 * t + hh],
                                      0.0, SUB, op)
                        if buf is dt_:
                            last.then_inc(rows[t][1], 1)
                dve.wait_ge(s["decay_ready"], 2 * g + 1)
                tt(by(dn[:, :], 8), by(dn[:, :], 8), spread(low, 8), MUL)
                dve.wait_ge(s["decay_ready"], 2 * g + 2)
                tt(by(dt_[:, :], 8), by(dt_[:, :], 8), spread(tri, 8), MUL)
                dve.drain()
                kk, kk_done = full("gdn", "kk", g)
                for t in range(TT):
                    for hh in range(4):
                        at = (2 * t + hh // 2) * P
                        last = stt(out=per(t, lw, hh), in0=kk[:, at:at + P], scalar=small[:, 16 + 4 * t + hh:17 + 4 * t + hh],
                                   in1=per(t, dn, hh), op0=MUL, op1=MUL)
                last.then_inc(kk_done, 1)
                dve.drain()
                tt(by(xi[:, :], 8), by(lw[:, :], 8), spread(negm1, 8), MUL)
                dve.drain()
                for t in range(TT):
                    c = slice(t * COL, (t + 1) * COL)
                    tt(by(xi[:, c], 4), by(xi[:, c], 4), spread(ident, 4), ADD).then_inc(s["lower_ready"], 1)
                qk, qk_done = full("gdn", "qk", g)
                for t in range(TT):
                    for v in range(2):
                        to = by(dt_[:, t * COL:(t + 1) * COL], 4).rearrange("p (h v) c -> p h v c", v=2)[:, :, v, :]
                        last = tt(to, to, by(qk[:, 2 * t * P:2 * (t + 1) * P], 2), MUL)
                last.then_inc(qk_done, 1)
                for n in range(1, 7):
                    if n <= 4:
                        adds(n - 1)
                    gdn_level_p(g, n)
                    if n == 1:
                        copied("gdn", "va", g)
                        copied("gdn", "vb", g)
                    if n <= 2:
                        conv_tap(sq, 4, 2 * n - 2)
                    gdn_level_n(g, n)
                    if n <= 2:
                        conv_tap(sq, 4, 2 * n - 1)
                copied("gdn", "kn", g)
                for hh in range(4):
                    last = ts(per(0, xi, hh), kn[:, (hh // 2) * P:(hh // 2 + 1) * P], small[:, 32 + hh:33 + hh], None, MUL)
                last.then_inc(s["kn_ready"], 1)
                b, done = full("gdn", "o0", g)
                dve.tensor_copy(dn[:, 0:COL], b[:, :]).then_inc(done, 1)
                b, done = full("gdn", "ks", g)
                for hh in range(4):
                    last = stt(out=per(1, xi, hh), in0=b[:, hh * P:(hh + 1) * P], scalar=small[:, 44 + hh:45 + hh],
                               in1=per(1, n1, hh), op0=MUL, op1=ADD)
                last.then_inc(done, 1)
                gdn_squares(0)

            def gdn_squares(t):
                c = slice(t * COL, (t + 1) * COL)
                dve.drain()
                tt(pi[:, c], dn[:, c], dn[:, c], MUL)
                dve.drain()
                return dve.tensor_reduce(small[:, 218 + 4 * t:222 + 4 * t], by(pi[:, c], 4), AX.X, ADD)

            def gdn_out(g):
                copied("gdn", "qs", g)
                b, done = full("gdn", "o1", g)
                tt(dn[:, COL:], b[:, :], kn[:, :], ADD).then_inc(done, 1)
                gdn_squares(1).then_inc(s["stats"], 1)
                dve.wait_ge(s["root_ready"], GROUPS + g + 1)
                dve.reciprocal(small[:, 234:242], small[:, 226:234])
                dve.drain()
                dve.wait_ge(wide_taken, 2 * (W_GDN + 3 * g + 3))
                for t in range(TT):
                    for hh in range(4):
                        n = 4 * t + hh
                        last = stt(out=per(t, br, hh), in0=per(t, dn, hh), scalar=small[:, 234 + n:235 + n], in1=per(t, zs, hh),
                                   op0=MUL, op1=MUL)
                last.then_inc(s["branch_ready"], 1)

            def head_norm(src, tmp, n, between):
                dve.drain()
                tt(tmp[:, :], src[:, 0:1024], src[:, 0:1024], MUL)
                dve.drain()
                dve.tensor_reduce(small[:, 218:226], by(tmp[:, :], 8), AX.X, ADD).then_inc(s["stats"], 1)
                between()
                dve.wait_ge(s["root_ready"], n + 1)
                dve.reciprocal(small[:, 234:242], small[:, 226:234])
                dve.drain()
                tt(by(tmp[:, :], 8), by(src[:, 0:1024], 8), small[:, 234:242].unsqueeze(2).to_broadcast([P, 8, P]), MUL)
                dve.drain()

            def gdn_level_p(g, n):
                size = LEVELS[n]
                for t in range(TT):
                    b, done = full("gdn", f"p{size}_{t}", g)
                    tt(by(pi[:, t * COL:(t + 1) * COL], 4), by(b[:, :], 4), spread(level_mask(n), 4), MUL).then_inc(done, 1)

            def gdn_level_n(g, n):
                size, last_level = LEVELS[n], n == len(LEVELS) - 1
                if n == 1:
                    for t in range(TT):
                        copied("gdn", f"u{t}", g)
                for t in range(TT):
                    b, done = full("gdn", f"n{size}_{t}", g)

                    def halves(buf, side):
                        return buf[:, t * COL:(t + 1) * COL].rearrange("p (n two s) -> p n two s", two=2, s=size)[:, :, side, :]

                    def res(at):
                        return b[:, at:at + 256].rearrange("p (n s) -> p n s", s=size)
                    last = tt(halves(ui, 1), halves(ui, 1), res(0), SUB)
                    if not last_level:
                        last = tt(halves(xi, 0), halves(xi, 0), res(256), SUB)
                    last.then_inc(done, 1)

            def gdn_scale(k):
                return cols[:, C_GG:C_GG + 1]

            def att_mid(att, n, g, w, i, adds):
                for t in range(TT):
                    b, _ = full(att, f"s{t}", g)
                    dve.tensor_reduce(small[:, 114 + 2 * t:116 + 2 * t], by(b[:, :], 2), AX.X, MAX)
                dve.drain()
                for t in range(TT):
                    ts(small[:, 110 + 2 * t:112 + 2 * t], small[:, 114 + 2 * t:116 + 2 * t], -MSCALE, None, MUL).then_inc(s["mneg"], 1)
                adds(0)
                adds(1)
                copied(att, "s0", g)
                copied(att, "s1", g)
                dve.reciprocal(small[:, 124:128], small[:, 120:124])
                dve.drain()
                adds(2)
                for t in range(TT):
                    b, done = full(att, f"o{t}", g)
                    for h in range(2):
                        c = 2 * t + h
                        last = ts(pi[:, c * SEQ:(c + 1) * SEQ], b[:, h * SEQ:(h + 1) * SEQ], small[:, 124 + c:125 + c], None, MUL)
                    last.then_inc(done, 1)
                dve.drain()
                gated(i, att, g, w + 2 * g + 1, pi[:, :])
                adds(3)

            def ret_layer_body(g, at, pair, first=False):
                if not first:
                    ret_end(g - 1, g - 1)
                ret_mid(g, first, (lambda j: None) if first else (lambda j: add(at + 3, j, 1 - pair, x_sb)))

            def gdn_layer_body(g, at, pair, first=False):
                gdn_qk(g)
                if not first:
                    gdn_out(g - 1)
                gdn_unit(g)
                if not first:
                    b_parts("gdn", g - 1, B_L1 + g - 1, gdn_scale)
                gdn_mid(g, (lambda j: None) if first else (lambda j: add(at + 3, j, 1 - pair, x_sb)))

            def gdn_end(g, i):
                gdn_out(g)
                b_parts("gdn", g, i, gdn_scale)

            def layer(m, w, b0, body, end, att, n_att):
                body(0, m, 0, True)
                body(1, m + 3, 1)
                with dve.Fori(0, (GROUPS - 2) // 2) as r:
                    for g, pair in ((2 * r + 2, 0), (2 * r + 3, 1)):
                        body(g, 4 * g + (m - 1), pair)
                m += 3 + 4 * (GROUPS - 1)
                w += 3 * GROUPS
                for g in range(MGROUPS):
                    i = b0 + GROUPS + g
                    if g == 0:
                        end(GROUPS - 1, i - 1)
                    else:
                        b_parts(att, g - 1, i - 1)
                    att_mid(att, n_att + g, g, w, i, lambda j: add(m + 2, j, 0, x_sb))
                    m += 3
                b_parts(att, MGROUPS - 1, b0 + BR - 1)
                for j in range(4):
                    add(m, j, 0, x_sb)
                    dve.drain()
                    for t in range(TT):
                        at = 170 + 6 * (4 * t + j)
                        dve.bn_stats(small[:, at:at + 6], x_sb[:, t * D + j * COL:t * D + (j + 1) * COL])
                dve.drain()

            def layer_norm(i, part=None):
                for t in range(TT):
                    last = dve.bn_aggr(small[:, 156 + 2 * t:158 + 2 * t], small[:, 170 + 24 * t:194 + 24 * t])
                last.then_inc(s["ln_stats"], 1)
                dve.wait_ge(s["ln_root"], i + 1)
                dve.reciprocal(small[:, 162:164], small[:, 160:162])
                dve.drain()
                dve.wait_ge(s["rows_spread"], 32 * (i + 1))

                def chunk(c):
                    col = slice(c * COL, (c + 1) * COL)
                    rows = [x_sb[:, t * D + c * COL:t * D + (c + 1) * COL] for t in range(TT)]
                    for t in range(TT):
                        stt(out=rows[t], in0=rows[t], scalar=small[:, 156 + 2 * t:157 + 2 * t], in1=lnw[:, col], op0=SUB, op1=MUL)
                    dve.drain()
                    for t in range(TT):
                        stt(out=rows[t], in0=rows[t], scalar=small[:, 162 + t:163 + t], in1=lnw[:, D + c * COL:D + (c + 1) * COL],
                            op0=MUL, op1=ADD).then_inc(s["x_final"], 1)
                by_chunks(chunk, part)

            def scale_x():
                return ts(x_sb[:, :], x_sb[:, :], ALPHA, None, MUL)

            a_parts("mem0", 0)
            dve.wait_ge(s["pos_loaded"], 16)
            dve.wait_ge(s["consts_loaded"], 16)
            dve.tensor_copy(small[:, 0:TT], pos_sb[:, :])
            dve.drain()
            for t in range(TT):
                ts(gates[:, P + t * 64:P + (t + 1) * 64], cst[:, C_FREQ:C_FREQ + 64], small[:, t:t + 1], None, MUL)
            dve.drain()
            turns, whole = dn[:, 0:2 * P], dn[:, 2 * P:4 * P]
            for k, shift in enumerate((0.25, 0.0)):
                ts(turns[:, k * P:(k + 1) * P], gates[:, P:2 * P], 1 / TWO_PI, shift, MUL, ADD)
            dve.drain()
            ts(whole, turns, ROUND, None, ADD)
            dve.drain()
            ts(turns, whole, ROUND, None, SUB)
            dve.drain()
            for n, part in enumerate(TURN_PARTS):
                for k in (0, 1):
                    to = gates[:, k * P:(k + 1) * P]
                    stt(out=to, in0=turns[:, k * P:(k + 1) * P], scalar=-part, in1=gates[:, P:2 * P] if n == 0 else to, op0=MUL, op1=ADD)
                    if n == 0 and k == 0:
                        dve.drain()
                dve.drain()
            ts(gates[:, 0:P], gates[:, 0:P], math.pi / 2, None, ADD)
            dve.drain()
            ts(gates[:, 0:2 * P], gates[:, 0:2 * P], PI_BELOW, -PI_BELOW, MIN, MAX).then_inc(s["trig_arg"], 1)
            dve.wait_ge(s["cols_ready"], 1)
            tt(lb[:, 0:8], cols[:, C_LB:C_LB + 8], cols[:, C_LB + 8:C_LB + 16], SUB).then_inc(s["lb_arg"], 1)
            dve.wait_ge(s["lb_ready"], 1)
            ts(lb[:, 8:16], lb[:, 0:8], -1.0, 1.0, MUL, ADD)
            dve.wait_ge(s["trig_ready"], 1)
            a_parts("x0", 1)
            scale_x()
            dve.drain()
            layer(U_RET, W_RET, 0, ret_layer_body, ret_end, "att0", 0)
            a_parts("mem1", 2)
            layer_norm(0)
            n48 = 2 * NVH
            dve.wait_ge(s["ab_hi"], 1)
            tt(b_lo[:, 0:16 * n48], n0[:, 0:16 * n48], b_hi[:, 0:16 * n48].bitcast(f32), SUB).then_inc(s["ab_lo"], 1)
            dve.memset(cb[:, :], 0.0)
            a_parts("x1", 3)
            scale_x()
            dve.drain()
            b, done = full("gates", "ab")
            xa, xs = n1[:, 64:112], n1[:, 112:160]
            dve.wait_ge(s["gate_step"], 1)
            tt(by(xa, TT), b[:, 0:2 * n48].rearrange("p (t c) -> p t c", t=TT)[:, :, 0:NVH], spread(n1[:, 0:NVH], TT), ADD)
            dve.drain()
            stt(out=xs, in0=xa, scalar=-1.0, in1=xa, op0=MUL, op1=MAX).then_inc(s["gate_dve"], 1)
            ts(xa, xa, 0.0, None, MAX)
            dve.drain()
            dve.wait_ge(s["gate_step"], 4)
            tt(xa, xa, n1[:, 208:256], ADD).then_inc(done, 1)
            dve.drain()
            stt(out=by(gates[:, 0:n48], TT), in0=by(xa, TT), scalar=-1.0, in1=spread(n1[:, 256:256 + NVH], TT), op0=MUL, op1=MUL)\
                .then_inc(s["g_ready"], 1)
            copied("gates", "cum")
            b, done = full("gates", "last")
            tt(n1[:, 288:336], b[:, 0:n48], gates[:, n48:2 * n48], SUB).then_inc(done, 1)
            stt(out=gates[:, 5 * n48:6 * n48], in0=gates[:, 2 * n48:3 * n48], scalar=-1.0, in1=gates[:, 3 * n48:4 * n48], op0=MUL, op1=MUL)\
                .then_inc(s["gate_dve"], 1)
            dve.wait_ge(s["gate_dve"], 2)
            dve.wait_ge(s["gate_step"], 5)
            layer(U_GDN, W_GDN, B_L1, gdn_layer_body, gdn_end, "att1", 2)
            layer_norm(1, lambda f: a_part(f, "h2", 4, C_MP))

            def invert_rms(n):
                dve.wait_ge(s["rms_root"], n + 1)
                return dve.reciprocal(inverse_rms(n), small[:, 242 + 2 * n:244 + 2 * n])

            def add_normalised(n, w, done, part=None):
                dve.wait_ge(s["y_squared"], n // 2 + 1)
                dve.tensor_reduce(small[:, 148:150], by(small[:, 140:148], 2), AX.X, ADD).then_inc(s["y_summed"], 1)
                invert_rms(n)
                dve.drain()

                def chunk(c):
                    xs, ys = ([buf[:, t * D + c * COL:t * D + (c + 1) * COL] for t in range(TT)] for buf in (x_sb, y_sb))
                    for t in range(TT):
                        stt(out=ys[t], in0=ys[t], scalar=inverse_rms(n)[:, t:t + 1], in1=w[:, c * COL:(c + 1) * COL],
                            op0=MUL, op1=MUL)
                    dve.drain()
                    for t in range(TT):
                        tt(xs[t], xs[t], ys[t], ADD).then_inc(done, 1)
                by_chunks(chunk, part)

            invert_rms(0).then_inc(s["inverse_rms"], 1)
            dve.memset(y_sb, 0.0)
            dve.memset(xi[:, :], 0.0)
            dve.memset(ui[:, :], 0.0)
            dve.drain()

            def hgrn_gates(g):
                copied("hgrn", "fa", g)
                copied("hgrn", "fb", g)
                for hh in range(4):
                    c = slice(hh * SEQ, (hh + 1) * SEQ)
                    low_, rest = (lb[:, k + 4 * g + hh:k + 4 * g + hh + 1] for k in (0, 8))
                    ts(dn[:, c], sq[:, c], rest, low_, MUL, ADD)
                    ts(lw[:, c], sq[:, c], -1.0, 1.0, MUL, ADD)
                dve.drain()
                ts(dn[:, :], dn[:, :], TINY, None, MAX)
                for hh in range(4):
                    c = slice(hh * SEQ, (hh + 1) * SEQ)
                    ts(lw[:, c], lw[:, c], lb[:, 8 + 4 * g + hh:9 + 4 * g + hh], None, MUL)
                dve.drain()
                dve.tensor_copy(small[:, 0:1], lw[:, 0:1]).then_inc(s["ksc_ready"], 1)
                dve.wait_ge(s["logf_ready"], g + 1)
                for hh in range(4):
                    c = slice(hh * SEQ, (hh + 1) * SEQ)
                    dve.tensor_tensor_scan(pi[:, c], one_row, dn[:, c], 0.0, MUL, ADD)
                dve.drain()

            def sides(buf, size):
                v = buf[:, :].rearrange("p (n two s) -> p n two s", two=2, s=size)
                return v[:, :, 0, :], v[:, :, 1, :]

            def compact(buf, size):
                return buf.rearrange("p (n s) -> p n s", s=size)

            def hgrn_arg(g, n):
                size = 2 ** n
                left, right = sides(pi, size)
                mid = left[:, :, size - 1:size].to_broadcast([P, COL // size, size])
                buf = (sq, br)[n % 2]
                tt(compact(buf[:, 0:COL], size), right, mid, SUB)
                tt(compact(buf[:, COL:], size), mid, left, SUB).then_inc(s["lev_arg"], 1)

            def hgrn_scale(g, n):
                size = 2 ** n
                buf, ks, qs = (sq, br)[n % 2], (xi, ui)[n % 2], dn[:, (n % 2) * COL:(n % 2 + 1) * COL]
                dve.wait_ge(s["lev_exp"], 8 * g + n + 1)
                if n >= 2:
                    turned("hgrn", f"l{LEVELS[n - 2]}", g)
                elif g:
                    turned("hgrn", "x", g - 1)
                tt(compact(qs, size), sides(cv, size)[1], compact(buf[:, 0:COL], size), MUL)
                tt(sides(ks, size)[0], sides(lw, size)[0], compact(buf[:, COL:], size), MUL).then_inc(s["lev_ready"], 1)

            def hgrn_diagonal(g):
                for t in range(TT):
                    b, done = full("hgrn", f"d{t}", g)
                    to = dt_.rearrange("p (h t c) -> p h t c", t=TT, c=P)[:, :, t, :]
                    tt(to, by(b[:, :], 4), spread(ident, 4), MUL).then_inc(done, 1)
                dve.drain()

            def hgrn_place(g, n):
                if n == 7:
                    b, done = full("hgrn", "x", g)
                    dve.tensor_copy(kn[:, :], b[:, :]).then_inc(done, 1)
                    return
                size = LEVELS[n]
                b, done = full("hgrn", f"l{size}", g)
                for i in range(8):
                    at = i * P
                    to = dt_[:, at:at + P].rearrange("p (n two s) -> p n two s", two=2, s=size)[:, :, 1, :]
                    mask = level_mask(n).bitcast(u32).rearrange("p (n two s) -> p n two s", two=2, s=size)[:, :, 1, :]
                    last = dve.copy_predicated(to, mask, compact(b[:, i * 64:(i + 1) * 64], size))
                last.then_inc(done, 1)
                dve.drain()

            def hgrn_end(g, between=lambda n: None):
                dve.wait_ge(wide_taken, 2 * (W_HG + 4 * g + 4))
                for t in range(TT):
                    b, done = full("hgrn", f"o{t}", g)
                    tt(cb[:, t * COL:(t + 1) * COL], b[:, :], zs[:, t * COL:(t + 1) * COL], MUL).then_inc(done, 1)
                between(0)
                head_norm(cb, sq, 2 * GROUPS + g, lambda: between(1))
                dve.tensor_copy(br[:, :], sq[:, :]).then_inc(s["branch_ready"], 1)

            def hgrn_levels(g):
                hgrn_arg(g, 0)
                hgrn_arg(g, 1)
                hgrn_diagonal(g)
                for n in range(8):
                    hgrn_scale(g, n)
                    if n >= 1:
                        hgrn_place(g, n - 1)
                    if n + 2 < 8:
                        dve.drain()
                        hgrn_arg(g, n + 2)
                hgrn_place(g, 7)

            hgrn_gates(0)
            hgrn_levels(0)
            hgrn_end(0)
            b_parts("hgrn", 0, B_HG, lambda k: cols[:, C_HW + k:C_HW + k + 1])
            hgrn_gates(1)
            hgrn_levels(1)
            hgrn_end(1, lambda n: add(U_P0 + 1, n, 1, y_sb))
            add(U_P0 + 1, 2, 1, y_sb)
            b_parts("hgrn", 1, B_HG + 1, lambda k: cols[:, C_HW + 4 + k:C_HW + 5 + k])
            add(U_P0 + 1, 3, 1, y_sb)

            def pool_scaled(g):
                dst = (sq, br)[g]
                for n, step in enumerate(("ya", "yb")):
                    b, done = full("pool", step, g)
                    for c in range(2):
                        i = 4 * g + 2 * n + c
                        last = ts(dst[:, (2 * n + c) * SEQ:(2 * n + c + 1) * SEQ], b[:, c * SEQ:(c + 1) * SEQ],
                                  cols[:, C_PB + i:C_PB + i + 1], cols[:, C_PS + i:C_PS + i + 1], ADD, MUL)
                    last.then_inc(done, 1)
                dve.drain()
                dve.tensor_copy(small[:, 0:1], dst[:, 0:1]).then_inc(s["pool_mapped"], 1)

            def pool_parts(g):
                at = slice(g * KB * SEQ, (g + 1) * KB * SEQ)
                dve.wait_ge(s["pool_hi"], g + 1)
                tt(a_lo[:, at], (sq, br)[g][:, :], a_hi[:, at].bitcast(f32), SUB).then_inc(s["pool_in"], 1)

            pool_scaled(0)
            add(U_P0 + 3, 0, 0, y_sb)
            add(U_P0 + 3, 1, 0, y_sb)
            pool_parts(0)
            pool_scaled(1)
            add(U_P0 + 3, 2, 0, y_sb)
            pool_parts(1)
            add(U_P0 + 3, 3, 0, y_sb)
            for m in (U_P0 + 4, U_P0 + 5):
                for j in range(4):
                    add(m, j, 0, y_sb)
            dve.wait_ge(s["rows_spread"], 16 * 5)
            add_normalised(1, big[:, 0:D], s["x_final"], lambda f: a_part(f, "h3", 5, C_LP))
            invert_rms(2).then_inc(s["inverse_rms"], 1)
            dve.memset(y_sb, 0.0)
            dve.drain()

            def mlp_squares(g):
                dve.wait_ge(wide_taken, 2 * g + 2 * W_MLP + 2)
                tt(br[:, :], n0[:, :], n0[:, :], MUL).then_inc(s["branch_ready"], 1)

            def mlp(g, pair):
                if not (isinstance(g, int) and g == FFG):
                    mlp_squares(g - 1)
                b_parts("mlp", g - 1, g + (B_MLP - 3))
                for j in range(4):
                    if isinstance(g, int) and g == FFG - 1 and j == 2:
                        mlp_squares(g)
                    add(2 * g + U_MLP if not isinstance(g, int) or g < FFG else UNITS - 1, j, 1 - pair, y_sb)
            with dve.Fori(0, (FFG - 2) // 2) as r:
                mlp(2 * r + 1, 1)
                mlp(2 * r + 2, 0)
            mlp(FFG - 1, 1)
            mlp(FFG, 1)
            dve.wait_ge(s["rows_spread"], 16 * 6)
            add_normalised(3, big[:, 2048:2048 + D], s["out_ready"])
    return nc


INPUTS = ["x", "mem", "positions", "w_in_ret", "ret_norm_g", "w_in_gdn", "conv_w", "a_log", "dt_bias", "gdn_norm_g",
          "w_mem_kv", "w_out", "ln_g", "ln_b", "w_in_2", "pool_w_2", "pool_b_2", "pool_scale_2", "lb_logits_2",
          "hgrn_norm_w_2", "w_out_2", "norm_mix_pre_2", "norm_mix_post_2", "norm_mlp_pre_2", "norm_mlp_post_2",
          "w_mlp_in_2", "w_mlp_out_2"]


def kernel(**inputs):
    import concourse.bacc as bacc
    from concourse.bass_utils import run_bass_kernel_spmd

    nc = bacc.Bacc("TRN2", target_bir_lowering=False, num_devices=1)
    arrays = {f"in_{n}": np.ascontiguousarray(inputs[n]) for n in INPUTS}
    arrays["shape_constants"] = shape_constants()
    args = [nc.dram_tensor(n, a.shape, mybir.dt.from_np(a.dtype), kind="ExternalInput").ap() for n, a in arrays.items()]
    out = nc.dram_tensor("out", (1, SEQ, D), mybir.dt.float32, kind="ExternalOutput").ap()
    build(nc, *args, out)
    r = run_bass_kernel_spmd(nc, [arrays], core_ids=[0])
    return r.results[0]["out"]
```
